# Optimizing a Trainium2 kernel written in Bass

```python
import math
import jax, jax.numpy as jnp
from jax import lax
import numpy as np

D_MODEL = 1024
BATCH = 1
SEQ = 256
DEPTH = 2

N_MIXERS = 2
N_Q_HEADS = 8
N_KV_HEADS = 2
HEAD_DIM = D_MODEL // N_Q_HEADS
Q_PER_KV = N_Q_HEADS // N_KV_HEADS
ROT_DIM = HEAD_DIM // 4
ROPE_THETA = 500000.0
WINDOW = 128
BLOCK = 128
D_RNN = 3 * D_MODEL // 2
N_RNN_BLOCKS = 16
RNN_BLOCK_W = D_RNN // N_RNN_BLOCKS
CONV_W = 4
CONV_LEFT = 2
LRU_C = 8.0
D_FF = 4 * D_MODEL
DN_ALPHA = (2.0 * DEPTH) ** 0.25
DN_BETA = (8.0 * DEPTH) ** -0.25
LN_EPS = 1e-5
ADA_INIT = 0.5

N_ATTN_LAYERS = (DEPTH + N_MIXERS - 1) // N_MIXERS
N_RNN_LAYERS = DEPTH // N_MIXERS


def layer_norm(x, g, b):
    xf = x.astype(jnp.float32)
    mu = jnp.mean(xf, axis=-1, keepdims=True)
    var = jnp.mean(jnp.square(xf - mu), axis=-1, keepdims=True)
    y = (xf - mu) * lax.rsqrt(var + LN_EPS)
    return (y * g.astype(jnp.float32) + b.astype(jnp.float32)).astype(x.dtype)

def ada_modulation(c, w, b):
    mod = jax.nn.silu(c) @ w + b
    shift, scale, gate = jnp.split(mod, 3, axis=-1)
    return shift[:, None, :], scale[:, None, :], gate[:, None, :]

def partial_rope(t, cos, sin):
    half = ROT_DIM // 2
    tr = t[..., :ROT_DIM].astype(jnp.float32)
    t1, t2 = tr[..., :half], tr[..., half:]
    cs, sn = cos[None, :, None, :], sin[None, :, None, :]
    rot = jnp.concatenate([t1 * cs - t2 * sn, t2 * cs + t1 * sn], axis=-1).astype(t.dtype)
    return jnp.concatenate([rot, t[..., ROT_DIM:]], axis=-1)

def windowed_gqa(h, w_in, w_out, sinks):
    B, S, _ = h.shape
    nblk = S // BLOCK
    qkv = h @ w_in
    q, k, v = jnp.split(qkv, [N_Q_HEADS * HEAD_DIM, (N_Q_HEADS + N_KV_HEADS) * HEAD_DIM], axis=-1)
    q = q.reshape(B, S, N_Q_HEADS, HEAD_DIM)
    k = k.reshape(B, S, N_KV_HEADS, HEAD_DIM)
    v = v.reshape(B, S, N_KV_HEADS, HEAD_DIM)
    pos = jnp.arange(S, dtype=jnp.float32)
    inv_freq = ROPE_THETA ** (-jnp.arange(0, ROT_DIM, 2, dtype=jnp.float32) / ROT_DIM)
    ang = pos[:, None] * inv_freq[None, :]
    cos, sin = jnp.cos(ang), jnp.sin(ang)
    q = partial_rope(q, cos, sin)
    k = partial_rope(k, cos, sin)
    qb = q.reshape(B, nblk, BLOCK, N_KV_HEADS, Q_PER_KV, HEAD_DIM)

    def band(t):
        tp = jnp.pad(t, ((0, 0), (BLOCK, BLOCK), (0, 0), (0, 0)))
        tb = tp.reshape(B, nblk + 2, BLOCK, N_KV_HEADS, HEAD_DIM)
        return jnp.concatenate([tb[:, :-2], tb[:, 1:-1], tb[:, 2:]], axis=2)

    kb, vb = band(k), band(v)
    scores = jnp.einsum("bnqhgd,bnjhd->bnhgqj", qb, kb,
                        preferred_element_type=jnp.float32) * (HEAD_DIM ** -0.5)
    blk = jnp.arange(nblk)[:, None, None] * BLOCK
    qpos = blk + jnp.arange(BLOCK)[None, :, None]
    kpos = blk - BLOCK + jnp.arange(3 * BLOCK)[None, None, :]
    valid = (jnp.abs(qpos - kpos) <= WINDOW) & (kpos >= 0) & (kpos < S)
    scores = jnp.where(valid[None, :, None, None], scores, -jnp.inf)
    sink = sinks.astype(jnp.float32).reshape(N_KV_HEADS, Q_PER_KV)[None, None, :, :, None, None]
    m = jnp.maximum(jnp.max(scores, axis=-1, keepdims=True), sink)
    p = jnp.exp(scores - m)
    denom = jnp.sum(p, axis=-1, keepdims=True) + jnp.exp(sink - m)
    probs = (p / denom).astype(v.dtype)
    o = jnp.einsum("bnhgqj,bnjhd->bnqhgd", probs, vb)
    o = o.reshape(B, S, N_Q_HEADS * HEAD_DIM)
    return o @ w_out

def centred_depthwise_conv(x, w, b):
    S = x.shape[1]
    xp = jnp.pad(x, ((0, 0), (CONV_LEFT, CONV_W - 1 - CONV_LEFT), (0, 0)))
    out = xp[:, 0:S] * w[0] + b
    for j in range(1, CONV_W):
        out = out + xp[:, j:j + S] * w[j]
    return out

def rg_lru(x, w_a, b_a, w_x, b_x, lam, reverse):
    B, S, _ = x.shape
    xb = x.reshape(B, S, N_RNN_BLOCKS, RNN_BLOCK_W)
    r = jax.nn.sigmoid((jnp.einsum("bsni,nij->bsnj", xb, w_a).reshape(B, S, D_RNN) + b_a).astype(jnp.float32))
    i = jax.nn.sigmoid((jnp.einsum("bsni,nij->bsnj", xb, w_x).reshape(B, S, D_RNN) + b_x).astype(jnp.float32))
    log_a = -LRU_C * r * jax.nn.softplus(-lam.astype(jnp.float32))
    a = jnp.exp(log_a)
    mult = jnp.sqrt(-jnp.expm1(2.0 * log_a))
    u = mult * (i * x.astype(jnp.float32))

    def combine(left, right):
        a_l, b_l = left
        a_r, b_r = right
        return a_l * a_r, a_r * b_l + b_r

    _, hs = lax.associative_scan(combine, (a, u), axis=1, reverse=reverse)
    return hs

def recurrent_block(h, w_in, conv_w, conv_b, w_a, b_a, w_x, b_x, lam, w_out):
    z = h @ w_in
    xr, gate = jnp.split(z, 2, axis=-1)
    xr = centred_depthwise_conv(xr, conv_w, conv_b)
    y = (rg_lru(xr, w_a[0], b_a[0], w_x[0], b_x[0], lam[0], reverse=False)
         + rg_lru(xr, w_a[1], b_a[1], w_x[1], b_x[1], lam[1], reverse=True))
    y = y.astype(h.dtype) * jax.nn.gelu(gate)
    return y @ w_out

def sq_relu_mlp(h, w1, w2):
    return jnp.square(jax.nn.relu(h @ w1)) @ w2

def first_inputs(seed: int = 0) -> dict:
    key = jax.random.key(seed)
    ks = jax.random.split(key, 24)
    nrm = lambda k, shape, s: jax.random.normal(k, shape, jnp.float32) * s
    u = jax.random.uniform(ks[17], (N_RNN_LAYERS, 2, D_RNN), jnp.float32, 0.9, 0.999)
    s_lam = u ** (1.0 / LRU_C)
    lam = jnp.log(s_lam) - jnp.log1p(-s_lam)
    return {
        "x": nrm(ks[0], (BATCH, SEQ, D_MODEL), 1.0),
        "c": nrm(ks[1], (BATCH, D_MODEL), 1.0),
        "ada_w": nrm(ks[2], (DEPTH, 2, D_MODEL, 3 * D_MODEL), ADA_INIT * D_MODEL ** -0.5),
        "ada_b": nrm(ks[3], (DEPTH, 2, 3 * D_MODEL), 0.01),
        "ln_g": 1.0 + nrm(ks[4], (DEPTH, 2, D_MODEL), 0.02),
        "ln_b": nrm(ks[5], (DEPTH, 2, D_MODEL), 0.02),
        "attn_w_in": nrm(ks[6], (N_ATTN_LAYERS, D_MODEL, (N_Q_HEADS + 2 * N_KV_HEADS) * HEAD_DIM), D_MODEL ** -0.5),
        "attn_w_out": nrm(ks[7], (N_ATTN_LAYERS, N_Q_HEADS * HEAD_DIM, D_MODEL), DN_BETA * (N_Q_HEADS * HEAD_DIM) ** -0.5),
        "attn_sinks": nrm(ks[8], (N_ATTN_LAYERS, N_Q_HEADS), 1.0),
        "rnn_w_in": nrm(ks[9], (N_RNN_LAYERS, D_MODEL, 2 * D_RNN), D_MODEL ** -0.5),
        "rnn_conv_w": nrm(ks[10], (N_RNN_LAYERS, CONV_W, D_RNN), CONV_W ** -0.5),
        "rnn_conv_b": nrm(ks[11], (N_RNN_LAYERS, D_RNN), 0.01),
        "rnn_w_a": nrm(ks[12], (N_RNN_LAYERS, 2, N_RNN_BLOCKS, RNN_BLOCK_W, RNN_BLOCK_W), RNN_BLOCK_W ** -0.5),
        "rnn_b_a": nrm(ks[13], (N_RNN_LAYERS, 2, D_RNN), 0.01),
        "rnn_w_x": nrm(ks[14], (N_RNN_LAYERS, 2, N_RNN_BLOCKS, RNN_BLOCK_W, RNN_BLOCK_W), RNN_BLOCK_W ** -0.5),
        "rnn_b_x": nrm(ks[15], (N_RNN_LAYERS, 2, D_RNN), 0.01),
        "rnn_lam": lam,
        "rnn_w_out": nrm(ks[16], (N_RNN_LAYERS, D_RNN, D_MODEL), DN_BETA * D_RNN ** -0.5),
        "mlp_w1": nrm(ks[18], (DEPTH, D_MODEL, D_FF), D_MODEL ** -0.5),
        "mlp_w2": nrm(ks[19], (DEPTH, D_FF, D_MODEL), DN_BETA * D_FF ** -0.5),
    }

def first_block(x, c, ada_w, ada_b, ln_g, ln_b, attn_w_in, attn_w_out, attn_sinks,
              rnn_w_in, rnn_conv_w, rnn_conv_b, rnn_w_a, rnn_b_a, rnn_w_x, rnn_b_x, rnn_lam,
              rnn_w_out, mlp_w1, mlp_w2):
    for i in range(DEPTH):
        j = i // N_MIXERS
        shift, scale, gate = ada_modulation(c, ada_w[i, 0], ada_b[i, 0])
        h = x * (1.0 + scale) + shift
        if i % N_MIXERS == 0:
            y = windowed_gqa(h, attn_w_in[j], attn_w_out[j], attn_sinks[j])
        else:
            y = recurrent_block(h, rnn_w_in[j], rnn_conv_w[j], rnn_conv_b[j], rnn_w_a[j], rnn_b_a[j],
                                rnn_w_x[j], rnn_b_x[j], rnn_lam[j], rnn_w_out[j])
        x = layer_norm(DN_ALPHA * x + (1.0 + gate) * y, ln_g[i, 0], ln_b[i, 0])
        shift, scale, gate = ada_modulation(c, ada_w[i, 1], ada_b[i, 1])
        y = sq_relu_mlp(x * (1.0 + scale) + shift, mlp_w1[i], mlp_w2[i])
        x = layer_norm(DN_ALPHA * x + (1.0 + gate) * y, ln_g[i, 1], ln_b[i, 1])
    return x


N_HEADS_A = 16
N_KV_A = 4
HEAD_DIM_A = 64
N_HEADS_B = 8
KEY_DIM_B = 128
VAL_DIM_B = 128
CONV_K = 4
CHUNK = 64
D_FF_2 = 2816
NUM_BUCKETS = 32
MAX_DISTANCE = 128
DN_ALPHA_2 = (2 * DEPTH) ** 0.25
DN_BETA_2 = (8 * DEPTH) ** -0.25
NORM_EPS = 1e-6
NEG_INF = -1e30

Q_A = N_HEADS_A * HEAD_DIM_A
KV_W = N_KV_A * HEAD_DIM_A
QK_B = N_HEADS_B * KEY_DIM_B
V_B = N_HEADS_B * VAL_DIM_B
CONV_CH = 2 * QK_B + V_B
SPLIT_SIZES = (Q_A, KV_W, KV_W, CONV_CH, N_HEADS_B, N_HEADS_B, V_B, 2 * D_MODEL)
N_IN = sum(SPLIT_SIZES)
SPLIT_POINTS = tuple(int(s) for s in np.cumsum(SPLIT_SIZES)[:-1])


def layernorm(x, g, b):
    xf = x.astype(jnp.float32)
    mu = xf.mean(-1, keepdims=True)
    var = jnp.square(xf - mu).mean(-1, keepdims=True)
    y = (xf - mu) * lax.rsqrt(var + LN_EPS) * g.astype(jnp.float32) + b.astype(jnp.float32)
    return y.astype(x.dtype)

def swiglu(x, w13, w2):
    gate, up = jnp.split(x @ w13, 2, axis=-1)
    return (jax.nn.silu(gate) * up) @ w2

def t5_bucket(rel):
    n = jnp.maximum(rel, 0)
    max_exact = NUM_BUCKETS // 2
    nf = jnp.maximum(n, 1).astype(jnp.float32)
    large = max_exact + (jnp.log(nf / max_exact) / math.log(MAX_DISTANCE / max_exact)
                         * (NUM_BUCKETS - max_exact)).astype(jnp.int32)
    large = jnp.minimum(large, NUM_BUCKETS - 1)
    return jnp.where(n < max_exact, n, large)

def band_rel():
    r = jnp.arange(WINDOW)[:, None]
    j = jnp.arange(2 * WINDOW)[None, :]
    return r + WINDOW - j

def sliding_window_attention(q, k, v, pos_bias, sink):
    b, l = q.shape[:2]
    nb = l // WINDOW
    grp = N_HEADS_A // N_KV_A
    qb = (q.astype(jnp.float32) * HEAD_DIM_A ** -0.5).reshape(b, nb, WINDOW, N_KV_A, grp, HEAD_DIM_A)
    kb = k.astype(jnp.float32).reshape(b, nb, WINDOW, N_KV_A, HEAD_DIM_A)
    vb = v.astype(jnp.float32).reshape(b, nb, WINDOW, N_KV_A, HEAD_DIM_A)

    def with_prev(t):
        prev = jnp.concatenate([jnp.zeros_like(t[:, :1]), t[:, :-1]], axis=1)
        return jnp.concatenate([prev, t], axis=2)

    kk, vv = with_prev(kb), with_prev(vb)
    rel = band_rel()
    in_band = (rel >= 0) & (rel < WINDOW)
    key_in_own_block = jnp.arange(2 * WINDOW) >= WINDOW
    bias = pos_bias.reshape(N_KV_A, grp, WINDOW, 2 * WINDOW)
    sk = sink.astype(jnp.float32).reshape(N_KV_A, grp, 1, 1)

    def one_block(args):
        qi, ki, vi, i = args
        s = jnp.einsum('bqkgd,bskd->bkgqs', qi, ki) + bias
        valid = in_band & ((i > 0) | key_in_own_block)
        s = jnp.where(valid, s, NEG_INF)
        m = jnp.maximum(s.max(-1, keepdims=True), sk)
        p = jnp.exp(s - m)
        p = p / (p.sum(-1, keepdims=True) + jnp.exp(sk - m))
        return jnp.einsum('bkgqs,bskd->bqkgd', p, vi)

    o = lax.map(one_block, (jnp.moveaxis(qb, 1, 0), jnp.moveaxis(kk, 1, 0),
                            jnp.moveaxis(vv, 1, 0), jnp.arange(nb)))
    return jnp.moveaxis(o, 0, 1).reshape(b, l, Q_A)

def causal_depthwise_conv(u, w):
    return lax.conv_general_dilated(u, w[:, None, :].astype(u.dtype), window_strides=(1,),
                                    padding=[(CONV_K - 1, 0)],
                                    dimension_numbers=('NWC', 'WIO', 'NWC'),
                                    feature_group_count=u.shape[-1])

def l2norm(t):
    t = t.astype(jnp.float32)
    return t * lax.rsqrt(jnp.sum(t * t, -1, keepdims=True) + NORM_EPS)

def gated_delta_rule(q, k, v, g, beta):
    b, l, h, dk = q.shape
    dv = v.shape[-1]
    n = l // CHUNK

    def chunked(t):
        return t.reshape(b, n, CHUNK, h, t.shape[-1]).transpose(0, 3, 1, 2, 4)

    q = chunked(q * dk ** -0.5)
    k = chunked(k)
    v = chunked(v)
    g = jnp.cumsum(g.reshape(b, n, CHUNK, h).transpose(0, 3, 1, 2), axis=-1)
    beta = beta.reshape(b, n, CHUNK, h).transpose(0, 3, 1, 2)[..., None]
    kb, vb = k * beta, v * beta

    causal = jnp.tril(jnp.ones((CHUNK, CHUNK), bool))
    strict = jnp.tril(jnp.ones((CHUNK, CHUNK), bool), -1)
    decay = jnp.exp(jnp.where(causal, g[..., :, None] - g[..., None, :], NEG_INF))
    lower = jnp.where(strict, jnp.einsum('bhncd,bhnmd->bhncm', kb, k) * decay, 0.0)
    eye = jnp.eye(CHUNK, dtype=jnp.float32)
    t_inv = lax.linalg.triangular_solve(lower + eye, jnp.broadcast_to(eye, lower.shape),
                                        left_side=True, lower=True, unit_diagonal=True)
    u = t_inv @ vb
    w = t_inv @ (kb * jnp.exp(g)[..., None])
    a_intra = jnp.where(causal, jnp.einsum('bhncd,bhnmd->bhncm', q, k) * decay, 0.0)
    g_last = g[..., -1]
    k_tail = k * jnp.exp(g_last[..., None] - g)[..., None]
    q_dec = q * jnp.exp(g)[..., None]

    def step(s, xs):
        qd, kt, uc, wc, ac, gl = xs
        v_new = uc - jnp.einsum('bhcd,bhde->bhce', wc, s)
        o = jnp.einsum('bhcd,bhde->bhce', qd, s) + jnp.einsum('bhcm,bhme->bhce', ac, v_new)
        s = s * jnp.exp(gl)[..., None, None] + jnp.einsum('bhcd,bhce->bhde', kt, v_new)
        return s, o

    xs = tuple(jnp.moveaxis(t, 2, 0) for t in (q_dec, k_tail, u, w, a_intra, g_last))
    s0 = jnp.zeros((b, h, dk, dv), jnp.float32)
    _, o = lax.scan(step, s0, xs)
    return o.transpose(1, 0, 3, 2, 4).reshape(b, l, h, dv)

def hybrid_mixer(x, w_in, conv_w, a_log, dt_bias, dn_norm_g, sink,
                 w_branch_a, w_branch_b, w_out, pos_bias):
    b, l, _ = x.shape
    hcat = x @ w_in
    qa, ka, va, qkv_b, beta_raw, dt_raw, z, gate_raw = jnp.split(hcat, SPLIT_POINTS, axis=-1)

    ya = sliding_window_attention(qa.reshape(b, l, N_HEADS_A, HEAD_DIM_A),
                                  ka.reshape(b, l, N_KV_A, HEAD_DIM_A),
                                  va.reshape(b, l, N_KV_A, HEAD_DIM_A), pos_bias, sink)
    ya = ya.astype(x.dtype) @ w_branch_a

    qkv_b = jax.nn.silu(causal_depthwise_conv(qkv_b, conv_w))
    qb, kb, vb = jnp.split(qkv_b, (QK_B, 2 * QK_B), axis=-1)
    qb = l2norm(qb.reshape(b, l, N_HEADS_B, KEY_DIM_B))
    kb = l2norm(kb.reshape(b, l, N_HEADS_B, KEY_DIM_B))
    vb = vb.reshape(b, l, N_HEADS_B, VAL_DIM_B).astype(jnp.float32)
    beta = jax.nn.sigmoid(beta_raw.astype(jnp.float32))
    g = -jnp.exp(a_log.astype(jnp.float32)) * jax.nn.softplus(
        dt_raw.astype(jnp.float32) + dt_bias.astype(jnp.float32))
    o = gated_delta_rule(qb, kb, vb, g, beta)
    o = (o * lax.rsqrt(jnp.mean(o * o, -1, keepdims=True) + NORM_EPS)
         * dn_norm_g.astype(jnp.float32)
         * jax.nn.silu(z.reshape(b, l, N_HEADS_B, VAL_DIM_B).astype(jnp.float32)))
    yb = o.reshape(b, l, V_B).astype(x.dtype) @ w_branch_b

    gate_a, gate_b = jnp.split(jax.nn.sigmoid(gate_raw), 2, axis=-1)
    return (gate_a * ya + gate_b * yb) @ w_out

def second_inputs(seed: int = 0) -> dict:
    key = jax.random.key(seed)
    ks = jax.random.split(key, 16)
    f32 = jnp.float32

    def nrm(k, shape, scale):
        return jax.random.normal(k, shape, f32) * scale

    dt = jnp.exp(jax.random.uniform(ks[9], (DEPTH, N_HEADS_B), f32, math.log(1e-3), math.log(1e-1)))
    return {
        "x": nrm(ks[0], (BATCH, SEQ, D_MODEL), 1.0),
        "rel_bias": nrm(ks[1], (NUM_BUCKETS, N_HEADS_A), 0.5),
        "ln_g": 1.0 + nrm(ks[2], (DEPTH, 3, D_MODEL), 0.05),
        "ln_b": nrm(ks[3], (DEPTH, 3, D_MODEL), 0.02),
        "ffn_w13": nrm(ks[4], (DEPTH, 2, D_MODEL, 2 * D_FF_2), D_MODEL ** -0.5),
        "ffn_w2": nrm(ks[5], (DEPTH, 2, D_FF_2, D_MODEL), DN_BETA_2 * D_FF_2 ** -0.5),
        "w_in": nrm(ks[6], (DEPTH, D_MODEL, N_IN), D_MODEL ** -0.5),
        "conv_w": nrm(ks[7], (DEPTH, CONV_K, CONV_CH), CONV_K ** -0.5),
        "a_log": jnp.log(jax.random.uniform(ks[8], (DEPTH, N_HEADS_B), f32, 1.0, 16.0)),
        "dt_bias": dt + jnp.log(-jnp.expm1(-dt)),
        "dn_norm_g": 1.0 + nrm(ks[10], (DEPTH, VAL_DIM_B), 0.05),
        "sinks": nrm(ks[11], (DEPTH, N_HEADS_A), 0.5),
        "w_branch_a": nrm(ks[12], (DEPTH, Q_A, D_MODEL), Q_A ** -0.5),
        "w_branch_b": nrm(ks[13], (DEPTH, V_B, D_MODEL), V_B ** -0.5),
        "w_out": nrm(ks[14], (DEPTH, D_MODEL, D_MODEL), DN_BETA_2 * D_MODEL ** -0.5),
    }

def second_block(x, rel_bias, ln_g, ln_b, ffn_w13, ffn_w2, w_in, conv_w, a_log, dt_bias,
              dn_norm_g, sinks, w_branch_a, w_branch_b, w_out):
    pos_bias = jnp.transpose(rel_bias[t5_bucket(band_rel())], (2, 0, 1)).astype(jnp.float32)
    for i in range(DEPTH):
        x = layernorm(DN_ALPHA_2 * x + 0.5 * swiglu(x, ffn_w13[i, 0], ffn_w2[i, 0]), ln_g[i, 0], ln_b[i, 0])
        y = hybrid_mixer(x, w_in[i], conv_w[i], a_log[i], dt_bias[i], dn_norm_g[i], sinks[i],
                         w_branch_a[i], w_branch_b[i], w_out[i], pos_bias)
        x = layernorm(DN_ALPHA_2 * x + y, ln_g[i, 1], ln_b[i, 1])
        x = layernorm(DN_ALPHA_2 * x + 0.5 * swiglu(x, ffn_w13[i, 1], ffn_w2[i, 1]), ln_g[i, 2], ln_b[i, 2])
    return x


def setup_inputs(seed=0):
    out = dict(first_inputs(seed))
    for name, value in second_inputs(seed + 1).items():
        if name != "x":
            out[name + "_2"] = value
    return out


def reference(
    x, c, ada_w, ada_b, ln_g, ln_b, attn_w_in, attn_w_out, attn_sinks, rnn_w_in, rnn_conv_w,
    rnn_conv_b, rnn_w_a, rnn_b_a, rnn_w_x, rnn_b_x, rnn_lam, rnn_w_out, mlp_w1, mlp_w2,
    rel_bias_2, ln_g_2, ln_b_2, ffn_w13_2, ffn_w2_2, w_in_2, conv_w_2, a_log_2, dt_bias_2,
    dn_norm_g_2, sinks_2, w_branch_a_2, w_branch_b_2, w_out_2,
):
    x = first_block(
        x, c, ada_w, ada_b, ln_g, ln_b, attn_w_in, attn_w_out, attn_sinks, rnn_w_in, rnn_conv_w,
        rnn_conv_b, rnn_w_a, rnn_b_a, rnn_w_x, rnn_b_x, rnn_lam, rnn_w_out, mlp_w1, mlp_w2,
    )
    return second_block(
        x, rel_bias_2, ln_g_2, ln_b_2, ffn_w13_2, ffn_w2_2, w_in_2, conv_w_2, a_log_2,
        dt_bias_2, dn_norm_g_2, sinks_2, w_branch_a_2, w_branch_b_2, w_out_2,
    )


_drawn_inputs = setup_inputs


def setup_inputs(seed=0):
    import zlib

    import numpy as np

    out = dict(_drawn_inputs(seed))
    spreads = {}
    factors = {'attn_sinks': 8.0,
     'rnn_conv_b': 3.249,
     'rnn_b_a': 47.308,
     'rnn_b_x': 8.0,
     'dn_norm_g_2': 6.867,
     'sinks_2': 8.0,
     'rel_bias_2': 3.361}
    for name, (base, spread) in spreads.items():
        noise = np.random.default_rng([zlib.crc32(name.encode()), seed]).standard_normal(out[name].shape)
        drawn = base * np.exp(spread * noise) if base else spread * noise
        out[name] = __import__('jax').numpy.asarray(drawn.astype(out[name].dtype))
    for name, factor in factors.items():
        out[name] = (out[name] * factor).astype(out[name].dtype)
    return out
```

```python
import math
from contextlib import ExitStack

import numpy as np

import concourse.bass as bass
from concourse import mybir

F32 = mybir.dt.float32
F32R = mybir.dt.float32r
ALU = mybir.AluOpType
ACT = mybir.ActivationFunctionType
AX = mybir.AxisListType

P = 128
S = 256
NT = S // P
D = 1024
KC = D // P
NEG = -1e30
N_SUB = 10
LN_EPS = 1e-5
ALPHA = 4.0 ** 0.25
NRAW = 3
NSPL = 3
SLOT = 2048
NTB = 4
NADR = 4
HD1 = 128
NH1 = 8
RB_N = 16
RB_W = 96
FF1 = 4096
FF2 = 2816
NB_BUCKETS = 32
NORM_EPS = 1e-6
EXT = 3 * P


def shape_constants():
    c = {}
    c["ident"] = np.eye(P, dtype=np.float32)
    q = np.arange(P)[:, None, None] + P * np.arange(2)[None, :, None]
    k = np.arange(S)[None, None, :]
    c["window"] = np.where(np.abs(q - k) <= P, 0.0, NEG).astype(np.float32).reshape(P, 2 * S)
    inv = np.float32(500000.0) ** (-np.arange(0, 32, 2, dtype=np.float32) / np.float32(32))
    ang = np.arange(S, dtype=np.float32)[:, None] * inv[None, :].astype(np.float32)
    cs = np.cos(ang).T.astype(np.float32)
    sn = np.sin(ang).T.astype(np.float32)
    c["rope_cos"] = np.tile(np.concatenate([cs, cs]), (1, 2)).astype(np.float32)
    c["rope_sin"] = np.tile(np.concatenate([sn, sn]), (1, 2)).astype(np.float32)
    rot = np.zeros((32, 32), np.float32)
    for m in range(16):
        rot[m + 16, m] = -1.0
        rot[m, m + 16] = 1.0
    c["rope_rot"] = rot
    rel = 255 - np.arange(EXT)
    n = np.maximum(rel, 0)
    nf = np.maximum(n, 1).astype(np.float32)
    large = 16 + (np.log(nf / np.float32(16)) / np.float32(math.log(128 / 16)) * np.float32(16)).astype(np.int32)
    bucket = np.where(n < 16, n, np.minimum(large, 31))
    band = (rel >= 0) & (rel < P)
    hot = np.zeros((33, EXT), np.float32)
    for m in range(EXT):
        if band[m]:
            hot[bucket[m], m] = 1.0
        else:
            hot[32, m] = NEG
    c["bucket_hot"] = hot
    mi, ci = np.arange(P)[:, None], np.arange(P)[None, :]
    c["causal_t"] = np.where(ci >= mi, 0.0, NEG).astype(np.float32)
    lv = []
    for i in range(7):
        s = 1 << i
        lv.append(((ci // (2 * s) == mi // (2 * s)) & (ci % (2 * s) >= s) & (mi % (2 * s) < s)).astype(np.float32))
    c["levels_t"] = np.concatenate(lv, 1)
    sc = np.ones((16, 1), np.float32)
    sc[0:8] = 1.0 / 128
    c["norm_scale"] = sc
    return c


def build(nc, I, C, out, counts, n_sub):
    final = len(counts) > 0
    known = dict(counts)
    made = {}
    ctx = ExitStack()
    with ctx:
        base = -(-nc.sbuf_base // 32) * 32
        KB = 1024
        pos = {"at": base}

        def put(name, shape, dt=F32, at=None):
            n = 4
            for x in shape[1:]:
                n *= x
            n = -(-n // 32) * 32
            off = pos["at"] if at is None else at
            if at is None:
                pos["at"] += n
            return nc.alloc_sbuf_tensor_at(name, shape, dt, offset=off)

        RAW = put("weights_raw", [P, NRAW, SLOT])
        WHI = put("weights_hi", [P, NSPL, SLOT], F32R)
        WLO = put("weights_lo", [P, NSPL, SLOT], F32R)
        XN = put("x_rows", [P, NT, D])
        XS = put("x_scaled", [P, NT, D])
        XH = put("xt_hi", [P, KC, S], F32R, at=pos["at"])
        act1 = pos["at"]
        pos["at"] += 8 * KB
        XL = put("xt_lo", [P, KC, S], F32R)
        act2 = pos["at"]
        OH = put("ot_hi", [P, KC, S], F32R)
        OL = put("ot_lo", [P, KC, S], F32R)
        YH = put("rnn_yt_hi", [RB_W, 4, 2, S], F32R, at=act2)
        YL = put("rnn_yt_lo", [RB_W, 4, 2, S], F32R, at=act2 + 8 * KB)
        gbc_at = pos["at"]
        GB = put("ln_gb_rows", [P, 2, D])
        IDN = put("ident", [P, P])
        ONES = put("ones", [P, P])
        ESEL = put("ones_column", [P, 31])
        NSC = put("norm_scale", [16, 1])
        lv_at = pos["at"]
        WIN = put("window", [P, 2 * S], at=lv_at)
        COS = put("rope_cos", [32, 2 * S], at=lv_at + 2 * KB)
        SIN = put("rope_sin", [32, 2 * S], at=lv_at + 4 * KB)
        ROT = put("rope_rot", [32, 32], at=lv_at + 6 * KB)
        LVL = put("levels_t", [P, 7 * P], at=lv_at)
        TRI = put("causal_t", [P, P], at=lv_at + 3584)
        pos["at"] = lv_at + 6 * KB + 128
        LNC1 = put("ln1_cols", [P, 64])
        CC = put("c_cols", [P, 8])
        ADB = put("ada_bias_cols", [P, 96])
        LNC2 = put("ln2_cols", [P, 96])
        CW2 = put("conv2_cols", [P, 2, 96])
        DNG = put("dn_norm_cols", [P, 2])
        RC1 = put("rnn_conv_cols", [RB_W, 80])
        RC2 = put("rnn_gate_cols", [RB_W, 96])
        MOD = put("ada_mod_cols", [P, 4, 24])
        GP = put("prep_scale", [P, 4, 8])
        BP = put("prep_shift", [P, 4, 8])
        SNK = put("sinks1", [P, 8])
        SNK2 = put("sinks2", [P, 2, 16])
        AL2 = put("a_log_dt", [8, 8])
        ST = put("ln_stats", [P, NT, 2, 6])
        MV = put("ln_mean_var", [P, NT, 2])
        RV = put("ln_rstd", [P, NT, 2])
        RCOL = put("rnn_decay_cols", [RB_W, 8, 32])
        AT1 = put("attn_small", [P, 6, 16])
        A2S = put("attn2_small", [P, 3, 8])
        GCOL = put("g_cols", [P, 4, 8])
        GLT = put("g_last_tail", [P, 2, 8])
        gate_at = pos["at"]
        GATE = put("gate_rows", [P, D])
        pos["at"] += 64
        hid_at = pos["at"]
        HH = put("hid_hi", [P, 2, 512], F32R)
        HL = put("hid_lo", [P, 2, 512], F32R)
        RB = put("hid_act", [P, 2, 512])
        VB = put("hid_val", [P, 2, 512])
        area = pos["at"]

        ACC = put("ada_acc", [P, 3, D], at=area)
        ADR = put("ada_ring", [P, NADR, D], at=area + 12 * KB)
        a = area + (12 + 4 * NADR) * KB
        QT = put("q1_t", [P, NH1, S], at=a)
        KT = put("k1_t", [P, 2, S], at=a + 8 * KB)
        VR = put("v1_rows", [P, NT, S], at=a + 10 * KB)
        PTB = put("probs1_t", [P, 2, 4, P], at=a + 12 * KB)
        PR = put("probs1", [P, NH1, 2, S], at=hid_at)
        PST = put("param_rows", [P, 8, P], at=hid_at)
        RTMP = put("rope_tmp", [32, 2, 512], at=a + 12 * KB)
        EXS = put("bias_stage", [P, 2, EXT], at=hid_at + 8 * KB)
        HOT = put("bucket_hot", [33, EXT], at=hid_at + 4 * KB)
        RBI = put("rel_bias", [33, 16], at=hid_at + 4 * KB + 1536)
        XTF = put("xt", [P, KC, S], at=hid_at)
        a = hid_at
        XC = put("rnn_conv_out", [RB_W, RB_N, S], at=a)
        GG = put("rnn_gelu_gate", [RB_W, RB_N, S], at=a + 16 * KB)
        WG = put("rnn_gate_w", [RB_W, 2, 8, RB_W], at=a + 32 * KB)
        RR = put("rnn_r", [RB_W, 2, 2, 2, S], at=a + 38 * KB)
        RI = put("rnn_i", [RB_W, 2, 2, 2, S], at=a + 46 * KB)
        RA = put("rnn_a", [RB_W, 2, 2, 2, S], at=a + 54 * KB)
        XP = put("rnn_conv_in", [RB_W, 2, 2, 260], at=gbc_at)
        RTM = put("rnn_tmp", [RB_W, 2, 2, S], at=lv_at)
        a = hid_at
        CB = put("conv_qkv_t", [P, 24, S], at=a)
        ZT = put("z_silu_t", [P, 8, S], at=a + 24 * KB)
        QA = put("qa_t", [P, 8, S], at=a + 32 * KB)
        M1 = put("mix_t", [P, 8, S], at=a + 32 * KB)
        KA = put("ka_t", [P, 2, S], at=a + 40 * KB)
        VA = put("va_rows", [P, NT, S], at=a + 42 * KB)
        PA = put("probs_a", [P, 3, 384], at=a + 44 * KB)
        BI = put("bias_rows", [P, 3, S], at=a + 44 * KB + 4608)
        PTA = put("probs_a_t", [P, 2, 384], at=a + 44 * KB + 7680)
        TH = put("silu_tanh", [P, 2, 2, S], at=gbc_at)
        GBT = put("gate_b_t", [P, 8, S], at=a + 40 * KB)
        b = a + 55 * KB
        CIN = put("conv_in", [P, 2, 2, 260], at=gate_at)
        ROWS = put("dn_rows", [16, 6, S], at=b)
        a2 = a + 48 * KB
        EG = put("exp_g", [P, 2, S], at=a2)
        KBT = put("k_beta_t", [P, 2, S], at=a2 + 2 * KB)
        GT = put("gate_a_t", [P, 2, S], at=a2 + 2 * KB)
        KBG = put("k_beta_g_t", [P, 4, P], at=a2 + 4 * KB)
        QD = put("q_decay_t", [P, 4, P], at=gate_at)
        KTL = put("k_tail_rows", [P, 4, P], at=gate_at + 2 * KB)
        SQ = put("squares", [P, 2, 256], at=a2 + 4 * KB)
        LT = put("l_t", [P, 2, 4, P], at=act2)
        EA = put("a_t", [P, 2, 4, P], at=act2 + 4 * KB)
        MM = put("l_level_t", [P, 2, 4, P], at=act2 + 8 * KB)
        XX = put("x_level", [P, 2, 4, P], at=act2 + 12 * KB)
        TT = put("t_inv", [P, 2, 4, P], at=gbc_at)
        UU = put("t_inv_t", [P, 2, 4, P], at=gbc_at + 4 * KB)

        TB = ctx.enter_context(nc.psum_tensor("tiles", [P, NTB, 512], F32))
        Y = ctx.enter_context(nc.psum_tensor("y_rows", [P, NT, D], F32))

        def y_bank(i):
            return Y[:, i // 2, i % 2 * 512:i % 2 * 512 + 512]

        BIAS = nc.dram_tensor("bias_ext", [16, P, EXT], F32, kind="Internal").ap()

        sems = {}

        def sem(name):
            if name not in sems:
                sems[name] = ctx.enter_context(nc.semaphore(name))
            return sems[name]

        for name in sorted({k[0] for k in known}):
            sem(name)
        level = {}

        def inc(name, key=None, by=1):
            level[name] = level.get(name, 0) + by
            made[(name, key)] = level[name]
            return sem(name), by

        def past(name, key=None):
            return sem(name), known.get((name, key), 1)

        def link(eng, ins, name):
            level[name] = level.get(name, 0) + 1
            ins.then_inc(sem(name), 1)
            eng.wait_ge(sem(name), level[name])

        block = ctx.enter_context(nc.Block())

        slots = []

        def kview(w, c0, n):
            return w.rearrange("(k p) n -> p k n", p=P)[:, :, c0:c0 + n]

        def add_cols(label, w, c0, n):
            slots.append((label, P, (KC, n), [(None, kview(w, c0, n))]))

        def add_rows(label, w, r0, p, nk):
            slots.append((label, p, (nk, D), [(None, w[r0:r0 + p * nk, :].rearrange("(k p) n -> p k n", p=p))]))

        def plan():
            for s in range(n_sub):
                if s == 0:
                    for i in range(6):
                        add_cols((s, "in", i), I["attn_w_in"][0], 256 * i, 256)
                    for i in range(4):
                        add_rows((s, "out", i), I["attn_w_out"][0], 256 * i, P, 2)
                elif s in (1, 3):
                    n = FF1 // 256
                    for i in range(n + 1):
                        if i < n:
                            add_cols((s, "w1", i), I["mlp_w1"][s // 2], 256 * i, 256)
                        if i > 0:
                            add_rows((s, "w2", i - 1), I["mlp_w2"][s // 2], 256 * (i - 1), P, 2)
                elif s == 2:
                    for i in range(8):
                        add_cols((s, "gt", i), I["rnn_w_in"][0], 192 * (8 + i), 192)
                    for i in range(12):
                        if i < 8:
                            add_cols((s, "in", i), I["rnn_w_in"][0], 192 * i, 192)
                        if i >= 4:
                            add_rows((s, "out", i - 4), I["rnn_w_out"][0], 192 * (i - 4), RB_W, 2)
                elif s % 3 != 2:
                    l, f = (s - 4) // 3, (s - 4) % 3 // 2
                    n = FF2 // 256
                    for i in range(n + 1):
                        if i < n:
                            add_cols((s, "g", i), I["ffn_w13_2"][l, f], 256 * i, 256)
                            add_cols((s, "u", i), I["ffn_w13_2"][l, f], FF2 + 256 * i, 256)
                        if i > 0:
                            add_rows((s, "w2", i - 1), I["ffn_w2_2"][l, f], 256 * (i - 1), P, 2)
                else:
                    l = (s - 4) // 3
                    w = I["w_in_2"][l]
                    for i in range(4):
                        c, gg = i // 2, i % 2
                        src = [((slice(None), g * P + hh * 64, 64), kview(w, (2 * c + hh) * 256 + (2 * gg + g) * 64, 64))
                               for g in range(2) for hh in range(2)]
                        slots.append(((s, "qa", i), P, (KC, 256), src))
                    add_cols((s, "ka", 0), w, 1024, 256)
                    add_cols((s, "va", 0), w, 1280, 256)
                    add_cols((s, "bd", 0), w, 4608, 136)
                    for i in range(12):
                        add_cols((s, "cv", i), w, 1536 + 256 * i, 256)
                    for i in range(4):
                        add_cols((s, "z", i), w, 4624 + 256 * i, 256)
                    for i in range(4):
                        src = []
                        for hh in range(2):
                            for c in range(2):
                                r = (2 * c + hh) * 256
                                src.append(((slice(64 * hh, 64 * hh + 64), 4 * c, 4),
                                            I["w_branch_a_2"][l][r:r + 256, 256 * i:256 * i + 256]
                                            .rearrange("(g d) n -> d g n", d=64)))
                        slots.append(((s, "ba", i), P, (KC, 256), src))
                    for i in range(4):
                        add_cols((s, "gb", i), w, 6672 + 256 * i, 256)
                    for i in range(4):
                        add_cols((s, "ga", i), w, 5648 + 256 * i, 256)
                    for i in range(4):
                        add_cols((s, "bb", i), I["w_branch_b_2"][l], 256 * i, 256)
                    for i in range(4):
                        add_rows((s, "out", i), I["w_out_2"][l], 256 * i, P, 2)

        plan()
        number = {x[0]: n for n, x in enumerate(slots)}
        slot_end = [("rows_done" if x[0][1] in ("w2", "out") else "tile_done", x[0]) for x in slots]
        landed_at = {}
        total = [0] * NRAW
        for n, x in enumerate(slots):
            total[n % NRAW] += 16 * len(x[3])
            landed_at[n] = total[n % NRAW]

        y_end = {x[0][0]: ("rows_done", x[0]) for x in slots if x[0][1] in ("w2", "out")}

        def slot_view(ring, n, depth):
            _, p, (a_, b_), _ = slots[n]
            return ring[0:p, n % depth, 0:a_ * b_].rearrange("p (a b) -> p a b", a=a_)

        LN = {}
        for s in range(4):
            LN[s] = (I["ln_g"][s // 2, s % 2], I["ln_b"][s // 2, s % 2], LNC1[:, 8 * s:8 * s + 8],
                     LNC1[:, 32 + 8 * s:40 + 8 * s])
        for s in range(4, 10):
            i = s - 4
            LN[s] = (I["ln_g_2"][i // 3, i % 3], I["ln_b_2"][i // 3, i % 3], LNC2[:, 8 * i:8 * i + 8],
                     LNC2[:, 48 + 8 * i:56 + 8 * i])

        def is_mix(s):
            return s in (5, 8)

        def is_ffn(s):
            return s >= 4 and not is_mix(s)

        def row_view(x, p):
            return x.rearrange("(r p) -> r p", p=p)

        prm = []
        for s in range(4):
            prm.append((row_view(LN[s][0], P), 8 * s, 0))
            prm.append((row_view(LN[s][1], P), 32 + 8 * s, 0))
            prm.append((row_view(I["ada_b"][s // 2, s % 2], P), 24 * s, 1))
        prm.append((I["c"].rearrange("a (r p) -> (a r) p", p=P), 64, 0))
        for s in range(4, 10):
            prm.append((row_view(LN[s][0], P), 8 * (s - 4), 2))
            prm.append((row_view(LN[s][1], P), 48 + 8 * (s - 4), 2))
        for l in range(2):
            prm.append((I["conv_w_2"][l].rearrange("j (r p) -> (j r) p", p=P), 0, 3 + l))
        prm.append((I["dn_norm_g_2"], 0, 5))
        prm.append((I["rnn_conv_w"][0].rearrange("j (r p) -> (j r) p", p=RB_W), 0, 6))
        prm.append((I["rnn_conv_b"].rearrange("a (r p) -> (a r) p", p=RB_W), 64, 6))
        for n, name in enumerate(("rnn_b_a", "rnn_b_x", "rnn_lam")):
            prm.append((I[name][0].rearrange("j (r p) -> (j r) p", p=RB_W), 32 * n, 7))
        blocks = [(72, P, [LNC1[:, :], CC[:, :]]), (96, P, [ADB[:, :]]), (96, P, [LNC2[:, :]]), (96, P, [CW2[:, 0, :]]),
                  (96, P, [CW2[:, 1, :]]), (2, P, [DNG[:, :]]), (80, RB_W, [RC1[:, :]]), (96, RB_W, [RC2[:, :]])]

        n_ada = 24 * min(n_sub, 4)

        def ada_src(q):
            w = I["ada_w"][q // 48, q // 24 % 2]
            third, kc = divmod(q % 24, KC)
            return w[kc * P:(kc + 1) * P, third * D:(third + 1) * D]

        @block.sync
        def _(sp):
            def ada_load(q):
                if q >= NADR:
                    sp.wait_ge(*past("ada_used", q - NADR))
                sp.dma_start(ADR[:, q % NADR, :], ada_src(q)).then_inc(*inc(f"ada_in{q % NADR}", q, 16))

            for q in range(NADR):
                ada_load(q)
            for t in range(NT):
                sp.dma_start(XN[:, t, :], I["x"][0, t * P:(t + 1) * P, :]).then_inc(*inc("x_in", None, 16))

            def load(n):
                if n >= NRAW:
                    sp.wait_ge(*past("lo_ready", n - NRAW))
                view = slot_view(RAW, n, NRAW)
                for where, src in slots[n][3]:
                    if where is None:
                        dst = view
                    elif where[1] + where[2] <= KC and where[2] == 4:
                        dst = view[where[0], where[1]:where[1] + where[2], :]
                    else:
                        dst = view[where[0], :, where[1]:where[1] + where[2]]
                    sp.dma_start(dst, src).then_inc(*inc(f"landed{n % NRAW}", n, 16))

            for n in range(NRAW):
                load(n)
            for q in range(NADR, 24):
                ada_load(q)
            for n in range(NRAW, len(slots)):
                load(n)
            for t in range(NT):
                sp.wait_ge(*past("out_rows", t))
                sp.dma_start(out[0, t * P:(t + 1) * P, :], XN[:, t, :]).then_inc(*inc("out_done", None, 16))
            sp.wait_ge(*past("out_done"))

        @block.tensor
        def _(pe):
            tiles = [0]
            owner = {}

            def topen(label, consumer):
                t = tiles[0]
                tiles[0] += 1
                owner[t] = (label, consumer)
                made[("tile", label)] = t
                if t >= NTB:
                    pe.wait_ge(*past("free_" + owner[t - NTB][1], owner[t - NTB][0]))
                return TB[:, t % NTB, :]

            def open_slot(label):
                n = number[label]
                pe.wait_ge(*past("lo_ready", n))
                return n, slot_view(WHI, n, NSPL), slot_view(WLO, n, NSPL)

            def mm3(o, a, b, c, d, first, last):
                pe.matmul(o, a, c, start=first, stop=False)
                pe.matmul(o, a, d, start=False, stop=False)
                return pe.matmul(o, b, c, start=False, stop=last)

            def cols_slot(label, xh, xl, consumer, m=P, ready=None, nt=2, step=None):
                n, wh, wl = open_slot(label)
                bank = topen(label, consumer)
                nk = slots[n][2][0]
                for j in range(nt):
                    for k in range(nk):
                        if ready:
                            ready(k)
                        a_ = wh[:, k, (step or m) * j:(step or m) * j + m]
                        b_ = wl[:, k, (step or m) * j:(step or m) * j + m]
                        ins = mm3(bank[0:m, j * S:(j + 1) * S], a_, b_, xh[:, k, :], xl[:, k, :], k == 0, k == nk - 1)
                ins.then_inc(*inc("tile_done", label))

            def v_slot(label, xh, xl, ready=None):
                n, wh, wl = open_slot(label)
                bank = topen(label, "A")
                for t in range(NT):
                    for k in range(KC):
                        xa, xb = xh[:, k, t * P:(t + 1) * P], xl[:, k, t * P:(t + 1) * P]
                        ins = mm3(bank[:, t * S:(t + 1) * S], xa, xb, wh[:, k, :], wl[:, k, :], k == 0, k == KC - 1)
                ins.then_inc(*inc("tile_done", label))

            def rows_slot(label, lh, ll, k0, first, last, s):
                n, wh, wl = open_slot(label)
                for kk in range(2):
                    for t in range(NT):
                        xa, xb = lh(k0 + kk)[:, t * P:(t + 1) * P], ll(k0 + kk)[:, t * P:(t + 1) * P]
                        for h in range(2):
                            ins = mm3(Y[:, t, h * 512:(h + 1) * 512], xa, xb, wh[:, kk, h * 512:(h + 1) * 512],
                                      wl[:, kk, h * 512:(h + 1) * 512], first and kk == 0, last and kk == 1)
                ins.then_inc(*inc("rows_done", label))

            def y_wait(s):
                if s > 0:
                    for t in range(NT):
                        pe.wait_ge(*past("y_free", (s - 1, t)))

            def xready(s):
                seen = set()

                def f(k):
                    if k // 2 not in seen:
                        seen.add(k // 2)
                        pe.wait_ge(*past("xl_ready", (s, k // 2)))
                return f

            def ada_reduce(t):
                if 8 * t >= n_ada:
                    return
                pe.wait_ge(*past("ada_used", 8 * t + 7))
                bank = topen(("ada", t), "D")
                for j in range(8):
                    ins = pe.matmul(bank[:, j:j + 1], ACC[:, t % 3, j * P:(j + 1) * P], ONES[:, 0:1], start=True, stop=True)
                ins.then_inc(*inc("tile_done", ("ada", t)))

            def gate_rows(s):
                pe.wait_ge(*past("mod_ready", s))
                for h in range(2):
                    bank = topen(("gate", s, h), "A")
                    for j in range(4):
                        c0 = 16 + 4 * h + j
                        ins = pe.matmul(bank[:, j * P:(j + 1) * P], MOD[:, s, c0:c0 + 1].broadcast_to([P, P]), IDN[:, :],
                                        start=True, stop=True)
                    ins.then_inc(*inc("tile_done", ("gate", s, h)))

            def prep(s):
                for e in range(4):
                    bank = topen(("xt", s, e), "D")
                    for kk in range(2):
                        for t in range(NT):
                            if e == 0 and kk == 0:
                                if s == 0:
                                    pe.wait_ge(*past("x_in"))
                                else:
                                    pe.wait_ge(*past("xn_ready", (s - 1, t)))
                            k = 2 * e + kk
                            ins = pe.transpose(bank[:, kk * S + t * P:kk * S + (t + 1) * P], XN[:, t, k * P:(k + 1) * P],
                                               IDN[:, :])
                    ins.then_inc(*inc("tile_done", ("xt", s, e)))

            pe.wait_ge(*past("ident_in"))
            pe.wait_ge(*past("ones_ready"))
            for n, (rows, width, _) in enumerate(blocks):
                pe.wait_ge(*past(f"param_in{n}", None))
                bank = topen(("param", n), "D")
                pe.transpose(bank[0:width, 0:rows], PST[0:rows, n, 0:width], IDN[0:rows, 0:rows]).then_inc(*inc("tile_done", ("param", n)))
            pe.wait_ge(*past("rel_ready", None))
            for h in range(16):
                bank = topen(("ext", h), "A")
                pe.matmul(bank[:, 0:EXT], RBI[:, h:h + 1].broadcast_to([33, P]), HOT[:, :], start=True, stop=True).then_inc(*inc("tile_done", ("ext", h)))
            for t in range(3):
                ada_reduce(t)
            gate_rows(0)
            prep(0)


            for i in range(5):
                cols_slot((0, "in", i), XH, XL, "A", ready=xready(0))
            v_slot((0, "in", 5), XH, XL)
            ada_reduce(3)
            pe.wait_ge(*past("const_in"))
            for i in range(5):
                pe.wait_ge(*past("free_A", (0, "in", i)))
                src = QT[0:32, 2 * i:2 * i + 2, :] if i < 4 else KT[0:32, :, :]
                bank = topen(("rot", i), "D")
                pe.matmul(bank[0:32, :], ROT[:, :], src.rearrange("p a b -> p (a b)"), start=True, stop=True).then_inc(*inc("tile_done", ("rot", i)))

            def scores1(h):
                pe.wait_ge(*past("rope_ready", 4))
                bank = topen(("sc", h), "D")
                for b in range(2):
                    ins = pe.matmul(bank[:, b * S:(b + 1) * S], QT[:, h, b * P:(b + 1) * P], KT[:, h // 4, :],
                                    start=True, stop=True)
                ins.then_inc(*inc("tile_done", ("sc", h)))

            def turn1(h):
                pe.wait_ge(*past("probs_ready", h))
                bank = topen(("pt", h), "A")
                for b in range(2):
                    for k in range(2):
                        ins = pe.transpose(bank[:, (2 * b + k) * P:(2 * b + k + 1) * P], PR[:, h, b, k * P:(k + 1) * P],
                                           IDN[:, :])
                ins.then_inc(*inc("tile_done", ("pt", h)))

            def mix1(h):
                pe.wait_ge(*past("free_A", ("pt", h)))
                if h % 2 == 0:
                    pair["bank"] = topen(("o", h // 2), "D")
                for k in range(2):
                    lhs = VR[:, k, (h // 4) * P:(h // 4 + 1) * P]
                    rhs = PTB[:, h % 2, :, :].rearrange("p (b k) q -> p k b q", k=2)[:, k]
                    ins = pe.matmul(pair["bank"][:, (h % 2) * S:(h % 2 + 1) * S].rearrange("p (b q) -> p b q", b=2), lhs, rhs,
                                    start=(k == 0), stop=(k == 1))
                if h % 2 == 1:
                    ins.then_inc(*inc("tile_done", ("o", h // 2)))
                else:
                    ins.then_inc(*inc("mix_half", h))

            pair = {}
            pe.wait_ge(*past("free_A", (0, "in", 5)))
            for h in range(NH1 + 2):
                if h < NH1:
                    scores1(h)
                if 1 <= h <= NH1:
                    turn1(h - 1)
                if h >= 2:
                    mix1(h - 2)
                if h in (4, 6):
                    ada_reduce(2 + h // 2)
            for i in range(4):
                if i % 2 == 1:
                    ada_reduce(6 + i // 2)
                pe.wait_ge(*past("free_D", ("o", i)))
                rows_slot((0, "out", i), lambda k: OH[:, k, :], lambda k: OL[:, k, :], 2 * i, i == 0, i == 3, 0)

            def mlp(s):
                n = FF1 // 256
                for i in range(n + 1):
                    if i < n:
                        cols_slot((s, "w1", i), XH, XL, "A", ready=xready(s) if i == 0 else None)
                    if s == 1 and i % 4 == 3:
                        ada_reduce(8 + i // 4)
                    if i > 0:
                        hidden_rows(s, i - 1, n)

            def hidden_rows(s, i, n):
                pe.wait_ge(*past("hid_ready", (s, i)))
                if i == 0:
                    y_wait(s)
                hh, hl = HH[:, i % 2, :], HL[:, i % 2, :]
                rows_slot((s, "w2", i), lambda k: hh.rearrange("p (a b) -> p a b", a=2)[:, k],
                          lambda k: hl.rearrange("p (a b) -> p a b", a=2)[:, k], 0, i == 0, i == n - 1, s)

            def ffn(s):
                n = FF2 // 256
                for i in range(n + 1):
                    if i < n:
                        cols_slot((s, "g", i), XH, XL, "A", ready=xready(s) if i == 0 else None)
                        cols_slot((s, "u", i), XH, XL, "D")
                    if i > 0:
                        hidden_rows(s, i - 1, n)

            def between(s):
                if s + 1 < n_sub:
                    if s + 1 < 4:
                        gate_rows(s + 1)
                    prep(s + 1)

            def recurrence(s):
                for i in range(8):
                    cols_slot((s, "gt", i), XH, XL, "A", m=RB_W, ready=xready(s) if i == 0 else None)
                for i in range(12):
                    if i < 8:
                        cols_slot((s, "in", i), XH, XL, "A", m=RB_W)
                    g = i - 1
                    if 0 <= g < 8:
                        pe.wait_ge(*past(f"rnn_w_in{g % 2}", g))
                        for b in range(2):
                            pe.wait_ge(*past("xc_ready", 2 * g + b))
                            for d in range(2):
                                bank = topen(("gate", g, b, d), "A")
                                for q in range(2):
                                    ins = pe.matmul(bank[0:RB_W, q * S:(q + 1) * S], WG[:, g % 2, 4 * d + 2 * q + b, :],
                                                    XC[:, 2 * g + b, :], start=True, stop=True)
                                ins.then_inc(*inc("tile_done", ("gate", g, b, d)))
                    g = i - 4
                    if g >= 0:
                        pe.wait_ge(*past("yl", g))
                        if g == 0:
                            y_wait(s)
                        rows_slot((s, "out", g), lambda k: YH[:, g % 4, k, :], lambda k: YL[:, g % 4, k, :], 0, g == 0, g == 7, s)

            def mixer(s):
                l = (s - 4) // 3

                for i in range(4):
                    cols_slot((s, "qa", i), XH, XL, "A", ready=xready(s) if i == 0 else None)
                cols_slot((s, "ka", 0), XH, XL, "A")
                v_slot((s, "va", 0), XH, XL)
                cols_slot((s, "bd", 0), XH, XL, "A", step=8)

                def scores(j):
                    t, hh = divmod(j, 2)
                    lo, hi = 64 * hh, 64 * hh + 64
                    if j == 0:
                        pe.wait_ge(*past("free_A", (s, "ka", 0)))
                    bank = topen((s, "sc", j), "D")
                    pe.matmul(bank[:, 0:P], QA[lo:hi, t, 0:P], KA[lo:hi, t // 4, 0:P], start=True, stop=True)
                    pe.matmul(bank[:, P:384], QA[lo:hi, t, P:S], KA[lo:hi, t // 4, :], start=True, stop=True).then_inc(*inc("tile_done", (s, "sc", j)))

                def turn(j):
                    pe.wait_ge(*past("pa_ready", (s, j)))
                    pe.wait_ge(*past(*(("free_A", (s, "pt", j - 2)) if j >= 2 else ("y_free", (s - 1, 0)))))
                    bank = y_bank(j % 2)
                    for k in range(3):
                        ins = pe.transpose(bank[:, k * P:(k + 1) * P], PA[:, j % 3, k * P:(k + 1) * P], IDN[:, :])
                    ins.then_inc(*inc("tile_done", (s, "pt", j)))

                def mix(j):
                    t, hh = divmod(j, 2)
                    kv = 2 * (t // 4) + hh
                    pe.wait_ge(*past("free_A", (s, "pt", j)))
                    if hh == 0:
                        pe.wait_ge(*past(*(("free_D", (s, "oa", t - 2)) if t >= 2 else ("y_free", (s - 1, 1)))))
                        pair["bank"] = y_bank(2 + t % 2)
                    o = pair["bank"][64 * hh:64 * hh + 64]
                    v = VA[:, :, kv * 64:(kv + 1) * 64]
                    pt = PTA[:, j % 2, :]
                    pe.matmul(o[:, 0:P], v[:, 0, :], pt[:, 0:P], start=True, stop=True)
                    pe.matmul(o[:, P:S], v[:, 0, :], pt[:, P:2 * P], start=True, stop=False)
                    ins = pe.matmul(o[:, P:S], v[:, 1, :], pt[:, 2 * P:3 * P], start=False, stop=True)
                    if hh == 1:
                        ins.then_inc(*inc("tile_done", (s, "oa", t)))
                    else:
                        ins.then_inc(*inc("mix_half", (s, j)))

                pe.wait_ge(*past("free_A", (s, "va", 0)))
                for j in range(19):
                    if j < 12:
                        cols_slot((s, "cv", j), XH, XL, "A")
                    elif j < 16:
                        cols_slot((s, "z", j - 12), XH, XL, "A")
                    if j < 16:
                        scores(j)
                    if 2 <= j < 18:
                        turn(j - 2)
                    if j >= 3:
                        mix(j - 3)
                for i in range(4):
                    cols_slot((s, "ba", i), OH, OL, "A", ready=(lambda k: pe.wait_ge(*past("free_D", (s, "oa", k)))) if i == 0 else None)

                pe.wait_ge(*past("g_rows", s))
                bank = topen((s, "gcol"), "D")
                for n, r in ((0, 1), (2, 0)):
                    for c in range(2):
                        ins = pe.transpose(bank[:, 8 * (n + c):8 * (n + c) + 8], ROWS[0:8, r, c * P:(c + 1) * P], IDN[0:8, 0:8])
                ins.then_inc(*inc("tile_done", (s, "gcol")))
                bank = topen((s, "nrm"), "D")
                for i in range(16):
                    pe.wait_ge(*past("sq_ready", (s, i)))
                    ins = pe.matmul(bank[0:16, 0:S], ESEL[:, 15 - i:31 - i], SQ[:, i % 2, :], start=(i == 0), stop=(i == 15))
                    if i < 15:
                        ins.then_inc(*inc("sq_used", (s, i)))
                ins.then_inc(*inc("tile_done", (s, "nrm")))
                pe.wait_ge(*past("nrm_rows", s))
                for hf in range(2):
                    for j in range(5):
                        if j < 4:
                            h = 4 * hf + j
                            bank = topen((s, "bc", h, 0), "D")
                            for q, r in ((0, 1), (1, 0)):
                                ins = pe.matmul(bank[:, q * S:(q + 1) * S], IDN[0:8, h:h + 1].broadcast_to([8, P]), ROWS[0:8, r, :],
                                                start=True, stop=True)
                            ins.then_inc(*inc("tile_done", (s, "bc", h, 0)))
                            bank = topen((s, "bc", h, 1), "D")
                            for q in range(2):
                                ins = pe.matmul(bank[:, q * S:(q + 1) * S], IDN[0:16, 8 * q + h:8 * q + h + 1].broadcast_to([16, P]),
                                                ROWS[0:16, 2, :], start=True, stop=True)
                            ins.then_inc(*inc("tile_done", (s, "bc", h, 1)))
                        if j >= 1:
                            h = 4 * hf + j - 1
                            pe.wait_ge(*past("kb_ready", (s, h)))
                            bank = topen((s, "la", h), "D")
                            for n, rhs in ((0, KBT[:, h % 2, :]), (2, CB[:, h, :])):
                                for c in range(2):
                                    ins = pe.matmul(bank[:, (n + c) * P:(n + c + 1) * P], CB[:, 8 + h, c * P:(c + 1) * P],
                                                    rhs[:, c * P:(c + 1) * P], start=True, stop=True)
                            ins.then_inc(*inc("tile_done", (s, "la", h)))
                    k_ = (s, hf)
                    for c in range(2):
                        pe.wait_ge(*past("u0_ready", (k_, c)))
                        bank = topen((k_, "t0", c), "A")
                        for j in range(4):
                            ins = pe.transpose(bank[:, j * P:(j + 1) * P], UU[:, c, j, :], IDN[:, :])
                        ins.then_inc(*inc("tile_done", (k_, "t0", c)))
                    for i in range(1, 7):
                        for c in range(2):
                            pe.wait_ge(*past("m_ready", (k_, i, c)))
                            pe.wait_ge(*past(*(("free_A", (k_, "t0", c)) if i == 1 else ("free_D", (k_, "dt", i - 1, c)))))
                            bank = topen((k_, "x", i, c), "A")
                            for j in range(4):
                                ins = pe.matmul(bank[:, j * P:(j + 1) * P], MM[:, c, j, :], TT[:, c, j, :], start=True, stop=True)
                            ins.then_inc(*inc("tile_done", (k_, "x", i, c)))
                        if i <= 4:
                            cols_slot((s, "ga" if hf else "gb", i - 1), XH, XL, "A")
                        for c in range(2):
                            pe.wait_ge(*past("free_A", (k_, "x", i, c)))
                            pe.wait_ge(*past(*(("u0_ready", (k_, c)) if i == 1 else ("free_D", (k_, "du", i - 1, c)))))
                            if i < 6:
                                bank = topen((k_, "dt", i, c), "D")
                                for j in range(4):
                                    ins = pe.matmul(bank[:, j * P:(j + 1) * P], UU[:, c, j, :], XX[:, c, j, :], start=True, stop=True)
                                ins.then_inc(*inc("tile_done", (k_, "dt", i, c)))
                            bank = topen((k_, "du", i, c), "D")
                            for j in range(4):
                                ins = pe.matmul(bank[:, j * P:(j + 1) * P], XX[:, c, j, :], UU[:, c, j, :], start=True, stop=True)
                            ins.then_inc(*inc("tile_done", (k_, "du", i, c)))
                    pe.wait_ge(*past("cb_ready", (s, 11)))
                    for c in range(2):
                        bank = topen((k_, "vt", c), "D")
                        for j in range(4):
                            ins = pe.transpose(bank[:, j * P:(j + 1) * P], CB[:, 16 + 4 * hf + j, c * P:(c + 1) * P], IDN[:, :])
                        ins.then_inc(*inc("tile_done", (k_, "vt", c)))
                    bank = topen((k_, "kt"), "D")
                    for j in range(4):
                        ins = pe.transpose(bank[:, j * P:(j + 1) * P], CB[:, 8 + 4 * hf + j, 0:P], IDN[:, :])
                    ins.then_inc(*inc("tile_done", (k_, "kt")))

                    def four(label, consumer, lhs, rhs):
                        bank = topen((k_, label), consumer)
                        for j in range(4):
                            ins = pe.matmul(bank[:, j * P:(j + 1) * P], lhs(j), rhs(j), start=True, stop=True)
                        ins.then_inc(*inc("tile_done", (k_, label)))

                    pe.wait_ge(*past("free_D", (k_, "vt", 0)))
                    pe.wait_ge(*past("free_D", (k_, "du", 6, 0)))
                    four("vn0", "A", lambda j: UU[:, 0, j, :], lambda j: XX[:, 0, j, :])
                    pe.wait_ge(*past("free_D", (k_, "kt")))
                    pe.wait_ge(*past("free_A", (k_, "vn0")))
                    four("s1", "A", lambda j: KTL[:, j, :], lambda j: TT[:, 0, j, :])
                    pe.wait_ge(*past("free_A", (k_, "s1")))
                    four("ks", "D", lambda j: KBG[:, j, :], lambda j: MM[:, 0, j, :])
                    pe.wait_ge(*past("free_D", (k_, "ks")))
                    pe.wait_ge(*past("free_D", (k_, "du", 6, 1)))
                    four("vn1", "A", lambda j: UU[:, 1, j, :], lambda j: XX[:, 1, j, :])
                    pe.wait_ge(*past("free_A", (k_, "vn1")))
                    for m in range(2):
                        bank = topen((k_, "od", m), "A")
                        for jj in range(2):
                            j = 2 * m + jj
                            o = bank[:, jj * S:(jj + 1) * S]
                            pe.matmul(o[:, 0:P], TT[:, 0, j, :], EA[:, 0, j, :], start=True, stop=True)
                            pe.matmul(o[:, P:S], MM[:, 0, j, :], QD[:, j, :], start=True, stop=False)
                            ins = pe.matmul(o[:, P:S], TT[:, 1, j, :], EA[:, 1, j, :], start=False, stop=True)
                        ins.then_inc(*inc("tile_done", (k_, "od", m)))
                bank = topen((s, "onrm"), "D")
                for i in range(8):
                    pe.wait_ge(*past("osq_ready", (s, i)))
                    ins = pe.matmul(bank[0:8, 0:S], ESEL[:, 15 - i:23 - i], SQ[:, i % 2, :], start=(i == 0), stop=(i == 7))
                    if i < 7:
                        ins.then_inc(*inc("osq_used", (s, i)))
                ins.then_inc(*inc("tile_done", (s, "onrm")))
                pe.wait_ge(*past("orow_ready", s))
                for m in range(4):
                    bank = topen((s, "obc", m), "D")
                    for jj in range(2):
                        ins = pe.matmul(bank[:, jj * S:(jj + 1) * S], IDN[0:8, 2 * m + jj:2 * m + jj + 1].broadcast_to([8, P]),
                                        ROWS[0:8, 5, :], start=True, stop=True)
                    ins.then_inc(*inc("tile_done", (s, "obc", m)))
                for i in range(4):
                    cols_slot((s, "bb", i), OH, OL, "D", ready=(lambda k: pe.wait_ge(*past("olb_ready", (s, k // 2)))) if i == 0 else None)
                for i in range(4):
                    pe.wait_ge(*past("ml_ready", (s, i)))
                    if i == 0:
                        y_wait(s)
                    rows_slot((s, "out", i), lambda k: XH[:, k, :], lambda k: XL[:, k, :], 2 * i, i == 0, i == 3, s)

            between(0)
            for s in range(1, n_sub):
                if s in (1, 3):
                    mlp(s)
                elif s == 2:
                    recurrence(s)
                elif is_mix(s):
                    mixer(s)
                else:
                    ffn(s)
                between(s)

        @block.scalar
        def _(act):
            split = [0]

            def hi_upto(n):
                while split[0] <= min(n, len(slots) - 1):
                    m = split[0]
                    split[0] += 1
                    act.wait_ge(*past(f"landed{m % NRAW}", m))
                    if m >= NSPL:
                        act.wait_ge(*past(*slot_end[m - NSPL]))
                    act.activation(slot_view(WHI, m, NSPL), slot_view(RAW, m, NRAW), ACT.Copy).then_inc(*inc("hi_ready", m))

            def evac(label, dst, func=ACT.Copy, src=None, **kw):
                act.activation(dst, src, func, **kw).then_inc(*inc("free_A", label))

            def tile(label):
                act.wait_ge(*past("tile_done", label))
                return TB[:, known.get(("tile", label), 0) % NTB, :]

            def pair_of(bank, p=P):
                return bank[0:p, :].rearrange("p (a b) -> p a b", a=2)

            def step(label):
                hi_upto(number[label] + NSPL - 1)

            def in_dma(dst, src, name, key=None):
                act.dma_start(dst, src).then_inc(*inc(name, key, 16))

            def bcast_rows(vec, n):
                return bass.AP(vec.tensor, vec.offset, [[0, P], [1, n]])

            in_dma(IDN[:, :], C["ident"], "ident_in")
            for src, r0, blk in sorted(prm, key=lambda x: x[2]):
                in_dma(PST[r0:r0 + src.shape[0], blk, 0:src.shape[1]], src, f"param_in{blk}")
            in_dma(NSC[:, :], C["norm_scale"], "const_in")
            in_dma(WIN[:, :], C["window"], "const_in")
            in_dma(COS[:, :], C["rope_cos"], "const_in")
            in_dma(SIN[:, :], C["rope_sin"], "const_in")
            in_dma(ROT[:, :], C["rope_rot"], "const_in")
            in_dma(SNK[:, :], bcast_rows(I["attn_sinks"], 8), "const_in")
            for l in range(2):
                in_dma(SNK2[:, l, :], bcast_rows(I["sinks_2"][l], 16), "const_in")
                in_dma(AL2[:, l:l + 1], I["a_log_2"][l].rearrange("(a b) -> a b", b=1), "const_in")
                in_dma(AL2[:, 2 + l:3 + l], I["dt_bias_2"][l].rearrange("(a b) -> a b", b=1), "const_in")
            in_dma(HOT[:, :], C["bucket_hot"], "rel_in")
            in_dma(RBI[0:32, :], I["rel_bias_2"], "rel_in")
            act.wait_ge(*past("free_D", ("param", 0)))
            act.activation(CC[:, :], CC[:, :], ACT.Silu).then_inc(*inc("c_ready"))
            act.wait_ge(*past("const_in"))
            act.activation(AL2[:, 4:6], AL2[:, 0:2], ACT.Exp).then_inc(*inc("a_exp"))
            hi_upto(NSPL - 1)
            for h in range(16):
                bank = tile(("ext", h))
                if h >= 2:
                    act.wait_ge(*past(f"bias_out{h % 2}", h - 2))
                evac(("ext", h), EXS[:, h % 2, :], src=bank[:, 0:EXT])
                act.wait_ge(*past("free_A", ("ext", h)))
                act.dma_start(BIAS[h], EXS[:, h % 2, :]).then_inc(*inc(f"bias_out{h % 2}", h, 16))

            def gate_rows(s):
                for h in range(2):
                    bank = tile(("gate", s, h))
                    if s > 0 and h == 0:
                        act.wait_ge(*past("y_free", (s - 1, 1)))
                    evac(("gate", s, h), GATE[:, h * 512:(h + 1) * 512], src=bank)

            def prep(s):
                for e in range(4):
                    act.wait_ge(*past("free_D", ("xt", s, e)))
                    act.activation(XH[:, 2 * e:2 * e + 2, :], XTF[:, 2 * e:2 * e + 2, :], ACT.Copy).then_inc(*inc("xh_ready", (s, e)))

            gate_rows(0)
            prep(0)
            for i in range(6):
                step((0, "in", i))
                dst = QT[:, 2 * i:2 * i + 2, :] if i < 4 else (KT if i == 4 else VR)[:, :, :]
                evac((0, "in", i), dst, src=pair_of(tile((0, "in", i))))
            for h in range(NH1 + 2):
                if h < NH1:
                    act.wait_ge(*past("neg_max", h))
                    for b in range(2):
                        act.activation(PR[:, h, b, :], PR[:, h, b, :], ACT.Exp, bias=AT1[:, 1, 2 * h + b:2 * h + b + 1],
                                           accum_out=AT1[:, 2, 2 * h + b:2 * h + b + 1]).then_inc(*inc("p_exp_part", (h, b)))
                    act.activation(AT1[:, 3, 2 * h:2 * h + 2], AT1[:, 1, 2 * h:2 * h + 2], ACT.Exp,
                                       bias=SNK[:, h:h + 1]).then_inc(*inc("p_exp", h))
                if 1 <= h <= NH1:
                    bank = tile(("pt", h - 1))
                    evac(("pt", h - 1), PTB[:, (h - 1) % 2, :, :], src=bank.rearrange("p (a b) -> p a b", a=4))
                if h >= 2 and h % 2 == 1:
                    i = (h - 2) // 2
                    bank = tile(("o", i))
                    act.activation(OH[:, 2 * i:2 * i + 2, :], pair_of(bank), ACT.Copy).then_inc(*inc("oh_ready", (0, i)))
            for i in range(4):
                step((0, "out", i))

            def hi_hidden(s, i, func, src):
                if i >= 2:
                    act.wait_ge(*past("rows_done", (s, "w2", i - 2)))
                act.activation(HH[:, i % 2, :], src[:, i % 2, :], func).then_inc(*inc("hh_ready", (s, i)))

            def mlp(s):
                n = FF1 // 256
                for i in range(n + 1):
                    if i < n:
                        step((s, "w1", i))
                        bank = tile((s, "w1", i))
                        if i >= 2:
                            act.wait_ge(*past("hid_ready", (s, i - 2)))
                        evac((s, "w1", i), RB[:, i % 2, :], ACT.Relu, bank)
                        act.wait_ge(*past("free_A", (s, "w1", i)))
                        hi_hidden(s, i, ACT.Square, RB)
                    if i > 0:
                        step((s, "w2", i - 1))

            def ffn(s):
                n = FF2 // 256
                for i in range(n + 1):
                    if i < n:
                        step((s, "g", i))
                        bank = tile((s, "g", i))
                        if i >= 2:
                            act.wait_ge(*past("hid_ready", (s, i - 2)))
                        evac((s, "g", i), RB[:, i % 2, :], ACT.Silu, bank)
                        step((s, "u", i))
                        act.wait_ge(*past("free_D", (s, "u", i)))
                        hi_hidden(s, i, ACT.Copy, VB)
                    if i > 0:
                        step((s, "w2", i - 1))

            def norm(s):
                for t in range(NT):
                    act.wait_ge(*past("ln_recip", (s, t)))
                    act.activation(RV[:, t, 1:2], RV[:, t, 0:1], ACT.Sqrt).then_inc(*inc("ln_rstd", (s, t)))
                if s + 1 < n_sub:
                    if s + 1 < 4:
                        gate_rows(s + 1)
                    prep(s + 1)

            def recurrence(s):
                act.wait_ge(*past("lam_abs"))
                act.activation(RCOL[:, 4, :], RCOL[:, 3, :], ACT.Exp, scale=-1.0).then_inc(*inc("lam_exp"))
                for i in range(8):
                    step((s, "gt", i))
                    evac((s, "gt", i), GG[:, 2 * i:2 * i + 2, :], ACT.Gelu_apprx_tanh, pair_of(tile((s, "gt", i)), RB_W))
                for i in range(12):
                    if i < 8:
                        step((s, "in", i))
                        bank = tile((s, "in", i))
                        if i == 0:
                            act.wait_ge(*past("xp_zero"))
                        if i >= 2:
                            act.wait_ge(*past("xc_ready", 2 * i - 3))
                        evac((s, "in", i), XP[:, i % 2, :, 2:2 + S], src=pair_of(bank, RB_W))
                    g = i - 1
                    if 0 <= g < 8:
                        if g == 0:
                            act.wait_ge(*past("decay_cols"))
                        if g >= 2:
                            act.wait_ge(*past("yl", g - 2))
                        for b in range(2):
                            for d in range(2):
                                bank = tile(("gate", g, b, d))
                                ch = 16 * d + 2 * g + b
                                act.activation(RR[:, g % 2, d, b, :], bank[0:RB_W, 0:S], ACT.Tanh, scale=0.5,
                                                   bias=RC2[:, ch:ch + 1]).then_inc(*inc("rnn_r", (g, b, d)))
                                evac(("gate", g, b, d), RI[:, g % 2, d, b, :], ACT.Tanh, bank[0:RB_W, S:2 * S], scale=0.5,
                                     bias=RC2[:, 32 + ch:33 + ch])
                    if 0 <= g - 1 < 8:
                        if g - 1 >= 4:
                            act.wait_ge(*past("rows_done", (s, "out", g - 5)))
                        act.wait_ge(*past("rnn_v", g - 1))
                        act.activation(YH[:, (g - 1) % 4, :, :], RR[:, (g - 1) % 2, 0, :, :], ACT.Copy).then_inc(*inc("yh", g - 1))
                    if i >= 4:
                        step((s, "out", i - 4))
                    if 0 <= g < 8:
                        for d in range(2):
                            for b in range(2):
                                ch = 16 * d + 2 * g + b
                                a_, r_ = RA[:, g % 2, d, b, :], RR[:, g % 2, d, b, :]
                                act.wait_ge(*past("rnn_r", (g, b, d)))
                                act.activation(a_, r_, ACT.Exp, scale=RCOL[:, 0, ch:ch + 1], bias=RCOL[:, 0, ch:ch + 1]).then_inc(*inc("rnn_a", (g, d, b)))
                                act.activation(r_, r_, ACT.Tanh, scale=RCOL[:, 1, ch:ch + 1], bias=RCOL[:, 1, ch:ch + 1]).then_inc(*inc("rnn_th", (g, d, b)))
                        act.wait_ge(*past("rnn_one", (g, 1)))
                        act.activation(RR[:, g % 2, :, :, :], RR[:, g % 2, :, :, :], ACT.Sqrt).then_inc(*inc("rnn_mult", g))

            def mixer(s):
                l = (s - 4) // 3
                for i in range(4):
                    step((s, "qa", i))
                    evac((s, "qa", i), QA[:, 2 * i:2 * i + 2, :], src=pair_of(tile((s, "qa", i))))
                for name, dst in (("ka", KA), ("va", VA)):
                    step((s, name, 0))
                    evac((s, name, 0), dst[:, :, :], src=pair_of(tile((s, name, 0))))
                step((s, "bd", 0))
                bank = tile((s, "bd", 0))
                act.activation(ROWS[0:8, 0, :], bank[0:8, 0:S], ACT.Sigmoid).then_inc(*inc("beta_rows", s))
                evac((s, "bd", 0), ROWS[0:8, 3, :], ACT.Identity, bank[0:8, S:2 * S], bias=AL2[:, 2 + l:3 + l])
                act.wait_ge(*past("cin_zero", s))
                act.wait_ge(*past("xs_ready", (s - 1, 1)))
                for j in range(19):
                    if j < 12:
                        step((s, "cv", j))
                        bank = tile((s, "cv", j))
                        if j >= 2:
                            act.wait_ge(*past("conv_done", (s, j - 2)))
                        evac((s, "cv", j), CIN[:, j % 2, :, 3:3 + S], src=pair_of(bank))
                        act.wait_ge(*past("free_A", (s, "cv", j)))
                        for jj in range(2):
                            ct = 2 * j + jj
                            act.activation(CB[:, ct, :], CIN[:, j % 2, jj, 0:S], ACT.Identity, scale=CW2[:, l, ct:ct + 1]).then_inc(*inc("tap0", (s, j)))
                    elif j < 16:
                        step((s, "z", j - 12))
                        bank = tile((s, "z", j - 12))
                        act.activation(ZT[:, 2 * (j - 12):2 * (j - 12) + 2, :], pair_of(bank), ACT.Copy, scale=0.5).then_inc(*inc("z_half", (s, j)))
                        act.wait_ge(*past("cb_ready", (s, j - 2)))
                        act.activation(TH[:, j % 2, :, :], pair_of(bank), ACT.Tanh, scale=0.5).then_inc(*inc("free_A", (s, "z", j - 12)))
                    if j == 0:
                        act.wait_ge(*past("dt_abs", s))
                        act.activation(ROWS[0:8, 5, :], ROWS[0:8, 4, :], ACT.Exp, scale=-1.0).then_inc(*inc("dt_exp", s))
                    if 1 <= j <= 12:
                        u = j - 1
                        act.wait_ge(*past("conv_done", (s, u)))
                        if u >= 2:
                            act.wait_ge(*past("cb_ready", (s, u - 2)))
                        act.activation(TH[:, u % 2, :, :], CB[:, 2 * u:2 * u + 2, :], ACT.Tanh).then_inc(*inc("tanh_ready", (s, u)))
                    if 1 <= j <= 16:
                        t, hh = divmod(j - 1, 2)
                        head = (2 * (t // 4) + hh) * 4 + t % 4
                        r = (j - 1) % 3
                        act.wait_ge(*past("neg_max_a", (s, j - 1)))
                        for b, (lo, hi) in enumerate(((0, P), (P, 384))):
                            act.activation(PA[:, r, lo:hi], PA[:, r, lo:hi], ACT.Exp, bias=A2S[:, r, b:b + 1],
                                               accum_out=A2S[:, r, 2 + b:3 + b]).then_inc(*inc("pa_exp_part", (s, j - 1, b)))
                        act.activation(A2S[:, r, 4:6], A2S[:, r, 0:2], ACT.Exp, bias=SNK2[:, l, head:head + 1]).then_inc(*inc("pa_exp", (s, j - 1)))
                    if 2 <= j < 18:
                        act.wait_ge(*past("tile_done", (s, "pt", j - 2)))
                        evac((s, "pt", j - 2), PTA[:, j % 2, :], src=y_bank(j % 2)[:, 0:384])
                    if j >= 4 and j % 2 == 0:
                        t = (j - 4) // 2
                        act.wait_ge(*past("tile_done", (s, "oa", t)))
                        act.activation(OH[:, t, :], y_bank(2 + t % 2)[:, 0:S], ACT.Copy).then_inc(*inc("oh_ready", (s, t)))
                for i in range(4):
                    step((s, "ba", i))
                    evac((s, "ba", i), M1[:, 2 * i:2 * i + 2, :], src=pair_of(tile((s, "ba", i))))
                for i in range(16):
                    if i >= 2:
                        act.wait_ge(*past("sq_used", (s, i - 2)))
                    act.wait_ge(*past("cb_ready", (s, i // 2)))
                    act.activation(SQ[:, i % 2, :], CB[:, i, :], ACT.Square).then_inc(*inc("sq_ready", (s, i)))
                act.wait_ge(*past("nrm_recip", s))
                act.activation(ROWS[0:16, 2, :], ROWS[0:16, 4, :], ACT.Sqrt, scale=NSC[:, 0:1]).then_inc(*inc("nrm_rows", s))
                for hf in range(2):
                    k_ = (s, hf)
                    for j in range(4):
                        h = 4 * hf + j
                        bank = tile((s, "bc", h, 0))
                        if j >= 2:
                            act.wait_ge(*past("kb_ready", (s, h - 2)))
                        act.wait_ge(*past("e_raw", (s, h)))
                        act.activation(EG[:, h % 2, :], bank[:, 0:S], ACT.Exp).then_inc(*inc("eg_ready", (s, h)))
                        act.activation(EA[:, :, j, :], EA[:, :, j, :], ACT.Exp).then_inc(*inc("e_ready", (s, h)))
                        act.activation(GLT[:, 1, h:h + 1], GCOL[:, 0, h:h + 1], ACT.Exp, scale=-1.0,
                                           bias=GLT[:, 0, h:h + 1]).then_inc(*inc("tail_ready", (s, h)))

                    def four(label, dst):
                        bank = tile(label)
                        evac(label, dst, src=bank.rearrange("p (a b) -> p a b", a=4))

                    for c in range(2):
                        four((k_, "t0", c), TT[:, c, :, :])
                    for i in range(1, 7):
                        for c in range(2):
                            four((k_, "x", i, c), XX[:, c, :, :])
                        if hf == 1 and i <= 4:
                            step((s, "ga", i - 1))
                            bank = tile((s, "ga", i - 1))
                            if i > 1:
                                act.wait_ge(*past("gate_a_used", (s, i - 2)))
                            evac((s, "ga", i - 1), GT[:, :, :], ACT.Sigmoid, pair_of(bank))
                        if hf == 0 and i <= 4:
                            step((s, "gb", i - 1))
                            evac((s, "gb", i - 1), GBT[:, 2 * i - 2:2 * i, :], ACT.Sigmoid, pair_of(tile((s, "gb", i - 1))))
                    four((k_, "vn0"), TT[:, 0, :, :])
                    four((k_, "s1"), MM[:, 0, :, :])
                    four((k_, "vn1"), TT[:, 1, :, :])
                    for m in range(2):
                        q0 = 4 * hf + 2 * m
                        evac((k_, "od", m), CB[:, q0:q0 + 2, :], src=pair_of(tile((k_, "od", m))))
                for i in range(8):
                    if i >= 2:
                        act.wait_ge(*past("osq_used", (s, i - 2)))
                    act.wait_ge(*past("free_A", ((s, i // 4), "od", i % 4 // 2)))
                    act.activation(SQ[:, i % 2, :], CB[:, i, :], ACT.Square).then_inc(*inc("osq_ready", (s, i)))
                act.wait_ge(*past("onrm_recip", s))
                act.activation(ROWS[0:8, 5, :], ROWS[0:8, 3, :], ACT.Sqrt).then_inc(*inc("orow_ready", s))
                for m in range(4):
                    act.wait_ge(*past("ov_ready", (s, m)))
                    act.activation(OH[:, 2 * m:2 * m + 2, :], CB[:, 2 * m:2 * m + 2, :], ACT.Copy).then_inc(*inc("ohb_ready", (s, m)))
                for i in range(4):
                    step((s, "bb", i))
                    act.wait_ge(*past("mv_ready", (s, i)))
                    act.activation(XH[:, 2 * i:2 * i + 2, :], CB[:, 2 * i:2 * i + 2, :], ACT.Copy).then_inc(*inc("mh_ready", (s, i)))
                for i in range(4):
                    step((s, "out", i))

            norm(0)
            for s in range(1, n_sub):
                if s in (1, 3):
                    mlp(s)
                elif s == 2:
                    recurrence(s)
                elif is_mix(s):
                    mixer(s)
                else:
                    ffn(s)
                norm(s)

        @block.vector
        def _(dve):
            split = [0]

            def lo_upto(n):
                while split[0] <= min(n, len(slots) - 1):
                    m = split[0]
                    split[0] += 1
                    dve.wait_ge(*past("hi_ready", m))
                    dve.tensor_tensor(slot_view(WLO, m, NSPL), slot_view(RAW, m, NRAW),
                                          slot_view(WHI, m, NSPL).bitcast(F32), ALU.subtract).then_inc(*inc("lo_ready", m))

            def step(label):
                lo_upto(number[label] + NSPL - 1)

            def tile(label):
                dve.wait_ge(*past("tile_done", label))
                return TB[:, known.get(("tile", label), 0) % NTB, :]

            def pair_of(bank, p=P):
                return bank[0:p, :].rearrange("p (a b) -> p a b", a=2)

            def chain(ins):
                link(dve, ins, "dve_chain")

            def params(n):
                rows, width, dsts = blocks[n]
                bank = tile(("param", n))
                at = 0
                for q, dst in enumerate(dsts):
                    w = dst.shape[1]
                    ins = dve.tensor_copy(dst, bank[0:width, at:at + w])
                    at += w
                    if q < len(dsts) - 1:
                        chain(ins)
                ins.then_inc(*inc("free_D", ("param", n)))
                dve.wait_ge(*past("free_D", ("param", n)))
                if n == 7:
                    chain(dve.tensor_scalar(RC2[:, 0:64], RC2[:, 0:64], 0.5, None, ALU.mult))
                if n in (3, 4):
                    chain(dve.tensor_scalar(dsts[0], dsts[0], 0.5, None, ALU.mult))

            chunk = [0]

            def ada_upto(q):
                while chunk[0] <= min(q, n_ada - 1):
                    m = chunk[0]
                    chunk[0] += 1
                    t, kc = divmod(m, KC)
                    dve.wait_ge(*past(f"ada_in{m % NADR}" if m < 24 else f"ada_next{m % NADR}", m))
                    if kc == 0:
                        if t >= 3:
                            dve.wait_ge(*past("tile_done", ("ada", t - 3)))
                        ins = dve.tensor_scalar(ACC[:, t % 3, :], ADR[:, m % NADR, :], CC[:, kc:kc + 1], None, ALU.mult)
                    else:
                        dve.wait_ge(*past("ada_used", m - 1))
                        ins = dve.scalar_tensor_tensor(ACC[:, t % 3, :], ADR[:, m % NADR, :], CC[:, kc:kc + 1], ACC[:, t % 3, :],
                                                       ALU.mult, ALU.add)
                    ins.then_inc(*inc("ada_used", m))

            params(0)
            dve.wait_ge(*past("c_ready"))
            ada_upto(3)
            for n in range(1, len(blocks)):
                params(n)
            ada_upto(12)
            lo_upto(0)
            ada_upto(17)
            lo_upto(NSPL - 1)
            ada_upto(23)

            def modulation(t):
                if 8 * t >= n_ada:
                    return
                s, third = divmod(t, 3)
                bank = tile(("ada", t))
                m = MOD[:, s, 8 * third:8 * third + 8]
                dve.tensor_tensor(m, bank[:, 0:8], ADB[:, 8 * t:8 * t + 8], ALU.add).then_inc(*inc("free_D", ("ada", t)))
                dve.wait_ge(*past("free_D", ("ada", t)))
                if third < 2:
                    return
                chain(dve.tensor_scalar(MOD[:, s, 8:24], MOD[:, s, 8:24], 1.0, None, ALU.add))
                if s == 0:
                    chain(dve.tensor_copy(GP[:, s, :], MOD[:, s, 8:16]))
                    dve.tensor_copy(BP[:, s, :], MOD[:, s, 0:8]).then_inc(*inc("mod_ready", s))
                else:
                    g, b = LN[s - 1][2], LN[s - 1][3]
                    chain(dve.tensor_tensor(GP[:, s, :], MOD[:, s, 8:16], g, ALU.mult))
                    chain(dve.tensor_tensor(BP[:, s, :], MOD[:, s, 8:16], b, ALU.mult))
                    dve.tensor_tensor(BP[:, s, :], BP[:, s, :], MOD[:, s, 0:8], ALU.add).then_inc(*inc("mod_ready", s))
                dve.wait_ge(*past("mod_ready", s))

            def prep(s):
                def lo(e):
                    dve.wait_ge(*past("xh_ready", (s, e)))
                    dve.tensor_tensor(XL[:, 2 * e:2 * e + 2, :], XTF[:, 2 * e:2 * e + 2, :],
                                          XH[:, 2 * e:2 * e + 2, :].bitcast(F32), ALU.subtract).then_inc(*inc("xl_ready", (s, e)))

                gp, bp = (GP[:, s, :], BP[:, s, :]) if s < 4 else (LN[s - 1][2], LN[s - 1][3])
                for e in range(4):
                    bank = tile(("xt", s, e))
                    for kk in range(2):
                        k = 2 * e + kk
                        ins = dve.tensor_scalar(XTF[:, k, :], bank[:, kk * S:(kk + 1) * S], gp[:, k:k + 1], bp[:, k:k + 1],
                                                ALU.mult, ALU.add)
                        if kk == 0:
                            ins.then_inc(*inc("xtf_half", (s, e)))
                    ins.then_inc(*inc("free_D", ("xt", s, e)))
                    if e:
                        lo(e - 1)
                lo(3)

            for t in range(3):
                modulation(t)
            prep(0)
            for i in range(6):
                step((0, "in", i))
                ada_upto(25 + 2 * i)
            modulation(3)
            for i in range(5):
                bank = tile(("rot", i))
                src = (QT[0:32, 2 * i:2 * i + 2, :] if i < 4 else KT[0:32, :, :]).rearrange("p a b -> p (a b)")
                dve.tensor_tensor(RTMP[:, i % 2, :], bank[0:32, :], SIN[:, :], ALU.mult).then_inc(*inc("free_D", ("rot", i)))
                chain(dve.tensor_tensor(src, src, COS[:, :], ALU.mult))
                dve.wait_ge(*past("free_D", ("rot", i)))
                dve.tensor_tensor(src, src, RTMP[:, i % 2, :], ALU.add).then_inc(*inc("rope_ready", i))
            for n in range(2):
                dve.wait_ge(*past(f"bias_out{n}", 14 + n))

            def norm1(h):
                dve.wait_ge(*past("p_exp", h))
                w = slice(2 * h, 2 * h + 2)
                chain(dve.tensor_tensor(AT1[:, 4, w], AT1[:, 2, w], AT1[:, 3, w], ALU.add))
                chain(dve.reciprocal(AT1[:, 5, w], AT1[:, 4, w]))
                for b in range(2):
                    dve.tensor_scalar(PR[:, h, b, :], PR[:, h, b, :], AT1[:, 5, 2 * h + b:2 * h + b + 1], None, ALU.mult).then_inc(*inc("probs_ready", h))

            for h in range(NH1 + 2):
                if h < NH1:
                    bank = tile(("sc", h))
                    w = slice(2 * h, 2 * h + 2)
                    dve.scalar_tensor_tensor(PR[:, h, :, :].rearrange("p a b -> p (a b)"), bank, HD1 ** -0.5, WIN[:, :],
                                                 ALU.mult, ALU.add).then_inc(*inc("free_D", ("sc", h)))
                    dve.wait_ge(*past("free_D", ("sc", h)))
                    chain(dve.tensor_reduce(AT1[:, 0, w], PR[:, h, :, :], AX.X, ALU.max))
                    dve.tensor_scalar(AT1[:, 1, w], AT1[:, 0, w], SNK[:, h:h + 1], -1.0, ALU.max, ALU.mult).then_inc(*inc("neg_max", h))
                if 1 <= h <= NH1:
                    norm1(h - 1)
                if h >= 2 and h % 2 == 1:
                    i = (h - 2) // 2
                    bank = tile(("o", i))
                    dve.wait_ge(*past("oh_ready", (0, i)))
                    dve.tensor_tensor(OL[:, 2 * i:2 * i + 2, :], pair_of(bank), OH[:, 2 * i:2 * i + 2, :].bitcast(F32),
                                          ALU.subtract).then_inc(*inc("free_D", ("o", i)))
                if h in (4, 6):
                    modulation(2 + h // 2)
                ada_upto(38 + 3 * h)
            for i in range(4):
                step((0, "out", i))
                if i % 2 == 1:
                    modulation(6 + i // 2)
                ada_upto(66 + i)

            def norm(s):
                for t in range(NT):
                    if t == 0:
                        dve.wait_ge(*past(*y_end[s]))
                    dve.wait_ge(*past("xs_ready", (s - 1, t)))
                    if s < 4:
                        if t == 0:
                            dve.wait_ge(*past("free_A", ("gate", s, 1)))
                        dve.tensor_tensor(XN[:, t, :], Y[:, t, :], GATE[:, :], ALU.mult).then_inc(*inc("y_free", (s, t)))
                        dve.wait_ge(*past("y_free", (s, t)))
                        chain(dve.tensor_tensor(XN[:, t, :], XN[:, t, :], XS[:, t, :], ALU.add))
                    else:
                        dve.scalar_tensor_tensor(XN[:, t, :], Y[:, t, :], 1.0 if is_mix(s) else 0.5, XS[:, t, :],
                                                     ALU.mult, ALU.add).then_inc(*inc("y_free", (s, t)))
                        dve.wait_ge(*past("y_free", (s, t)))
                    for h in range(2):
                        ins = dve.bn_stats(ST[:, t, h, :], XN[:, t, h * 512:(h + 1) * 512])
                    chain(ins)
                    chain(dve.bn_aggr(MV[:, t, :], ST[:, t, :, :].rearrange("p a b -> p (a b)")))
                    chain(dve.tensor_scalar(RV[:, t, 0:1], MV[:, t, 1:2], LN_EPS, None, ALU.add))
                    dve.reciprocal(RV[:, t, 0:1], RV[:, t, 0:1]).then_inc(*inc("ln_recip", (s, t)))
                for t in range(NT):
                    dve.wait_ge(*past("ln_rstd", (s, t)))
                    dve.tensor_scalar(XN[:, t, :], XN[:, t, :], MV[:, t, 0:1], RV[:, t, 1:2], ALU.subtract, ALU.mult).then_inc(*inc("xn_ready", (s, t)))
                if s + 1 < n_sub:
                    prep(s + 1)
                else:
                    dve.wait_ge(*past("gb_in", s))
                    for t in range(NT):
                        dve.wait_ge(*past("xn_ready", (s, t)))
                        chain(dve.tensor_tensor(XN[:, t, :], XN[:, t, :], GB[:, 0, :], ALU.mult))
                        dve.tensor_tensor(XN[:, t, :], XN[:, t, :], GB[:, 1, :], ALU.add).then_inc(*inc("out_rows", t))

            def lo_hidden(s, i):
                dve.wait_ge(*past("hh_ready", (s, i)))
                dve.tensor_tensor(HL[:, i % 2, :], VB[:, i % 2, :], HH[:, i % 2, :].bitcast(F32), ALU.subtract).then_inc(*inc("hid_ready", (s, i)))

            def mlp(s):
                n = FF1 // 256
                for i in range(n + 1):
                    if i < n:
                        step((s, "w1", i))
                        dve.wait_ge(*past("free_A", (s, "w1", i)))
                        dve.tensor_tensor(VB[:, i % 2, :], RB[:, i % 2, :], RB[:, i % 2, :], ALU.mult).then_inc(*inc("hid_v", (s, i)))
                        dve.wait_ge(*past("hid_v", (s, i)))
                        lo_hidden(s, i)
                    if s == 1 and i % 4 == 3:
                        modulation(8 + i // 4)
                    if s == 1:
                        ada_upto(71 + 2 * i)
                    if i > 0:
                        step((s, "w2", i - 1))

            def ffn(s):
                n = FF2 // 256
                for i in range(n + 1):
                    if i < n:
                        step((s, "g", i))
                        step((s, "u", i))
                        bank = tile((s, "u", i))
                        dve.wait_ge(*past("free_A", (s, "g", i)))
                        dve.tensor_tensor(VB[:, i % 2, :], RB[:, i % 2, :], bank, ALU.mult).then_inc(*inc("free_D", (s, "u", i)))
                        lo_hidden(s, i)
                    if i > 0:
                        step((s, "w2", i - 1))

            def softplus(x, ax, e, t0, t1, exp_wait):
                exp_wait()
                chain(dve.tensor_scalar(t0, e, 2.0, None, ALU.add))
                chain(dve.reciprocal(t0, t0))
                chain(dve.tensor_tensor(e, e, t0, ALU.mult))
                chain(dve.tensor_tensor(t1, e, e, ALU.mult))
                chain(dve.tensor_scalar(t0, t1, 1.0 / 17, None, ALU.mult))
                for d in (15, 13, 11, 9, 7, 5, 3):
                    chain(dve.scalar_tensor_tensor(t0, t0, 1.0 / d, t1, ALU.add, ALU.mult))
                chain(dve.scalar_tensor_tensor(t0, t0, 1.0, e, ALU.add, ALU.mult))
                chain(dve.tensor_scalar(x, x, 0.0, 0.5, ALU.max, ALU.mult))
                chain(dve.tensor_tensor(t0, t0, x, ALU.add))
                chain(dve.tensor_scalar(t0, t0, 2.0, None, ALU.mult))

            def recurrence(s):
                x, ax, e, t0, t1 = (RCOL[:, q, :] for q in range(2, 7))
                chain(dve.tensor_scalar(x, RC2[:, 64:96], -1.0, None, ALU.mult))
                dve.tensor_tensor(ax, x, RC2[:, 64:96], ALU.max).then_inc(*inc("lam_abs"))
                softplus(x, ax, e, t0, t1, lambda: dve.wait_ge(*past("lam_exp")))
                chain(dve.tensor_scalar(RCOL[:, 0, :], t0, -4.0, None, ALU.mult))
                dve.tensor_scalar(RCOL[:, 1, :], t0, 4.0, None, ALU.mult).then_inc(*inc("decay_cols"))
                for i in range(8):
                    step((s, "gt", i))
                for i in range(12):
                    if i < 8:
                        step((s, "in", i))
                        dve.wait_ge(*past("free_A", (s, "in", i)))
                        for jj in range(2):
                            ct = 2 * i + jj
                            xin = XP[:, i % 2, jj, :]
                            chain(dve.tensor_scalar(XC[:, ct, :], xin[:, 0:S], RC1[:, ct:ct + 1], RC1[:, 64 + ct:65 + ct],
                                                    ALU.mult, ALU.add))
                            for j in range(1, 4):
                                ins = dve.scalar_tensor_tensor(XC[:, ct, :], xin[:, j:j + S], RC1[:, 16 * j + ct:16 * j + ct + 1],
                                                               XC[:, ct, :], ALU.mult, ALU.add)
                                if j < 3:
                                    chain(ins)
                            ins.then_inc(*inc("xc_ready", ct))
                    g = i - 1
                    if i >= 4:
                        step((s, "out", i - 4))
                    if 0 <= g - 1 < 8:
                        dve.wait_ge(*past("yh", g - 1))
                        dve.tensor_tensor(YL[:, (g - 1) % 4, :, :], RR[:, (g - 1) % 2, 0, :, :],
                                              YH[:, (g - 1) % 4, :, :].bitcast(F32), ALU.subtract).then_inc(*inc("yl", g - 1))
                    if 0 <= g < 8:
                        r = RR[:, g % 2]
                        for d in range(2):
                            dve.wait_ge(*past("rnn_a", (g, d, 1)))
                            chain(dve.tensor_tensor(RTM[:, d, :, :], RA[:, g % 2, d, :, :], RA[:, g % 2, d, :, :], ALU.mult))
                            dve.wait_ge(*past("rnn_th", (g, d, 1)))
                            dve.scalar_tensor_tensor(r[:, d, :, :], RTM[:, d, :, :], 1.0, r[:, d, :, :], ALU.add, ALU.mult).then_inc(*inc("rnn_one", (g, d)))
                        dve.wait_ge(*past("rnn_mult", g))
                        dve.wait_ge(*past("rnn_ix", g))
                        chain(dve.tensor_tensor(RI[:, g % 2, :, :, :], RI[:, g % 2, :, :, :], r, ALU.mult))
                        for d in range(2):
                            for b in range(2):
                                a_, u_, o_ = RA[:, g % 2, d, b, :], RI[:, g % 2, d, b, :], RR[:, g % 2, d, b, :]
                                if d == 1:
                                    a_, u_, o_ = a_[:, ::-1], u_[:, ::-1], o_[:, ::-1]
                                ins = dve.tensor_tensor_scan(o_, a_, u_, 0.0, ALU.mult, ALU.add)
                                ins.then_inc(*inc("rnn_scan", (g, d, b)))
                        dve.wait_ge(*past("rnn_scan", (g, 1, 1)))
                        chain(dve.tensor_tensor(r[:, 0, :, :], r[:, 0, :, :], r[:, 1, :, :], ALU.add))
                        dve.scalar_tensor_tensor(r[:, 0, :, :], r[:, 0, :, :], 0.5, GG[:, 2 * g:2 * g + 2, :], ALU.mult,
                                                     ALU.mult).then_inc(*inc("rnn_v", g))

            def mixer(s):
                l = (s - 4) // 3
                for i in range(4):
                    step((s, "qa", i))
                step((s, "ka", 0))
                step((s, "va", 0))
                step((s, "bd", 0))
                dve.wait_ge(*past("free_A", (s, "bd", 0)))
                x, t0, e, t1 = ROWS[0:8, 3, :], ROWS[0:8, 4, :], ROWS[0:8, 5, :], ROWS[0:8, 1, :]
                dve.scalar_tensor_tensor(t0, x, -1.0, x, ALU.mult, ALU.max).then_inc(*inc("dt_abs", s))

                def norm_a(j):
                    r = j % 3
                    dve.wait_ge(*past("pa_exp", (s, j)))
                    chain(dve.tensor_tensor(A2S[:, r, 4:6], A2S[:, r, 2:4], A2S[:, r, 4:6], ALU.add))
                    chain(dve.reciprocal(A2S[:, r, 6:8], A2S[:, r, 4:6]))
                    for b, (lo, hi) in enumerate(((0, P), (P, 384))):
                        dve.tensor_scalar(PA[:, r, lo:hi], PA[:, r, lo:hi], A2S[:, r, 6 + b:7 + b], None, ALU.mult).then_inc(*inc("pa_ready", (s, j)))

                for j in range(19):
                    if j < 12:
                        step((s, "cv", j))
                        dve.wait_ge(*past("tap0", (s, j)))
                        for tap in range(1, 4):
                            for jj in range(2):
                                ct = 2 * j + jj
                                w = CW2[:, l, 24 * tap + ct:24 * tap + ct + 1]
                                ins = dve.scalar_tensor_tensor(CB[:, ct, :], CIN[:, j % 2, jj, tap:tap + S], w, CB[:, ct, :],
                                                               ALU.mult, ALU.add)
                                if tap < 3 or jj == 0:
                                    ins.then_inc(*inc("conv_tap", (s, j, tap, jj)))
                            if tap < 3:
                                dve.wait_ge(*past("conv_tap", (s, j, tap, 1)))
                        ins.then_inc(*inc("conv_done", (s, j)))
                    elif j < 16:
                        step((s, "z", j - 12))
                    if j < 16:
                        t, hh = divmod(j, 2)
                        head = (2 * (t // 4) + hh) * 4 + t % 4
                        r = j % 3
                        bank = tile((s, "sc", j))
                        dve.wait_ge(*past(f"bias_in{r}", (s, j)))
                        if j >= 3:
                            dve.wait_ge(*past("tile_done", (s, "pt", j - 3)))
                        dve.scalar_tensor_tensor(PA[:, r, 0:P], bank[:, 0:P], 0.125, BI[:, r, P:S], ALU.mult, ALU.add).then_inc(*inc("pa_part", (s, j)))
                        dve.scalar_tensor_tensor(PA[:, r, P:384], bank[:, P:384], 0.125, BI[:, r, :], ALU.mult, ALU.add).then_inc(*inc("free_D", (s, "sc", j)))
                        dve.wait_ge(*past("pa_part", (s, j)))
                        chain(dve.tensor_reduce(A2S[:, r, 6:7], PA[:, r, 0:P], AX.X, ALU.max))
                        dve.wait_ge(*past("free_D", (s, "sc", j)))
                        chain(dve.tensor_reduce(A2S[:, r, 7:8], PA[:, r, P:384], AX.X, ALU.max))
                        dve.tensor_scalar(A2S[:, r, 0:2], A2S[:, r, 6:8], SNK2[:, l, head:head + 1], -1.0, ALU.max, ALU.mult).then_inc(*inc("neg_max_a", (s, j)))
                    if 1 <= j <= 16:
                        norm_a(j - 1)
                    if j >= 4 and j % 2 == 0:
                        t = (j - 4) // 2
                        bank = y_bank(2 + t % 2)
                        dve.wait_ge(*past("oh_ready", (s, t)))
                        dve.tensor_tensor(OL[:, t, :], bank[:, 0:S], OH[:, t, :].bitcast(F32), ALU.subtract).then_inc(*inc("free_D", (s, "oa", t)))
                softplus(x, None, e, t0, t1, lambda: dve.wait_ge(*past("dt_exp", s)))
                dve.wait_ge(*past("a_exp"))
                chain(dve.tensor_scalar(t0, t0, AL2[:, 4 + l:5 + l], -1.0, ALU.mult, ALU.mult))
                for c in range(2):
                    w = slice(c * P, (c + 1) * P)
                    dve.tensor_tensor_scan(ROWS[0:8, 1, w], ONES[0:8, 0:P], ROWS[0:8, 4, w], 0.0, ALU.mult, ALU.add).then_inc(*inc("g_rows", s))
                for i in range(4):
                    step((s, "ba", i))
                bank = tile((s, "gcol"))
                dve.tensor_copy(GCOL[:, :, :], bank[:, 0:32].rearrange("p (a b) -> p a b", a=4)).then_inc(*inc("free_D", (s, "gcol")))
                bank = tile((s, "nrm"))
                dve.tensor_scalar(ROWS[0:16, 4, :], bank[0:16, 0:S], NORM_EPS, None, ALU.add).then_inc(*inc("free_D", (s, "nrm")))
                dve.wait_ge(*past("free_D", (s, "nrm")))
                dve.reciprocal(ROWS[0:16, 4, :], ROWS[0:16, 4, :]).then_inc(*inc("nrm_recip", s))
                for hf in range(2):
                    k_ = (s, hf)
                    for j in range(5):
                        if j < 4:
                            h = 4 * hf + j
                            b0 = tile((s, "bc", h, 0))
                            dve.tensor_copy(GLT[:, 0, h:h + 1], b0[:, P - 1:P]).then_inc(*inc("gl_part", (s, h)))
                            for c in range(2):
                                dve.wait_ge(*past("free_D", (s, "gcol")))
                                dve.scalar_tensor_tensor(EA[:, c, j, :], b0[:, c * P:(c + 1) * P], GCOL[:, c, h:h + 1], TRI[:, :],
                                                             ALU.subtract, ALU.add).then_inc(*inc("e_raw", (s, h)))
                            b1 = tile((s, "bc", h, 1))
                            k, q = CB[:, 8 + h, :], CB[:, h, :]
                            chain(dve.tensor_tensor(k, k, b1[:, S:2 * S], ALU.mult))
                            dve.tensor_tensor(q, q, b1[:, 0:S], ALU.mult).then_inc(*inc("free_D", (s, "bc", h, 1)))
                            dve.wait_ge(*past("eg_ready", (s, h)))
                            dve.tensor_tensor(KBT[:, h % 2, :], k, b0[:, S:2 * S], ALU.mult).then_inc(*inc("free_D", (s, "bc", h, 0)))
                            dve.wait_ge(*past("free_D", (s, "bc", h, 0)))
                            chain(dve.tensor_tensor(KBG[:, j, :], KBT[:, h % 2, P:S], EG[:, h % 2, P:S], ALU.mult))
                            dve.tensor_tensor(QD[:, j, :], q[:, P:S], EG[:, h % 2, P:S], ALU.mult).then_inc(*inc("kb_ready", (s, h)))
                        if j >= 1:
                            h = 4 * hf + j - 1
                            bank = tile((s, "la", h))
                            dve.wait_ge(*past("e_ready", (s, h)))
                            dve.tensor_tensor(LT[:, :, h % 4, :], pair_of(bank[:, 0:S]), EA[:, :, h % 4, :], ALU.mult).then_inc(*inc("lt_ready", (s, h)))
                            dve.wait_ge(*past("lt_ready", (s, h)))
                            dve.tensor_tensor(EA[:, :, h % 4, :], pair_of(bank[:, S:2 * S]), EA[:, :, h % 4, :], ALU.mult).then_inc(*inc("free_D", (s, "la", h)))
                    for c in range(2):
                        dve.wait_ge(*past("m_ready", (k_, 0, c)))
                        eye = IDN[:, :].rearrange("p (a b) -> p a b", a=1).broadcast_to([P, 4, P])
                        dve.tensor_tensor(UU[:, c, :, :], eye, MM[:, c, :, :], ALU.subtract).then_inc(*inc("u0_ready", (k_, c)))
                    for i in range(1, 7):
                        if i <= 4:
                            step((s, "ga" if hf else "gb", i - 1))
                        if hf == 1 and 2 <= i <= 5:
                            dve.wait_ge(*past("free_A", (s, "ga", i - 2)))
                            m = M1[:, 2 * i - 4:2 * i - 2, :]
                            dve.tensor_tensor(m, m, GT[:, :, :], ALU.mult).then_inc(*inc("gate_a_used", (s, i - 2)))
                        for c in range(2):
                            for kind, dst in (("dt", TT), ("du", UU)):
                                if kind == "dt" and i == 6:
                                    continue
                                bank = tile((k_, kind, i, c))
                                m = dst[:, c, :, :]
                                if i == 1:
                                    dve.wait_ge(*past("free_A", (k_, "t0", c)))
                                dve.tensor_tensor(m, m, bank.rearrange("p (a b) -> p a b", a=4), ALU.subtract).then_inc(*inc("free_D", (k_, kind, i, c)))
                    for c in range(2):
                        bank = tile((k_, "vt", c))
                        for j in range(4):
                            ins = dve.tensor_scalar(XX[:, c, j, :], bank[:, j * P:(j + 1) * P],
                                                    GCOL[:, 2 + c, 4 * hf + j:4 * hf + j + 1], None, ALU.mult)
                            ins.then_inc(*(inc("free_D", (k_, "vt", c)) if j == 3 else inc("vb_part", (k_, c, j))))
                    bank = tile((k_, "kt"))
                    dve.wait_ge(*past("tail_ready", (s, 4 * hf + 3)))
                    for j in range(4):
                        ins = dve.tensor_scalar(KTL[:, j, :], bank[:, j * P:(j + 1) * P],
                                                GLT[:, 1, 4 * hf + j:4 * hf + j + 1], None, ALU.mult)
                        ins.then_inc(*(inc("free_D", (k_, "kt")) if j == 3 else inc("kt_part", (k_, j))))
                    bank = tile((k_, "ks"))
                    dve.wait_ge(*past("free_D", (k_, "vt", 1)))
                    dve.tensor_tensor(XX[:, 1, :, :], XX[:, 1, :, :], bank.rearrange("p (a b) -> p a b", a=4), ALU.subtract).then_inc(*inc("free_D", (k_, "ks")))
                bank = tile((s, "onrm"))
                dve.tensor_scalar(ROWS[0:8, 4, :], bank[0:8, 0:S], 1.0 / 128, NORM_EPS, ALU.mult, ALU.add).then_inc(*inc("free_D", (s, "onrm")))
                dve.wait_ge(*past("free_D", (s, "onrm")))
                dve.reciprocal(ROWS[0:8, 3, :], ROWS[0:8, 4, :]).then_inc(*inc("onrm_recip", s))

                def lo_pair(dst, hi, m, wait, name):
                    dve.wait_ge(*past(wait, (s, m)))
                    dve.tensor_tensor(dst[:, 2 * m:2 * m + 2, :], CB[:, 2 * m:2 * m + 2, :],
                                          hi[:, 2 * m:2 * m + 2, :].bitcast(F32), ALU.subtract).then_inc(*inc(name, (s, m)))

                for m in range(4):
                    bank = tile((s, "obc", m))
                    o = CB[:, 2 * m:2 * m + 2, :]
                    of = o.rearrange("p a b -> p (a b)")
                    dve.scalar_tensor_tensor(of, of, DNG[:, l:l + 1], bank, ALU.mult, ALU.mult).then_inc(*inc("free_D", (s, "obc", m)))
                    dve.wait_ge(*past("free_D", (s, "obc", m)))
                    dve.wait_ge(*past("cb_ready", (s, 15)))
                    dve.tensor_tensor(o, o, ZT[:, 2 * m:2 * m + 2, :], ALU.mult).then_inc(*inc("ov_ready", (s, m)))
                    if m:
                        lo_pair(OL, OH, m - 1, "ohb_ready", "olb_ready")
                lo_pair(OL, OH, 3, "ohb_ready", "olb_ready")
                for i in range(4):
                    step((s, "bb", i))
                    bank = tile((s, "bb", i))
                    dve.wait_ge(*past("free_A", (s, "gb", i)))
                    o = CB[:, 2 * i:2 * i + 2, :]
                    dve.tensor_tensor(o, GBT[:, 2 * i:2 * i + 2, :], pair_of(bank), ALU.mult).then_inc(*inc("free_D", (s, "bb", i)))
                    dve.wait_ge(*past("free_D", (s, "bb", i)))
                    dve.tensor_tensor(o, o, M1[:, 2 * i:2 * i + 2, :], ALU.add).then_inc(*inc("mv_ready", (s, i)))
                    dve.wait_ge(*past("mv_ready", (s, i)))
                    lo_pair(XL, XH, i, "mh_ready", "ml_ready")
                for i in range(4):
                    step((s, "out", i))

            norm(0)
            for s in range(1, n_sub):
                if s in (1, 3):
                    mlp(s)
                elif s == 2:
                    recurrence(s)
                elif is_mix(s):
                    mixer(s)
                else:
                    ffn(s)
                norm(s)

        @block.gpsimd
        def _(pool):
            def chain(ins):
                link(pool, ins, "pool_chain")

            pool.memset(ONES[:, :], 1.0).then_inc(*inc("ones_part"))
            pool.wait_ge(*past("ones_part"))
            chain(pool.memset(ESEL[:, :], 0.0))
            pool.memset(ESEL[:, 15:16], 1.0).then_inc(*inc("ones_ready"))
            pool.wait_ge(*past("ones_ready"))
            pool.wait_ge(*past("ones_ready"))
            pool.wait_ge(*past("rel_in"))
            pool.memset(RBI[32:33, :], 1.0).then_inc(*inc("rel_ready"))
            pool.wait_ge(*past("rel_ready"))

            def load_gb(s):
                for q in range(2):
                    v = LN[s][q]
                    pool.dma_start(GB[:, q, :], bass.AP(v.tensor, v.offset, [[0, P], [1, D]])).then_inc(*inc("gb_in", s, 16))

            def scaled(s):
                pool.wait_ge(*past("gb_in", s))
                for t in range(NT):
                    pool.wait_ge(*past("xn_ready", (s, t)))
                    chain(pool.tensor_tensor(XS[:, t, :], XN[:, t, :], GB[:, 0, :], ALU.mult))
                    chain(pool.tensor_tensor(XS[:, t, :], XS[:, t, :], GB[:, 1, :], ALU.add))
                    pool.tensor_scalar(XS[:, t, :], XS[:, t, :], ALPHA, None, ALU.mult).then_inc(*inc("xs_ready", (s, t)))
                    pool.wait_ge(*past("xs_ready", (s, t)))
                pool.wait_ge(*past("xs_ready", (s, 1)))

            load_gb(0)
            for t in range(NT):
                pool.wait_ge(*past("x_in"))
                pool.tensor_scalar(XS[:, t, :], XN[:, t, :], ALPHA, None, ALU.mult).then_inc(*inc("xs_ready", (-1, t)))
                pool.wait_ge(*past("xs_ready", (-1, t)))

            def ada_load(q0, q1):
                for q in range(q0, min(q1, n_ada)):
                    pool.wait_ge(*past("ada_used", q - NADR))
                    pool.dma_start(ADR[:, q % NADR, :], ada_src(q)).then_inc(*inc(f"ada_next{q % NADR}", q, 16))

            ada_load(24, 70 + NADR)
            if n_sub > 1:
                scaled(0)
                load_gb(1)
                ada_load(70 + NADR, n_ada)
            if n_sub > 2:
                scaled(1)
            for s in range(2, n_sub):
                l = (s - 4) // 3
                if s == 2:
                    pool.wait_ge(*past("xl_ready", (2, 3)))
                    pool.memset(XP[:, :, :, :], 0.0).then_inc(*inc("xp_zero"))
                    pool.wait_ge(*past("xp_zero"))

                    def gate_weights(g):
                        if g >= 2:
                            pool.wait_ge(*past("tile_done", ("gate", g - 2, 1, 1)))
                        for d in range(2):
                            for q, name in enumerate(("rnn_w_a", "rnn_w_x")):
                                i0 = 4 * d + 2 * q
                                pool.dma_start(WG[:, g % 2, i0:i0 + 2, :], I[name][0, d, 2 * g:2 * g + 2].rearrange("b i j -> i b j")).then_inc(*inc(f"rnn_w_in{g % 2}", g, 16))

                    pool.wait_ge(*past("tile_done", ("ada", n_ada // 8 - 1)))
                    for g in range(2):
                        gate_weights(g)
                    for g in range(8):
                        pool.wait_ge(*past("free_A", ("gate", g, 1, 1)))
                        xc = XC[:, 2 * g:2 * g + 2, :].rearrange("p (o b) s -> p o b s", o=1).broadcast_to([RB_W, 2, 2, S])
                        chain(pool.tensor_tensor(RI[:, g % 2, :, :, :], RI[:, g % 2, :, :, :], xc, ALU.mult))
                        pool.tensor_tensor(RI[:, g % 2, :, :, :], RI[:, g % 2, :, :, :], xc, ALU.add).then_inc(*inc("rnn_ix", g))
                        pool.wait_ge(*past("rnn_ix", g))
                        if g < 6:
                            gate_weights(g + 2)
                    load_gb(2)
                elif is_mix(s):
                    if s == 5:
                        pool.wait_ge(*past("y_free", (3, 1)))
                    pool.wait_ge(*past("xl_ready", (s, 3)))
                    pool.memset(CIN[:, :, :, :], 0.0).then_inc(*inc("cin_zero", s))
                    pool.wait_ge(*past("cin_zero", s))

                    def bias(j):
                        t, hh = divmod(j, 2)
                        head = (2 * (t // 4) + hh) * 4 + t % 4
                        if j >= 3:
                            pool.wait_ge(*past("free_D", (s, "sc", j - 3)))
                        src = bass.AP(BIAS.tensor, head * P * EXT + P - 1, [[EXT - 1, P], [1, S]])
                        pool.dma_start(BI[:, j % 3, :], src).then_inc(*inc(f"bias_in{j % 3}", (s, j), 16))

                    if s == 5:
                        pool.dma_start(LVL[:, :], C["levels_t"]).then_inc(*inc("dn_const_in", None, 16))
                        pool.dma_start(TRI[:, :], C["causal_t"]).then_inc(*inc("dn_const_in", None, 16))
                        pool.wait_ge(*past("dn_const_in"))
                    for j in range(19):
                        if j < 16:
                            bias(j)
                        if j >= 3:
                            u = j - 3
                            pool.wait_ge(*past(*(("tanh_ready", (s, u)) if u < 12 else ("free_A", (s, "z", u - 12)))))
                            v = CB[:, 2 * u:2 * u + 2, :] if u < 12 else ZT[:, 2 * u - 24:2 * u - 22, :]
                            chain(pool.tensor_tensor(TH[:, u % 2, :, :], TH[:, u % 2, :, :], v, ALU.mult))
                            pool.tensor_tensor(v, v, TH[:, u % 2, :, :], ALU.add).then_inc(*inc("cb_ready", (s, u)))
                            pool.wait_ge(*past("cb_ready", (s, u)))
                    for hf in range(2):
                        k_ = (s, hf)
                        for i in range(7):
                            for c in range(2):
                                if i == 0:
                                    pool.wait_ge(*past("free_D", (s, "la", 4 * hf + 3)))
                                elif i == 1:
                                    pool.wait_ge(*past("u0_ready", (k_, c)))
                                else:
                                    pool.wait_ge(*past("tile_done", (k_, "x", i - 1, c)))
                                lev = LVL[:, i * P:(i + 1) * P].rearrange("p (a b) -> p a b", a=1).broadcast_to([P, 4, P])
                                pool.tensor_tensor(MM[:, c, :, :], LT[:, c, :, :], lev, ALU.mult).then_inc(*inc("m_ready", (k_, i, c)))
                                pool.wait_ge(*past("m_ready", (k_, i, c)))
                    pool.wait_ge(*past("olb_ready", (s, 3)))
                    load_gb(s)
                else:
                    load_gb(s)
                if s + 1 < n_sub:
                    scaled(s)

    return made


_INS = ["x", "c", "ada_w", "ada_b", "ln_g", "ln_b", "attn_w_in", "attn_w_out", "attn_sinks", "rnn_w_in", "rnn_conv_w",
        "rnn_conv_b", "rnn_w_a", "rnn_b_a", "rnn_w_x", "rnn_b_x", "rnn_lam", "rnn_w_out", "mlp_w1", "mlp_w2",
        "rel_bias_2", "ln_g_2", "ln_b_2", "ffn_w13_2", "ffn_w2_2", "w_in_2", "conv_w_2", "a_log_2", "dt_bias_2",
        "dn_norm_g_2", "sinks_2", "w_branch_a_2", "w_branch_b_2", "w_out_2"]


def kernel(**inputs):
    import concourse.bacc as _bacc
    from concourse.bass_utils import run_bass_kernel_spmd as _run

    arrays = {n: np.ascontiguousarray(inputs[n]) for n in _INS}
    tables = shape_constants()

    def program(counts):
        nc = _bacc.Bacc("TRN2", target_bir_lowering=False, num_devices=1)

        def dram(name, a, kind):
            return nc.dram_tensor(name, a.shape, mybir.dt.from_np(a.dtype), kind=kind).ap()

        ins = {n: dram(f"in_{n}_dram", a, "ExternalInput") for n, a in arrays.items()}
        consts = {n: dram(f"table_{n}_dram", a, "ExternalInput") for n, a in tables.items()}
        out = nc.dram_tensor("out_0_dram", (1, S, D), F32, kind="ExternalOutput").ap()
        return nc, build(nc, ins, consts, out, counts, N_SUB)

    _, counts = program({})
    nc, _ = program(counts)
    feed = {f"in_{n}_dram": a for n, a in arrays.items()}
    feed.update({f"table_{n}_dram": a for n, a in tables.items()})
    r = _run(nc, [feed], core_ids=[0])
    return r.results[0]["out_0_dram"]
```

```python
import math
from contextlib import ExitStack

import numpy as np

import concourse.bass as bass
from concourse import mybir

F32 = mybir.dt.float32
F32R = mybir.dt.float32r
ALU = mybir.AluOpType
ACT = mybir.ActivationFunctionType
AX = mybir.AxisListType

P = 128
S = 256
NT = S // P
D = 1024
KC = D // P
NEG = -1e30
N_SUB = 10
LN_EPS = 1e-5
ALPHA = 4.0 ** 0.25
NRAW = 3
NSPL = 3
SLOT = 2048
NTB = 4
NADR = 4
HD1 = 128
NH1 = 8
RB_N = 16
RB_W = 96
FF1 = 4096
FF2 = 2816
NB_BUCKETS = 32
NORM_EPS = 1e-6
EXT = 3 * P


def shape_constants():
    c = {}
    c["ident"] = np.eye(P, dtype=np.float32)
    q = np.arange(P)[:, None, None] + P * np.arange(2)[None, :, None]
    k = np.arange(S)[None, None, :]
    c["window"] = np.where(np.abs(q - k) <= P, 0.0, NEG).astype(np.float32).reshape(P, 2 * S)
    inv = np.float32(500000.0) ** (-np.arange(0, 32, 2, dtype=np.float32) / np.float32(32))
    ang = np.arange(S, dtype=np.float32)[:, None] * inv[None, :].astype(np.float32)
    cs = np.cos(ang).T.astype(np.float32)
    sn = np.sin(ang).T.astype(np.float32)
    c["rope_cos"] = np.tile(np.concatenate([cs, cs]), (1, 2)).astype(np.float32)
    c["rope_sin"] = np.tile(np.concatenate([sn, sn]), (1, 2)).astype(np.float32)
    rot = np.zeros((32, 32), np.float32)
    for m in range(16):
        rot[m + 16, m] = -1.0
        rot[m, m + 16] = 1.0
    c["rope_rot"] = rot
    rel = 255 - np.arange(EXT)
    n = np.maximum(rel, 0)
    nf = np.maximum(n, 1).astype(np.float32)
    large = 16 + (np.log(nf / np.float32(16)) / np.float32(math.log(128 / 16)) * np.float32(16)).astype(np.int32)
    bucket = np.where(n < 16, n, np.minimum(large, 31))
    band = (rel >= 0) & (rel < P)
    hot = np.zeros((33, EXT), np.float32)
    for m in range(EXT):
        if band[m]:
            hot[bucket[m], m] = 1.0
        else:
            hot[32, m] = NEG
    c["bucket_hot"] = hot
    mi, ci = np.arange(P)[:, None], np.arange(P)[None, :]
    c["causal_t"] = np.where(ci >= mi, 0.0, NEG).astype(np.float32)
    lv = []
    for i in range(7):
        s = 1 << i
        lv.append(((ci // (2 * s) == mi // (2 * s)) & (ci % (2 * s) >= s) & (mi % (2 * s) < s)).astype(np.float32))
    c["levels_t"] = np.concatenate(lv, 1)
    sc = np.ones((16, 1), np.float32)
    sc[0:8] = 1.0 / 128
    c["norm_scale"] = sc
    return c


def build(nc, I, C, out, counts, n_sub):
    final = len(counts) > 0
    known = dict(counts)
    made = {}
    ctx = ExitStack()
    with ctx:
        base = -(-nc.sbuf_base // 32) * 32
        KB = 1024
        pos = {"at": base}

        def put(name, shape, dt=F32, at=None):
            n = 4
            for x in shape[1:]:
                n *= x
            n = -(-n // 32) * 32
            off = pos["at"] if at is None else at
            if at is None:
                pos["at"] += n
            return nc.alloc_sbuf_tensor_at(name, shape, dt, offset=off)

        RAW = put("weights_raw", [P, NRAW, SLOT])
        WHI = put("weights_hi", [P, NSPL, SLOT], F32R)
        WLO = put("weights_lo", [P, NSPL, SLOT], F32R)
        XN = put("x_rows", [P, NT, D])
        XS = put("x_scaled", [P, NT, D])
        XH = put("xt_hi", [P, KC, S], F32R, at=pos["at"])
        act1 = pos["at"]
        pos["at"] += 8 * KB
        XL = put("xt_lo", [P, KC, S], F32R)
        act2 = pos["at"]
        OH = put("ot_hi", [P, KC, S], F32R)
        OL = put("ot_lo", [P, KC, S], F32R)
        YH = put("rnn_yt_hi", [RB_W, 4, 2, S], F32R, at=act2)
        YL = put("rnn_yt_lo", [RB_W, 4, 2, S], F32R, at=act2 + 8 * KB)
        gbc_at = pos["at"]
        GB = put("ln_gb_rows", [P, 2, D])
        IDN = put("ident", [P, P])
        ONES = put("ones", [P, P])
        ESEL = put("ones_column", [P, 31])
        NSC = put("norm_scale", [16, 1])
        lv_at = pos["at"]
        WIN = put("window", [P, 2 * S], at=lv_at)
        COS = put("rope_cos", [32, 2 * S], at=lv_at + 2 * KB)
        SIN = put("rope_sin", [32, 2 * S], at=lv_at + 4 * KB)
        ROT = put("rope_rot", [32, 32], at=lv_at + 6 * KB)
        LVL = put("levels_t", [P, 7 * P], at=lv_at)
        TRI = put("causal_t", [P, P], at=lv_at + 3584)
        pos["at"] = lv_at + 6 * KB + 128
        LNC1 = put("ln1_cols", [P, 64])
        CC = put("c_cols", [P, 8])
        ADB = put("ada_bias_cols", [P, 96])
        LNC2 = put("ln2_cols", [P, 96])
        CW2 = put("conv2_cols", [P, 2, 96])
        DNG = put("dn_norm_cols", [P, 2])
        RC1 = put("rnn_conv_cols", [RB_W, 80])
        RC2 = put("rnn_gate_cols", [RB_W, 96])
        MOD = put("ada_mod_cols", [P, 4, 24])
        GP = put("prep_scale", [P, 4, 8])
        BP = put("prep_shift", [P, 4, 8])
        SNK = put("sinks1", [P, 8])
        SNK2 = put("sinks2", [P, 2, 16])
        AL2 = put("a_log_dt", [8, 8])
        ST = put("ln_stats", [P, NT, 2, 6])
        MV = put("ln_mean_var", [P, NT, 2])
        RV = put("ln_rstd", [P, NT, 4])
        RCOL = put("rnn_decay_cols", [RB_W, 8, 32])
        AT1 = put("attn_small", [P, 6, 16])
        A2S = put("attn2_small", [P, 3, 8])
        GCOL = put("g_cols", [P, 4, 8])
        GLT = put("g_last_tail", [P, 2, 8])
        gate_at = pos["at"]
        GATE = put("gate_rows", [P, D])
        pos["at"] += 64
        hid_at = pos["at"]
        HH = put("hid_hi", [P, 2, 512], F32R)
        HL = put("hid_lo", [P, 2, 512], F32R)
        RB = put("hid_act", [P, 2, 512])
        VB = put("hid_val", [P, 2, 512])
        area = pos["at"]

        ACC = put("ada_acc", [P, 3, D], at=area)
        ADR = put("ada_ring", [P, NADR, D], at=area + 12 * KB)
        a = area + (12 + 4 * NADR) * KB
        QT = put("q1_t", [P, NH1, S], at=a)
        KT = put("k1_t", [P, 2, S], at=a + 8 * KB)
        VR = put("v1_rows", [P, NT, S], at=a + 10 * KB)
        PTB = put("probs1_t", [P, 2, 4, P], at=a + 12 * KB)
        PR = put("probs1", [P, NH1, 2, S], at=hid_at)
        PST = put("param_rows", [P, 8, P], at=hid_at)
        CROW = put("c_rows", [8, P], at=hid_at + 6 * KB)
        RTMP = put("rope_tmp", [32, 2, 512], at=a + 12 * KB)
        EXS = put("bias_stage", [P, 4, EXT], at=area + 28 * KB)
        HOT = put("bucket_hot", [33, EXT], at=area + 34 * KB)
        RBI = put("rel_bias", [33, 16], at=area + 35 * KB + 512)
        XTF = put("xt", [P, KC, S], at=hid_at)
        a = hid_at
        XC = put("rnn_conv_out", [RB_W, RB_N, S], at=a)
        GG = put("rnn_gelu_gate", [RB_W, RB_N, S], at=a + 16 * KB)
        WG = put("rnn_gate_w", [RB_W, 2, 8, RB_W], at=a + 32 * KB)
        RR = put("rnn_r", [RB_W, 2, 2, 2, S], at=a + 38 * KB)
        RI = put("rnn_i", [RB_W, 2, 2, 2, S], at=a + 46 * KB)
        RA = put("rnn_a", [RB_W, 2, 2, 2, S], at=a + 54 * KB)
        XP = put("rnn_conv_in", [RB_W, 2, 2, 260], at=gbc_at)
        RTM = put("rnn_tmp", [RB_W, 2, 2, S], at=lv_at)
        a = hid_at
        CB = put("conv_qkv_t", [P, 24, S], at=a)
        ZT = put("z_silu_t", [P, 8, S], at=a + 24 * KB)
        QA = put("qa_t", [P, 8, S], at=a + 32 * KB)
        M1 = put("mix_t", [P, 8, S], at=a + 32 * KB)
        KA = put("ka_t", [P, 2, S], at=a + 40 * KB)
        VA = put("va_rows", [P, NT, S], at=a + 42 * KB)
        PA = put("probs_a", [P, 3, 384], at=a + 44 * KB)
        BI = put("bias_rows", [P, 3, S], at=a + 44 * KB + 4608)
        PTA = put("probs_a_t", [P, 2, 384], at=a + 44 * KB + 7680)
        TH = put("silu_tanh", [P, 2, 2, S], at=gbc_at)
        GBT = put("gate_b_t", [P, 8, S], at=a + 40 * KB)
        b = a + 55 * KB
        CIN = put("conv_in", [P, 2, 2, 260], at=gate_at)
        ROWS = put("dn_rows", [16, 6, S], at=b)
        a2 = a + 48 * KB
        EG = put("exp_g", [P, 2, S], at=a2)
        KBT = put("k_beta_t", [P, 2, S], at=a2 + 2 * KB)
        GT = put("gate_a_t", [P, 2, S], at=a2 + 2 * KB)
        KBG = put("k_beta_g_t", [P, 4, P], at=a2 + 4 * KB)
        QD = put("q_decay_t", [P, 4, P], at=gate_at)
        KTL = put("k_tail_rows", [P, 4, P], at=gate_at + 2 * KB)
        SQ = put("squares", [P, 2, 256], at=a2 + 4 * KB)
        LT = put("l_t", [P, 2, 4, P], at=act2)
        EA = put("a_t", [P, 2, 4, P], at=act2 + 4 * KB)
        MM = put("l_level_t", [P, 2, 4, P], at=act2 + 8 * KB)
        XX = put("x_level", [P, 2, 4, P], at=act2 + 12 * KB)
        TT = put("t_inv", [P, 2, 4, P], at=gbc_at)
        UU = put("t_inv_t", [P, 2, 4, P], at=gbc_at + 4 * KB)

        TB = ctx.enter_context(nc.psum_tensor("tiles", [P, NTB, 512], F32))
        Y = ctx.enter_context(nc.psum_tensor("y_rows", [P, NT, D], F32))

        def y_bank(i):
            return Y[:, i // 2, i % 2 * 512:i % 2 * 512 + 512]

        BIAS = nc.dram_tensor("bias_ext", [16, P, EXT], F32, kind="Internal").ap()

        sems = {}

        def sem(name):
            if name not in sems:
                sems[name] = ctx.enter_context(nc.semaphore(name))
            return sems[name]

        for name in sorted({k[0] for k in known}):
            sem(name)
        level = {}

        def inc(name, key=None, by=1):
            level[name] = level.get(name, 0) + by
            made[(name, key)] = level[name]
            return sem(name), by

        def past(name, key=None):
            return sem(name), known.get((name, key), 1)

        def link(eng, ins, name):
            level[name] = level.get(name, 0) + 1
            ins.then_inc(sem(name), 1)
            eng.wait_ge(sem(name), level[name])

        block = ctx.enter_context(nc.Block())

        slots = []

        def kview(w, c0, n):
            return w.rearrange("(k p) n -> p k n", p=P)[:, :, c0:c0 + n]

        def add_cols(label, w, c0, n):
            slots.append((label, P, (KC, n), [(None, kview(w, c0, n))]))

        def add_rows(label, w, r0, p, nk):
            slots.append((label, p, (nk, D), [(None, w[r0:r0 + p * nk, :].rearrange("(k p) n -> p k n", p=p))]))

        def plan():
            for s in range(n_sub):
                if s == 0:
                    for i in range(6):
                        add_cols((s, "in", i), I["attn_w_in"][0], 256 * i, 256)
                    for i in range(4):
                        add_rows((s, "out", i), I["attn_w_out"][0], 256 * i, P, 2)
                elif s in (1, 3):
                    n = FF1 // 256
                    for i in range(n + 1):
                        if i < n:
                            add_cols((s, "w1", i), I["mlp_w1"][s // 2], 256 * i, 256)
                        if i > 0:
                            add_rows((s, "w2", i - 1), I["mlp_w2"][s // 2], 256 * (i - 1), P, 2)
                elif s == 2:
                    for i in range(8):
                        add_cols((s, "gt", i), I["rnn_w_in"][0], 192 * (8 + i), 192)
                    for i in range(12):
                        if i < 8:
                            add_cols((s, "in", i), I["rnn_w_in"][0], 192 * i, 192)
                        if i >= 4:
                            add_rows((s, "out", i - 4), I["rnn_w_out"][0], 192 * (i - 4), RB_W, 2)
                elif s % 3 != 2:
                    l, f = (s - 4) // 3, (s - 4) % 3 // 2
                    n = FF2 // 256
                    for i in range(n + 1):
                        if i < n:
                            add_cols((s, "g", i), I["ffn_w13_2"][l, f], 256 * i, 256)
                            add_cols((s, "u", i), I["ffn_w13_2"][l, f], FF2 + 256 * i, 256)
                        if i > 0:
                            add_rows((s, "w2", i - 1), I["ffn_w2_2"][l, f], 256 * (i - 1), P, 2)
                else:
                    l = (s - 4) // 3
                    w = I["w_in_2"][l]
                    for i in range(4):
                        c, gg = i // 2, i % 2
                        src = [((slice(None), g * P + hh * 64, 64), kview(w, (2 * c + hh) * 256 + (2 * gg + g) * 64, 64))
                               for g in range(2) for hh in range(2)]
                        slots.append(((s, "qa", i), P, (KC, 256), src))
                    add_cols((s, "ka", 0), w, 1024, 256)
                    add_cols((s, "va", 0), w, 1280, 256)
                    add_cols((s, "bd", 0), w, 4608, 136)
                    for i in range(12):
                        add_cols((s, "cv", i), w, 1536 + 256 * i, 256)
                    for i in range(4):
                        add_cols((s, "z", i), w, 4624 + 256 * i, 256)
                    for i in range(4):
                        src = []
                        for hh in range(2):
                            for c in range(2):
                                r = (2 * c + hh) * 256
                                src.append(((slice(64 * hh, 64 * hh + 64), 4 * c, 4),
                                            I["w_branch_a_2"][l][r:r + 256, 256 * i:256 * i + 256]
                                            .rearrange("(g d) n -> d g n", d=64)))
                        slots.append(((s, "ba", i), P, (KC, 256), src))
                    for i in range(4):
                        add_cols((s, "gb", i), w, 6672 + 256 * i, 256)
                    for i in range(4):
                        add_cols((s, "ga", i), w, 5648 + 256 * i, 256)
                    for i in range(4):
                        add_cols((s, "bb", i), I["w_branch_b_2"][l], 256 * i, 256)
                    for i in range(4):
                        add_rows((s, "out", i), I["w_out_2"][l], 256 * i, P, 2)

        plan()
        number = {x[0]: n for n, x in enumerate(slots)}
        last_slot = {x[0][0]: n for n, x in enumerate(slots)}

        def split_upto(label):
            n = number[label]
            return n + NSPL - (2 if n == last_slot[label[0]] else 1)

        slot_end = [("rows_done" if x[0][1] in ("w2", "out") else "tile_done", x[0]) for x in slots]
        landed_at = {}
        total = [0] * NRAW
        for n, x in enumerate(slots):
            total[n % NRAW] += 16 * len(x[3])
            landed_at[n] = total[n % NRAW]

        y_end = {x[0][0]: ("rows_done", x[0]) for x in slots if x[0][1] in ("w2", "out")}

        def slot_view(ring, n, depth):
            _, p, (a_, b_), _ = slots[n]
            return ring[0:p, n % depth, 0:a_ * b_].rearrange("p (a b) -> p a b", a=a_)

        LN = {}
        for s in range(4):
            LN[s] = (I["ln_g"][s // 2, s % 2], I["ln_b"][s // 2, s % 2], LNC1[:, 8 * s:8 * s + 8],
                     LNC1[:, 32 + 8 * s:40 + 8 * s])
        for s in range(4, 10):
            i = s - 4
            LN[s] = (I["ln_g_2"][i // 3, i % 3], I["ln_b_2"][i // 3, i % 3], LNC2[:, 8 * i:8 * i + 8],
                     LNC2[:, 48 + 8 * i:56 + 8 * i])

        def is_mix(s):
            return s in (5, 8)

        def is_ffn(s):
            return s >= 4 and not is_mix(s)

        def row_view(x, p):
            return x.rearrange("(r p) -> r p", p=p)

        prm = []
        for s in range(4):
            prm.append((row_view(LN[s][0], P), 8 * s, 0))
            prm.append((row_view(LN[s][1], P), 32 + 8 * s, 0))
            prm.append((row_view(I["ada_b"][s // 2, s % 2], P), 24 * s, 1))
        for s in range(4, 10):
            prm.append((row_view(LN[s][0], P), 8 * (s - 4), 2))
            prm.append((row_view(LN[s][1], P), 48 + 8 * (s - 4), 2))
        for l in range(2):
            prm.append((I["conv_w_2"][l].rearrange("j (r p) -> (j r) p", p=P), 0, 3 + l))
        prm.append((I["dn_norm_g_2"], 0, 5))
        prm.append((I["rnn_conv_w"][0].rearrange("j (r p) -> (j r) p", p=RB_W), 0, 6))
        prm.append((I["rnn_conv_b"].rearrange("a (r p) -> (a r) p", p=RB_W), 64, 6))
        for n, name in enumerate(("rnn_b_a", "rnn_b_x", "rnn_lam")):
            prm.append((I[name][0].rearrange("j (r p) -> (j r) p", p=RB_W), 32 * n, 7))
        blocks = [(64, P, [LNC1[:, :]]), (96, P, [ADB[:, :]]), (96, P, [LNC2[:, :]]), (96, P, [CW2[:, 0, :]]),
                  (96, P, [CW2[:, 1, :]]), (2, P, [DNG[:, :]]), (80, RB_W, [RC1[:, :]]), (96, RB_W, [RC2[:, :]])]

        n_ada = 24 * min(n_sub, 4)

        def ada_src(q):
            w = I["ada_w"][q // 48, q // 24 % 2]
            third, kc = divmod(q % 24, KC)
            return w[kc * P:(kc + 1) * P, third * D:(third + 1) * D]

        @block.sync
        def _(sp):
            def ada_load(q):
                if q >= NADR:
                    sp.wait_ge(*past("ada_used", q - NADR))
                sp.dma_start(ADR[:, q % NADR, :], ada_src(q)).then_inc(*inc(f"ada_in{q % NADR}", q, 16))

            sp.dma_start(CROW[:, :], I["c"].rearrange("a (r p) -> (a r) p", p=P)).then_inc(*inc("c_in", None, 16))
            sp.dma_start(IDN[:, :], C["ident"]).then_inc(*inc("ident_in", None, 16))
            for q in range(12):
                ada_load(q)
            for t in range(NT):
                sp.dma_start(XN[:, t, :], I["x"][0, t * P:(t + 1) * P, :]).then_inc(*inc("x_in", None, 16))
            for q in range(12, 16):
                ada_load(q)

            def load(n):
                if n >= NRAW:
                    sp.wait_ge(*past("lo_ready", n - NRAW))
                view = slot_view(RAW, n, NRAW)
                for where, src in slots[n][3]:
                    if where is None:
                        dst = view
                    elif where[1] + where[2] <= KC and where[2] == 4:
                        dst = view[where[0], where[1]:where[1] + where[2], :]
                    else:
                        dst = view[where[0], :, where[1]:where[1] + where[2]]
                    sp.dma_start(dst, src).then_inc(*inc(f"landed{n % NRAW}", n, 16))

            for n in range(NRAW):
                load(n)
            for q in range(16, 20):
                ada_load(q)
            for n in range(NRAW, len(slots)):
                load(n)
            for t in range(NT):
                sp.wait_ge(*past("out_rows", t))
                sp.dma_start(out[0, t * P:(t + 1) * P, :], XN[:, t, :]).then_inc(*inc("out_done", None, 16))
            for n in range(4):
                sp.wait_ge(*past(f"bias_out{n}", 12 + n))
            sp.wait_ge(*past("out_done"))

        @block.tensor
        def _(pe):
            tiles = [0]
            owner = {}

            def topen(label, consumer):
                t = tiles[0]
                tiles[0] += 1
                owner[t] = (label, consumer)
                made[("tile", label)] = t
                if t >= NTB:
                    pe.wait_ge(*past("free_" + owner[t - NTB][1], owner[t - NTB][0]))
                return TB[:, t % NTB, :]

            def open_slot(label):
                n = number[label]
                pe.wait_ge(*past("lo_ready", n))
                return n, slot_view(WHI, n, NSPL), slot_view(WLO, n, NSPL)

            def mm3(o, a, b, c, d, first, last):
                pe.matmul(o, a, c, start=first, stop=False)
                pe.matmul(o, a, d, start=False, stop=False)
                return pe.matmul(o, b, c, start=False, stop=last)

            def cols_slot(label, xh, xl, consumer, m=P, ready=None, nt=2, step=None):
                n, wh, wl = open_slot(label)
                bank = topen(label, consumer)
                nk = slots[n][2][0]
                order = [(j, k) for k in range(nk) for j in range(nt)] if ready else [(j, k) for j in range(nt) for k in range(nk)]
                for j, k in order:
                    if ready:
                        ready(k)
                    a_ = wh[:, k, (step or m) * j:(step or m) * j + m]
                    b_ = wl[:, k, (step or m) * j:(step or m) * j + m]
                    ins = mm3(bank[0:m, j * S:(j + 1) * S], a_, b_, xh[:, k, :], xl[:, k, :],
                              k == 0 and (j == 0 or not ready), k == nk - 1 and (j == nt - 1 or not ready))
                ins.then_inc(*inc("tile_done", label))

            def v_slot(label, xh, xl, ready=None):
                n, wh, wl = open_slot(label)
                bank = topen(label, "A")
                for t in range(NT):
                    for k in range(KC):
                        xa, xb = xh[:, k, t * P:(t + 1) * P], xl[:, k, t * P:(t + 1) * P]
                        ins = mm3(bank[:, t * S:(t + 1) * S], xa, xb, wh[:, k, :], wl[:, k, :], k == 0, k == KC - 1)
                ins.then_inc(*inc("tile_done", label))

            def rows_slot(label, lh, ll, k0, first, last, s):
                n, wh, wl = open_slot(label)
                for t in range(NT):
                    for kk in range(2):
                        xa, xb = lh(k0 + kk)[:, t * P:(t + 1) * P], ll(k0 + kk)[:, t * P:(t + 1) * P]
                        for h in range(2):
                            ins = mm3(Y[:, t, h * 512:(h + 1) * 512], xa, xb, wh[:, kk, h * 512:(h + 1) * 512],
                                      wl[:, kk, h * 512:(h + 1) * 512], first and kk == 0, last and kk == 1)
                    if last and t == 0:
                        ins.then_inc(*inc("y_half", s))
                ins.then_inc(*inc("rows_done", label))

            def y_wait(s):
                if s > 0:
                    for t in range(NT):
                        pe.wait_ge(*past("y_free", (s - 1, t)))

            def xready(s):
                seen = set()

                def f(k):
                    if k // 2 not in seen:
                        seen.add(k // 2)
                        pe.wait_ge(*past("xl_ready", (s, k // 2)))
                return f

            def ada_reduce(t):
                if 8 * t >= n_ada:
                    return
                pe.wait_ge(*past("ada_used", 8 * t + 7))
                bank = topen(("ada", t), "D")
                for j in range(8):
                    ins = pe.matmul(bank[:, j:j + 1], ACC[:, t % 3, j * P:(j + 1) * P], ONES[:, 0:1], start=True, stop=True)
                ins.then_inc(*inc("tile_done", ("ada", t)))

            def gate_rows(s):
                pe.wait_ge(*past("gate_cols", s))
                for h in range(2):
                    bank = topen(("gate", s, h), "A")
                    for j in range(4):
                        c0 = 16 + 4 * h + j
                        ins = pe.matmul(bank[:, j * P:(j + 1) * P], MOD[:, s, c0:c0 + 1].broadcast_to([P, P]), IDN[:, :],
                                        start=True, stop=True)
                    ins.then_inc(*inc("tile_done", ("gate", s, h)))

            def prep(s):
                banks = [topen(("xt", s, e), "AD"[e % 2 == 0]) for e in range(4)]
                for t in range(NT):
                    if s > 0:
                        pe.wait_ge(*past(f"xn_ready{t}", (s - 1, t)))
                    elif t == 0:
                        pe.wait_ge(*past("x_in"))
                    for e in range(4):
                        for kk in range(2):
                            k = 2 * e + kk
                            ins = pe.transpose(banks[e][:, kk * S + t * P:kk * S + (t + 1) * P], XN[:, t, k * P:(k + 1) * P],
                                               IDN[:, :])
                        if t == 1:
                            ins.then_inc(*inc("tile_done", ("xt", s, e)))

            pe.wait_ge(*past("ident_in"))
            pe.wait_ge(*past("ones_ready"))
            pe.wait_ge(*past("c_in"))
            bank = topen(("param", "c"), "D")
            pe.transpose(bank[:, 0:8], CROW[:, :], IDN[0:8, 0:8]).then_inc(*inc("tile_done", ("param", "c")))
            for n, (rows, width, _) in enumerate(blocks):
                pe.wait_ge(*past(f"param_in{n}", None))
                bank = topen(("param", n), "D")
                pe.transpose(bank[0:width, 0:rows], PST[0:rows, n, 0:width], IDN[0:rows, 0:rows]).then_inc(*inc("tile_done", ("param", n)))
            for t in range(2):
                ada_reduce(t)
            prep(0)

            for i in range(6):
                if i < 5:
                    cols_slot((0, "in", i), XH, XL, "A", ready=xready(0))
                else:
                    v_slot((0, "in", 5), XH, XL)
                if i == 1:
                    pe.wait_ge(*past("const_in"))
                if i > 0:
                    r = i - 1
                    pe.wait_ge(*past("free_A", (0, "in", r)))
                    src = QT[0:32, 2 * r:2 * r + 2, :] if r < 4 else KT[0:32, :, :]
                    bank = topen(("rot", r), "D")
                    pe.matmul(bank[0:32, :], ROT[:, :], src.rearrange("p a b -> p (a b)"), start=True, stop=True).then_inc(*inc("tile_done", ("rot", r)))
            def scores1(h):
                pe.wait_ge(*past("rope_ready", 4))
                bank = topen(("sc", h), "D")
                for b in range(2):
                    ins = pe.matmul(bank[:, b * S:(b + 1) * S], QT[:, h, b * P:(b + 1) * P], KT[:, h // 4, :],
                                    start=True, stop=True)
                ins.then_inc(*inc("tile_done", ("sc", h)))

            def turn1(h):
                pe.wait_ge(*past("probs_ready", h))
                if h >= 2:
                    pe.wait_ge(*past("free_A", ("pt", h - 2)))
                bank = y_bank(h % 2)
                for b in range(2):
                    for k in range(2):
                        ins = pe.transpose(bank[:, (2 * b + k) * P:(2 * b + k + 1) * P], PR[:, h, b, k * P:(k + 1) * P],
                                           IDN[:, :])
                ins.then_inc(*inc("tile_done", ("pt", h)))

            def mix1(h):
                pe.wait_ge(*past("free_A", ("pt", h)))
                if h % 2 == 0:
                    if h >= 4:
                        pe.wait_ge(*past("free_D", ("o", h // 2 - 2)))
                    pair["bank"] = y_bank(2 + h // 2 % 2)
                for k in range(2):
                    lhs = VR[:, k, (h // 4) * P:(h // 4 + 1) * P]
                    rhs = PTB[:, h % 2, :, :].rearrange("p (b k) q -> p k b q", k=2)[:, k]
                    ins = pe.matmul(pair["bank"][:, (h % 2) * S:(h % 2 + 1) * S].rearrange("p (b q) -> p b q", b=2), lhs, rhs,
                                    start=(k == 0), stop=(k == 1))
                if h % 2 == 1:
                    ins.then_inc(*inc("tile_done", ("o", h // 2)))
                else:
                    ins.then_inc(*inc("mix_half", h))

            pair = {}
            pe.wait_ge(*past("free_A", (0, "in", 5)))
            for h in range(NH1 + 3):
                if h < NH1:
                    scores1(h)
                if 2 <= h < NH1 + 2:
                    turn1(h - 2)
                if h >= 3:
                    mix1(h - 3)
                if h in (2, 3, 7):
                    ada_reduce({2: 2, 3: 3, 7: 4}[h])
                if h == 4:
                    gate_rows(0)
            pe.wait_ge(*past("free_D", ("o", 3)))
            for i in range(4):
                if i == 1:
                    ada_reduce(5)
                rows_slot((0, "out", i), lambda k: OH[:, k, :], lambda k: OL[:, k, :], 2 * i, i == 0, i == 3, 0)

            def mlp(s):
                n = FF1 // 256
                for i in range(n + 1):
                    if i < n:
                        cols_slot((s, "w1", i), XH, XL, "A", ready=xready(s) if i == 0 else None)
                        if i == 0:
                            gate_rows(s)
                    if s == 1 and i in (2, 4, 8, 11, 14, 16):
                        ada_reduce((2, 4, 8, 11, 14, 16).index(i) + 6)
                    if s == 1 and i < n:
                        if i == 0:
                            pe.wait_ge(*past("rel_in"))
                            pe.wait_ge(*past("rel_one"))
                        bank = topen(("ext", i), "A")
                        pe.matmul(bank[:, 0:EXT], RBI[:, i:i + 1].broadcast_to([33, P]), HOT[:, :], start=True, stop=True).then_inc(*inc("tile_done", ("ext", i)))
                    if i > 0:
                        hidden_rows(s, i - 1, n)

            def hidden_rows(s, i, n):
                pe.wait_ge(*past("hid_ready", (s, i)))
                if i == 0:
                    y_wait(s)
                hh, hl = HH[:, i % 2, :], HL[:, i % 2, :]
                rows_slot((s, "w2", i), lambda k: hh.rearrange("p (a b) -> p a b", a=2)[:, k],
                          lambda k: hl.rearrange("p (a b) -> p a b", a=2)[:, k], 0, i == 0, i == n - 1, s)

            def ffn(s):
                n = FF2 // 256
                for i in range(n + 1):
                    if i < n:
                        cols_slot((s, "g", i), XH, XL, "A", ready=xready(s) if i == 0 else None)
                        cols_slot((s, "u", i), XH, XL, "D")
                    if i > 0:
                        hidden_rows(s, i - 1, n)

            def between(s):
                if s + 1 < n_sub:
                    prep(s + 1)

            def recurrence(s):
                for i in range(8):
                    cols_slot((s, "gt", i), XH, XL, "A", m=RB_W, ready=xready(s) if i == 0 else None)
                    if i == 0:
                        gate_rows(s)
                for i in range(12):
                    if i < 8:
                        cols_slot((s, "in", i), XH, XL, "A", m=RB_W)
                    g = i - 1
                    if 0 <= g < 8:
                        pe.wait_ge(*past(f"rnn_w_in{g % 2}", g))
                        for b in range(2):
                            pe.wait_ge(*past("xc_ready", 2 * g + b))
                            for d in range(2):
                                bank = topen(("gate", g, b, d), "A")
                                for q in range(2):
                                    ins = pe.matmul(bank[0:RB_W, q * S:(q + 1) * S], WG[:, g % 2, 4 * d + 2 * q + b, :],
                                                    XC[:, 2 * g + b, :], start=True, stop=True)
                                ins.then_inc(*inc("tile_done", ("gate", g, b, d)))
                    g = i - 4
                    if g >= 0:
                        pe.wait_ge(*past("yl", g))
                        if g == 0:
                            y_wait(s)
                        rows_slot((s, "out", g), lambda k: YH[:, g % 4, k, :], lambda k: YL[:, g % 4, k, :], 0, g == 0, g == 7, s)

            def mixer(s):
                l = (s - 4) // 3

                for i in range(4):
                    cols_slot((s, "qa", i), XH, XL, "A", ready=xready(s) if i == 0 else None)
                cols_slot((s, "ka", 0), XH, XL, "A")
                v_slot((s, "va", 0), XH, XL)
                cols_slot((s, "bd", 0), XH, XL, "A", step=8)

                def scores(j):
                    t, hh = divmod(j, 2)
                    lo, hi = 64 * hh, 64 * hh + 64
                    if j == 0:
                        pe.wait_ge(*past("free_A", (s, "ka", 0)))
                    bank = topen((s, "sc", j), "D")
                    pe.matmul(bank[:, 0:P], QA[lo:hi, t, 0:P], KA[lo:hi, t // 4, 0:P], start=True, stop=True)
                    pe.matmul(bank[:, P:384], QA[lo:hi, t, P:S], KA[lo:hi, t // 4, :], start=True, stop=True).then_inc(*inc("tile_done", (s, "sc", j)))

                def turn(j):
                    pe.wait_ge(*past("pa_ready", (s, j)))
                    pe.wait_ge(*past(*(("free_A", (s, "pt", j - 2)) if j >= 2 else ("y_free", (s - 1, 0)))))
                    bank = y_bank(j % 2)
                    for k in range(3):
                        ins = pe.transpose(bank[:, k * P:(k + 1) * P], PA[:, j % 3, k * P:(k + 1) * P], IDN[:, :])
                    ins.then_inc(*inc("tile_done", (s, "pt", j)))

                def mix(j):
                    t, hh = divmod(j, 2)
                    kv = 2 * (t // 4) + hh
                    pe.wait_ge(*past("free_A", (s, "pt", j)))
                    if hh == 0:
                        pe.wait_ge(*past(*(("free_D", (s, "oa", t - 2)) if t >= 2 else ("y_free", (s - 1, 1)))))
                        pair["bank"] = y_bank(2 + t % 2)
                    o = pair["bank"][64 * hh:64 * hh + 64]
                    v = VA[:, :, kv * 64:(kv + 1) * 64]
                    pt = PTA[:, j % 2, :]
                    pe.matmul(o[:, 0:P], v[:, 0, :], pt[:, 0:P], start=True, stop=True)
                    pe.matmul(o[:, P:S], v[:, 0, :], pt[:, P:2 * P], start=True, stop=False)
                    ins = pe.matmul(o[:, P:S], v[:, 1, :], pt[:, 2 * P:3 * P], start=False, stop=True)
                    if hh == 1:
                        ins.then_inc(*inc("tile_done", (s, "oa", t)))
                    else:
                        ins.then_inc(*inc("mix_half", (s, j)))

                pe.wait_ge(*past("free_A", (s, "va", 0)))
                for j in range(19):
                    if j < 12:
                        cols_slot((s, "cv", j), XH, XL, "A")
                    elif j < 16:
                        cols_slot((s, "z", j - 12), XH, XL, "A")
                    if j < 16:
                        scores(j)
                    if 2 <= j < 18:
                        turn(j - 2)
                    if j >= 3:
                        mix(j - 3)
                for i in range(4):
                    cols_slot((s, "ba", i), OH, OL, "A", ready=(lambda k: pe.wait_ge(*past("free_D", (s, "oa", k)))) if i == 0 else None)
                    if i == 0:
                        norms = topen((s, "nrm"), "D")
                    for u in range(6 * i, min(6 * i + 6, 16)):
                        pe.wait_ge(*past("sq_ready", (s, u)))
                        ins = pe.matmul(norms[0:16, 0:S], ESEL[:, 15 - u:31 - u], SQ[:, u % 2, :], start=(u == 0), stop=(u == 15))
                        ins.then_inc(*(inc("sq_used", (s, u)) if u < 15 else inc("tile_done", (s, "nrm"))))
                    if i == 2:
                        pe.wait_ge(*past("g_rows", s))
                        bank = topen((s, "gcol"), "D")
                        for n, r in ((0, 1), (2, 0)):
                            for c in range(2):
                                ins = pe.transpose(bank[:, 8 * (n + c):8 * (n + c) + 8], ROWS[0:8, r, c * P:(c + 1) * P], IDN[0:8, 0:8])
                        ins.then_inc(*inc("tile_done", (s, "gcol")))
                pe.wait_ge(*past("nrm_rows", s))
                for hf in range(2):
                    for j in range(5):
                        if j < 4:
                            h = 4 * hf + j
                            bank = topen((s, "bc", h, 0), "D")
                            for q, r in ((0, 1), (1, 0)):
                                ins = pe.matmul(bank[:, q * S:(q + 1) * S], IDN[0:8, h:h + 1].broadcast_to([8, P]), ROWS[0:8, r, :],
                                                start=True, stop=True)
                            ins.then_inc(*inc("tile_done", (s, "bc", h, 0)))
                            bank = topen((s, "bc", h, 1), "D")
                            for q in range(2):
                                ins = pe.matmul(bank[:, q * S:(q + 1) * S], IDN[0:16, 8 * q + h:8 * q + h + 1].broadcast_to([16, P]),
                                                ROWS[0:16, 2, :], start=True, stop=True)
                            ins.then_inc(*inc("tile_done", (s, "bc", h, 1)))
                        if j >= 1:
                            h = 4 * hf + j - 1
                            pe.wait_ge(*past("kb_ready", (s, h)))
                            bank = topen((s, "la", h), "D")
                            for n, rhs in ((0, KBT[:, h % 2, :]), (2, CB[:, h, :])):
                                for c in range(2):
                                    ins = pe.matmul(bank[:, (n + c) * P:(n + c + 1) * P], CB[:, 8 + h, c * P:(c + 1) * P],
                                                    rhs[:, c * P:(c + 1) * P], start=True, stop=True)
                            ins.then_inc(*inc("tile_done", (s, "la", h)))
                    k_ = (s, hf)
                    for c in range(2):
                        pe.wait_ge(*past("u0_ready", (k_, c)))
                        bank = topen((k_, "t0", c), "A")
                        for j in range(4):
                            ins = pe.transpose(bank[:, j * P:(j + 1) * P], UU[:, c, j, :], IDN[:, :])
                        ins.then_inc(*inc("tile_done", (k_, "t0", c)))
                    for i in range(1, 7):
                        for c in range(2):
                            pe.wait_ge(*past("m_ready", (k_, i, c)))
                            pe.wait_ge(*past(*(("free_A", (k_, "t0", c)) if i == 1 else ("free_D", (k_, "dt", i - 1, c)))))
                            bank = topen((k_, "x", i, c), "A")
                            for j in range(4):
                                ins = pe.matmul(bank[:, j * P:(j + 1) * P], MM[:, c, j, :], TT[:, c, j, :], start=True, stop=True)
                            ins.then_inc(*inc("tile_done", (k_, "x", i, c)))
                        if i <= 4:
                            cols_slot((s, "ga" if hf else "gb", i - 1), XH, XL, "A")
                        for c in range(2):
                            pe.wait_ge(*past("free_A", (k_, "x", i, c)))
                            pe.wait_ge(*past(*(("u0_ready", (k_, c)) if i == 1 else ("free_D", (k_, "du", i - 1, c)))))
                            if i < 6:
                                bank = topen((k_, "dt", i, c), "D")
                                for j in range(4):
                                    ins = pe.matmul(bank[:, j * P:(j + 1) * P], UU[:, c, j, :], XX[:, c, j, :], start=True, stop=True)
                                ins.then_inc(*inc("tile_done", (k_, "dt", i, c)))
                            bank = topen((k_, "du", i, c), "D")
                            for j in range(4):
                                ins = pe.matmul(bank[:, j * P:(j + 1) * P], XX[:, c, j, :], UU[:, c, j, :], start=True, stop=True)
                            ins.then_inc(*inc("tile_done", (k_, "du", i, c)))
                    pe.wait_ge(*past("cb_ready", (s, 11)))
                    for c in range(2):
                        bank = topen((k_, "vt", c), "D")
                        for j in range(4):
                            ins = pe.transpose(bank[:, j * P:(j + 1) * P], CB[:, 16 + 4 * hf + j, c * P:(c + 1) * P], IDN[:, :])
                        ins.then_inc(*inc("tile_done", (k_, "vt", c)))
                    bank = topen((k_, "kt"), "D")
                    for j in range(4):
                        ins = pe.transpose(bank[:, j * P:(j + 1) * P], CB[:, 8 + 4 * hf + j, 0:P], IDN[:, :])
                    ins.then_inc(*inc("tile_done", (k_, "kt")))

                    def four(label, consumer, lhs, rhs):
                        bank = topen((k_, label), consumer)
                        for j in range(4):
                            ins = pe.matmul(bank[:, j * P:(j + 1) * P], lhs(j), rhs(j), start=True, stop=True)
                        ins.then_inc(*inc("tile_done", (k_, label)))

                    pe.wait_ge(*past("free_D", (k_, "vt", 0)))
                    pe.wait_ge(*past("free_D", (k_, "du", 6, 0)))
                    four("vn0", "A", lambda j: UU[:, 0, j, :], lambda j: XX[:, 0, j, :])
                    pe.wait_ge(*past("free_D", (k_, "kt")))
                    pe.wait_ge(*past("free_A", (k_, "vn0")))
                    four("s1", "A", lambda j: KTL[:, j, :], lambda j: TT[:, 0, j, :])
                    pe.wait_ge(*past("free_A", (k_, "s1")))
                    four("ks", "D", lambda j: KBG[:, j, :], lambda j: MM[:, 0, j, :])
                    pe.wait_ge(*past("free_D", (k_, "ks")))
                    pe.wait_ge(*past("free_D", (k_, "du", 6, 1)))
                    four("vn1", "A", lambda j: UU[:, 1, j, :], lambda j: XX[:, 1, j, :])
                    pe.wait_ge(*past("free_A", (k_, "vn1")))
                    for m in range(2):
                        bank = topen((k_, "od", m), "A")
                        for jj in range(2):
                            j = 2 * m + jj
                            o = bank[:, jj * S:(jj + 1) * S]
                            pe.matmul(o[:, 0:P], TT[:, 0, j, :], EA[:, 0, j, :], start=True, stop=True)
                            pe.matmul(o[:, P:S], MM[:, 0, j, :], QD[:, j, :], start=True, stop=False)
                            ins = pe.matmul(o[:, P:S], TT[:, 1, j, :], EA[:, 1, j, :], start=False, stop=True)
                        ins.then_inc(*inc("tile_done", (k_, "od", m)))
                bank = topen((s, "onrm"), "D")
                for i in range(8):
                    pe.wait_ge(*past("osq_ready", (s, i)))
                    ins = pe.matmul(bank[0:8, 0:S], ESEL[:, 15 - i:23 - i], SQ[:, i % 2, :], start=(i == 0), stop=(i == 7))
                    if i < 7:
                        ins.then_inc(*inc("osq_used", (s, i)))
                ins.then_inc(*inc("tile_done", (s, "onrm")))
                pe.wait_ge(*past("orow_ready", s))
                for m in range(4):
                    bank = topen((s, "obc", m), "D")
                    for jj in range(2):
                        ins = pe.matmul(bank[:, jj * S:(jj + 1) * S], IDN[0:8, 2 * m + jj:2 * m + jj + 1].broadcast_to([8, P]),
                                        ROWS[0:8, 5, :], start=True, stop=True)
                    ins.then_inc(*inc("tile_done", (s, "obc", m)))
                for i in range(4):
                    cols_slot((s, "bb", i), OH, OL, "D", ready=(lambda k: pe.wait_ge(*past("olb_ready", (s, k // 2)))) if i == 0 else None)
                for i in range(4):
                    pe.wait_ge(*past("ml_ready", (s, i)))
                    if i == 0:
                        y_wait(s)
                    rows_slot((s, "out", i), lambda k: XH[:, k, :], lambda k: XL[:, k, :], 2 * i, i == 0, i == 3, s)

            between(0)
            for s in range(1, n_sub):
                if s in (1, 3):
                    mlp(s)
                elif s == 2:
                    recurrence(s)
                elif is_mix(s):
                    mixer(s)
                else:
                    ffn(s)
                between(s)

        @block.scalar
        def _(act):
            split = [0]

            def hi_upto(n):
                while split[0] <= min(n, len(slots) - 1):
                    m = split[0]
                    split[0] += 1
                    act.wait_ge(*past(f"landed{m % NRAW}", m))
                    if m >= NSPL:
                        act.wait_ge(*past(*slot_end[m - NSPL]))
                    act.activation(slot_view(WHI, m, NSPL), slot_view(RAW, m, NRAW), ACT.Copy).then_inc(*inc("hi_ready", m))

            def evac(label, dst, func=ACT.Copy, src=None, **kw):
                act.activation(dst, src, func, **kw).then_inc(*inc("free_A", label))

            def tile(label):
                act.wait_ge(*past("tile_done", label))
                return TB[:, known.get(("tile", label), 0) % NTB, :]

            def pair_of(bank, p=P):
                return bank[0:p, :].rearrange("p (a b) -> p a b", a=2)

            def step(label):
                hi_upto(split_upto(label))

            def in_dma(dst, src, name, key=None):
                act.dma_start(dst, src).then_inc(*inc(name, key, 16))

            act.wait_ge(*past("free_D", ("param", "c")))
            act.activation(CC[:, :], CC[:, :], ACT.Silu).then_inc(*inc("c_ready"))
            for src, r0, blk in sorted(prm, key=lambda x: x[2]):
                in_dma(PST[r0:r0 + src.shape[0], blk, 0:src.shape[1]], src, f"param_in{blk}")

            def gate_rows(s):
                for h in range(2):
                    bank = tile(("gate", s, h))
                    if s > 0 and h == 0:
                        act.wait_ge(*past("y_free", (s - 1, 1)))
                    evac(("gate", s, h), GATE[:, h * 512:(h + 1) * 512], src=bank)

            def prep(s):
                gp, bp = (GP[:, s, :], BP[:, s, :]) if s < 4 else (LN[s - 1][2], LN[s - 1][3])
                if s < 4:
                    act.wait_ge(*past("mod_ready", s))

                def modulate(e):
                    bank = tile(("xt", s, e))
                    for kk in range(2):
                        k = 2 * e + kk
                        ins = act.activation(XTF[:, k, :], bank[:, kk * S:(kk + 1) * S], ACT.Identity, scale=gp[:, k:k + 1],
                                             bias=bp[:, k:k + 1])
                        ins.then_inc(*(inc("free_A", ("xt", s, e)) if kk else inc("xta_half", (s, e))))

                def hi(e):
                    act.wait_ge(*past("free_A" if e % 2 else "free_D", ("xt", s, e)))
                    act.activation(XH[:, 2 * e:2 * e + 2, :], XTF[:, 2 * e:2 * e + 2, :], ACT.Copy).then_inc(*inc("xh_ready", (s, e)))

                modulate(1)
                hi(0)
                hi(1)
                modulate(3)
                hi(2)
                hi(3)

            act.wait_ge(*past("const_in"))
            act.activation(AL2[:, 4:6], AL2[:, 0:2], ACT.Exp).then_inc(*inc("a_exp"))
            hi_upto(0)
            prep(0)
            for i in range(6):
                step((0, "in", i))
                dst = QT[:, 2 * i:2 * i + 2, :] if i < 4 else (KT if i == 4 else VR)[:, :, :]
                evac((0, "in", i), dst, src=pair_of(tile((0, "in", i))))
            for h in range(NH1 + 3):
                if h == 5:
                    gate_rows(0)
                if 1 <= h <= NH1:
                    g = h - 1
                    act.wait_ge(*past("neg_max", g))
                    for b in range(2):
                        act.activation(PR[:, g, b, :], PR[:, g, b, :], ACT.Exp, bias=AT1[:, 1, 2 * g + b:2 * g + b + 1],
                                           accum_out=AT1[:, 2, 2 * g + b:2 * g + b + 1]).then_inc(*inc("p_exp_part", (g, b)))
                    act.activation(AT1[:, 3, 2 * g:2 * g + 2], AT1[:, 1, 2 * g:2 * g + 2], ACT.Exp,
                                       bias=SNK[:, g:g + 1]).then_inc(*inc("p_exp", g))
                if 2 <= h < NH1 + 2:
                    act.wait_ge(*past("tile_done", ("pt", h - 2)))
                    evac(("pt", h - 2), PTB[:, h % 2, :, :], src=y_bank(h % 2).rearrange("p (a b) -> p a b", a=4))
                if h >= 4 and h % 2 == 0:
                    i = (h - 4) // 2
                    act.wait_ge(*past("tile_done", ("o", i)))
                    act.activation(OH[:, 2 * i:2 * i + 2, :], pair_of(y_bank(2 + i % 2)), ACT.Copy).then_inc(*inc("oh_ready", (0, i)))
            for i in range(4):
                step((0, "out", i))

            def hi_hidden(s, i, func, src):
                if i >= 2:
                    act.wait_ge(*past("rows_done", (s, "w2", i - 2)))
                act.activation(HH[:, i % 2, :], src[:, i % 2, :], func).then_inc(*inc("hh_ready", (s, i)))

            def mlp(s):
                n = FF1 // 256
                for i in range(n + 1):
                    if i < n:
                        step((s, "w1", i))
                        bank = tile((s, "w1", i))
                        if i >= 2:
                            act.wait_ge(*past("hid_ready", (s, i - 2)))
                        evac((s, "w1", i), RB[:, i % 2, :], ACT.Relu, bank)
                        act.wait_ge(*past("free_A", (s, "w1", i)))
                        hi_hidden(s, i, ACT.Square, RB)
                        if i == 0:
                            gate_rows(s)
                    if s == 1 and i < n:
                        bank = tile(("ext", i))
                        if i >= 4:
                            act.wait_ge(*past(f"bias_out{i % 4}", i - 4))
                        evac(("ext", i), EXS[:, i % 4, :], src=bank[:, 0:EXT])
                        act.wait_ge(*past("free_A", ("ext", i)))
                        act.dma_start(BIAS[i], EXS[:, i % 4, :]).then_inc(*inc(f"bias_out{i % 4}", i, 16))
                    if i > 0:
                        step((s, "w2", i - 1))

            def ffn(s):
                n = FF2 // 256
                for i in range(n + 1):
                    if i < n:
                        step((s, "g", i))
                        bank = tile((s, "g", i))
                        if i >= 2:
                            act.wait_ge(*past("hid_ready", (s, i - 2)))
                        evac((s, "g", i), RB[:, i % 2, :], ACT.Silu, bank)
                        step((s, "u", i))
                        act.wait_ge(*past("free_D", (s, "u", i)))
                        hi_hidden(s, i, ACT.Copy, VB)
                    if i > 0:
                        step((s, "w2", i - 1))

            def norm(s):
                act.activation(RV[:, 1, 3:4], ONES[:, 0:1], ACT.Sqrt).then_inc(*inc("sqrt_table", s))
                for t in range(NT):
                    act.wait_ge(*past("ln_recip", (s, t)))
                    act.activation(RV[:, t, 1:2], RV[:, t, 0:1], ACT.Sqrt).then_inc(*inc("ln_rstd", (s, t)))
                    if t == 0:
                        act.activation(RV[:, t, 2:3], MV[:, t, 0:1], ACT.Copy, scale=-1.0).then_inc(*inc("ln_minus", s))
                        act.wait_ge(*past("ln_minus", s))
                        act.activation(RV[:, t, 3:4], RV[:, t, 2:3], ACT.Identity, scale=RV[:, t, 1:2]).then_inc(*inc("ln_shift", s))
                        act.wait_ge(*past("ln_shift", s))
                        act.activation(XN[:, t, :], XN[:, t, :], ACT.Identity, scale=RV[:, t, 1:2], bias=RV[:, t, 3:4]).then_inc(*inc(f"xn_ready{t}", (s, t)))
                if s + 1 < n_sub:
                    prep(s + 1)

            def recurrence(s):
                for n in range(4):
                    act.wait_ge(*past(f"bias_out{n}", 12 + n))
                act.wait_ge(*past("lam_abs"))
                act.activation(RCOL[:, 4, :], RCOL[:, 3, :], ACT.Exp, scale=-1.0).then_inc(*inc("lam_exp"))
                for i in range(8):
                    step((s, "gt", i))
                    evac((s, "gt", i), GG[:, 2 * i:2 * i + 2, :], ACT.Gelu_apprx_tanh, pair_of(tile((s, "gt", i)), RB_W))
                    if i == 0:
                        gate_rows(s)
                for i in range(12):
                    if i < 8:
                        step((s, "in", i))
                        bank = tile((s, "in", i))
                        if i == 0:
                            act.wait_ge(*past("xp_zero"))
                        if i >= 2:
                            act.wait_ge(*past("xc_ready", 2 * i - 3))
                        evac((s, "in", i), XP[:, i % 2, :, 2:2 + S], src=pair_of(bank, RB_W))
                    g = i - 1
                    if 0 <= g < 8:
                        if g == 0:
                            act.wait_ge(*past("decay_cols"))
                        if g >= 2:
                            act.wait_ge(*past("yl", g - 2))
                        for b in range(2):
                            for d in range(2):
                                bank = tile(("gate", g, b, d))
                                ch = 16 * d + 2 * g + b
                                act.activation(RR[:, g % 2, d, b, :], bank[0:RB_W, 0:S], ACT.Tanh, scale=0.5,
                                                   bias=RC2[:, ch:ch + 1]).then_inc(*inc("rnn_r", (g, b, d)))
                                evac(("gate", g, b, d), RI[:, g % 2, d, b, :], ACT.Tanh, bank[0:RB_W, S:2 * S], scale=0.5,
                                     bias=RC2[:, 32 + ch:33 + ch])
                    if 0 <= g - 1 < 8:
                        if g - 1 >= 4:
                            act.wait_ge(*past("rows_done", (s, "out", g - 5)))
                        act.wait_ge(*past("rnn_v", g - 1))
                        act.activation(YH[:, (g - 1) % 4, :, :], RR[:, (g - 1) % 2, 0, :, :], ACT.Copy).then_inc(*inc("yh", g - 1))
                    if i >= 4:
                        step((s, "out", i - 4))
                    if 0 <= g < 8:
                        for d in range(2):
                            for b in range(2):
                                ch = 16 * d + 2 * g + b
                                a_, r_ = RA[:, g % 2, d, b, :], RR[:, g % 2, d, b, :]
                                act.wait_ge(*past("rnn_r", (g, b, d)))
                                act.activation(a_, r_, ACT.Exp, scale=RCOL[:, 0, ch:ch + 1], bias=RCOL[:, 0, ch:ch + 1]).then_inc(*inc("rnn_a", (g, d, b)))
                                act.activation(r_, r_, ACT.Tanh, scale=RCOL[:, 1, ch:ch + 1], bias=RCOL[:, 1, ch:ch + 1]).then_inc(*inc("rnn_th", (g, d, b)))
                        act.wait_ge(*past("rnn_one", (g, 1)))
                        act.activation(RR[:, g % 2, :, :, :], RR[:, g % 2, :, :, :], ACT.Sqrt).then_inc(*inc("rnn_mult", g))

            def mixer(s):
                l = (s - 4) // 3
                for i in range(4):
                    step((s, "qa", i))
                    evac((s, "qa", i), QA[:, 2 * i:2 * i + 2, :], src=pair_of(tile((s, "qa", i))))
                for name, dst in (("ka", KA), ("va", VA)):
                    step((s, name, 0))
                    evac((s, name, 0), dst[:, :, :], src=pair_of(tile((s, name, 0))))
                step((s, "bd", 0))
                bank = tile((s, "bd", 0))
                act.activation(ROWS[0:8, 0, :], bank[0:8, 0:S], ACT.Sigmoid).then_inc(*inc("beta_rows", s))
                evac((s, "bd", 0), ROWS[0:8, 3, :], ACT.Identity, bank[0:8, S:2 * S], bias=AL2[:, 2 + l:3 + l])
                act.wait_ge(*past("cin_zero", s))
                act.wait_ge(*past("xs_ready", (s - 1, 1)))
                for j in range(19):
                    if j < 12:
                        step((s, "cv", j))
                        bank = tile((s, "cv", j))
                        if j >= 2:
                            act.wait_ge(*past("conv_done", (s, j - 2)))
                        evac((s, "cv", j), CIN[:, j % 2, :, 3:3 + S], src=pair_of(bank))
                        act.wait_ge(*past("free_A", (s, "cv", j)))
                        for jj in range(2):
                            ct = 2 * j + jj
                            act.activation(CB[:, ct, :], CIN[:, j % 2, jj, 0:S], ACT.Identity, scale=CW2[:, l, ct:ct + 1]).then_inc(*inc("tap0", (s, j)))
                    elif j < 16:
                        step((s, "z", j - 12))
                        bank = tile((s, "z", j - 12))
                        act.activation(ZT[:, 2 * (j - 12):2 * (j - 12) + 2, :], pair_of(bank), ACT.Copy, scale=0.5).then_inc(*inc("z_half", (s, j)))
                        act.wait_ge(*past("cb_ready", (s, j - 2)))
                        act.activation(TH[:, j % 2, :, :], pair_of(bank), ACT.Tanh, scale=0.5).then_inc(*inc("free_A", (s, "z", j - 12)))
                    if j == 0:
                        act.wait_ge(*past("dt_abs", s))
                        act.activation(ROWS[0:8, 5, :], ROWS[0:8, 4, :], ACT.Exp, scale=-1.0).then_inc(*inc("dt_exp", s))
                    if 1 <= j <= 12:
                        u = j - 1
                        act.wait_ge(*past("conv_done", (s, u)))
                        if u >= 2:
                            act.wait_ge(*past("cb_ready", (s, u - 2)))
                        act.activation(TH[:, u % 2, :, :], CB[:, 2 * u:2 * u + 2, :], ACT.Tanh).then_inc(*inc("tanh_ready", (s, u)))
                    if 1 <= j <= 16:
                        t, hh = divmod(j - 1, 2)
                        head = (2 * (t // 4) + hh) * 4 + t % 4
                        r = (j - 1) % 3
                        act.wait_ge(*past("neg_max_a", (s, j - 1)))
                        for b, (lo, hi) in enumerate(((0, P), (P, 384))):
                            act.activation(PA[:, r, lo:hi], PA[:, r, lo:hi], ACT.Exp, bias=A2S[:, r, b:b + 1],
                                               accum_out=A2S[:, r, 2 + b:3 + b]).then_inc(*inc("pa_exp_part", (s, j - 1, b)))
                        act.activation(A2S[:, r, 4:6], A2S[:, r, 0:2], ACT.Exp, bias=SNK2[:, l, head:head + 1]).then_inc(*inc("pa_exp", (s, j - 1)))
                    if 2 <= j < 18:
                        act.wait_ge(*past("tile_done", (s, "pt", j - 2)))
                        evac((s, "pt", j - 2), PTA[:, j % 2, :], src=y_bank(j % 2)[:, 0:384])
                    if j >= 4 and j % 2 == 0:
                        t = (j - 4) // 2
                        act.wait_ge(*past("tile_done", (s, "oa", t)))
                        act.activation(OH[:, t, :], y_bank(2 + t % 2)[:, 0:S], ACT.Copy).then_inc(*inc("oh_ready", (s, t)))
                for i in range(4):
                    step((s, "ba", i))
                    if i == 3:
                        act.wait_ge(*past("nrm_recip", s))
                        act.activation(ROWS[0:16, 2, :], ROWS[0:16, 4, :], ACT.Sqrt, scale=NSC[:, 0:1]).then_inc(*inc("nrm_rows", s))
                    evac((s, "ba", i), M1[:, 2 * i:2 * i + 2, :], src=pair_of(tile((s, "ba", i))))
                    for u in range(6 * i, min(6 * i + 6, 16)):
                        if u >= 2:
                            act.wait_ge(*past("sq_used", (s, u - 2)))
                        act.wait_ge(*past("cb_ready", (s, u // 2)))
                        act.activation(SQ[:, u % 2, :], CB[:, u, :], ACT.Square).then_inc(*inc("sq_ready", (s, u)))
                for hf in range(2):
                    k_ = (s, hf)
                    for j in range(4):
                        h = 4 * hf + j
                        bank = tile((s, "bc", h, 0))
                        if j >= 2:
                            act.wait_ge(*past("kb_ready", (s, h - 2)))
                        act.wait_ge(*past("e_raw", (s, h)))
                        act.activation(EG[:, h % 2, :], bank[:, 0:S], ACT.Exp).then_inc(*inc("eg_ready", (s, h)))
                        act.activation(EA[:, :, j, :], EA[:, :, j, :], ACT.Exp).then_inc(*inc("e_ready", (s, h)))
                        act.activation(GLT[:, 1, h:h + 1], GCOL[:, 0, h:h + 1], ACT.Exp, scale=-1.0,
                                           bias=GLT[:, 0, h:h + 1]).then_inc(*inc("tail_ready", (s, h)))

                    def four(label, dst):
                        bank = tile(label)
                        evac(label, dst, src=bank.rearrange("p (a b) -> p a b", a=4))

                    for c in range(2):
                        four((k_, "t0", c), TT[:, c, :, :])
                    for i in range(1, 7):
                        for c in range(2):
                            four((k_, "x", i, c), XX[:, c, :, :])
                        if hf == 1 and i <= 4:
                            step((s, "ga", i - 1))
                            bank = tile((s, "ga", i - 1))
                            if i > 1:
                                act.wait_ge(*past("gate_a_used", (s, i - 2)))
                            evac((s, "ga", i - 1), GT[:, :, :], ACT.Sigmoid, pair_of(bank))
                        if hf == 0 and i <= 4:
                            step((s, "gb", i - 1))
                            evac((s, "gb", i - 1), GBT[:, 2 * i - 2:2 * i, :], ACT.Sigmoid, pair_of(tile((s, "gb", i - 1))))
                    four((k_, "vn0"), TT[:, 0, :, :])
                    four((k_, "s1"), MM[:, 0, :, :])
                    four((k_, "vn1"), TT[:, 1, :, :])
                    for m in range(2):
                        q0 = 4 * hf + 2 * m
                        evac((k_, "od", m), CB[:, q0:q0 + 2, :], src=pair_of(tile((k_, "od", m))))
                for i in range(8):
                    if i >= 2:
                        act.wait_ge(*past("osq_used", (s, i - 2)))
                    act.wait_ge(*past("free_A", ((s, i // 4), "od", i % 4 // 2)))
                    act.activation(SQ[:, i % 2, :], CB[:, i, :], ACT.Square).then_inc(*inc("osq_ready", (s, i)))
                act.wait_ge(*past("onrm_recip", s))
                act.activation(ROWS[0:8, 5, :], ROWS[0:8, 3, :], ACT.Sqrt).then_inc(*inc("orow_ready", s))
                for m in range(4):
                    act.wait_ge(*past("ov_ready", (s, m)))
                    act.activation(OH[:, 2 * m:2 * m + 2, :], CB[:, 2 * m:2 * m + 2, :], ACT.Copy).then_inc(*inc("ohb_ready", (s, m)))
                for i in range(4):
                    step((s, "bb", i))
                    act.wait_ge(*past("mv_ready", (s, i)))
                    act.activation(XH[:, 2 * i:2 * i + 2, :], CB[:, 2 * i:2 * i + 2, :], ACT.Copy).then_inc(*inc("mh_ready", (s, i)))
                for i in range(4):
                    step((s, "out", i))

            norm(0)
            for s in range(1, n_sub):
                if s in (1, 3):
                    mlp(s)
                elif s == 2:
                    recurrence(s)
                elif is_mix(s):
                    mixer(s)
                else:
                    ffn(s)
                norm(s)

        @block.vector
        def _(dve):
            split = [0]

            def lo_upto(n):
                while split[0] <= min(n, len(slots) - 1):
                    m = split[0]
                    split[0] += 1
                    dve.wait_ge(*past("hi_ready", m))
                    dve.tensor_tensor(slot_view(WLO, m, NSPL), slot_view(RAW, m, NRAW),
                                          slot_view(WHI, m, NSPL).bitcast(F32), ALU.subtract).then_inc(*inc("lo_ready", m))

            def step(label):
                lo_upto(split_upto(label))

            def tile(label):
                dve.wait_ge(*past("tile_done", label))
                return TB[:, known.get(("tile", label), 0) % NTB, :]

            def pair_of(bank, p=P):
                return bank[0:p, :].rearrange("p (a b) -> p a b", a=2)

            def chain(ins):
                link(dve, ins, "dve_chain")

            def params(n):
                rows, width, dsts = blocks[n]
                bank = tile(("param", n))
                at = 0
                for q, dst in enumerate(dsts):
                    w = dst.shape[1]
                    ins = dve.tensor_copy(dst, bank[0:width, at:at + w])
                    at += w
                    if q < len(dsts) - 1:
                        chain(ins)
                ins.then_inc(*inc("free_D", ("param", n)))
                dve.wait_ge(*past("free_D", ("param", n)))
                if n == 7:
                    chain(dve.tensor_scalar(RC2[:, 0:64], RC2[:, 0:64], 0.5, None, ALU.mult))
                if n in (3, 4):
                    chain(dve.tensor_scalar(dsts[0], dsts[0], 0.5, None, ALU.mult))

            chunk = [0]

            def ada_upto(q):
                while chunk[0] <= min(q, n_ada - 1):
                    m = chunk[0]
                    chunk[0] += 1
                    t, kc = divmod(m, KC)
                    dve.wait_ge(*past(f"ada_in{m % NADR}" if m < 20 else f"ada_next{m % NADR}", m))
                    if kc == 0:
                        if t >= 3:
                            dve.wait_ge(*past("tile_done", ("ada", t - 3)))
                        ins = dve.tensor_scalar(ACC[:, t % 3, :], ADR[:, m % NADR, :], CC[:, kc:kc + 1], None, ALU.mult)
                    else:
                        dve.wait_ge(*past("ada_used", m - 1))
                        ins = dve.scalar_tensor_tensor(ACC[:, t % 3, :], ADR[:, m % NADR, :], CC[:, kc:kc + 1], ACC[:, t % 3, :],
                                                       ALU.mult, ALU.add)
                    ins.then_inc(*inc("ada_used", m))

            bank = tile(("param", "c"))
            dve.tensor_copy(CC[:, :], bank[:, 0:8]).then_inc(*inc("free_D", ("param", "c")))
            dve.wait_ge(*past("free_D", ("param", "c")))
            dve.wait_ge(*past("c_ready"))
            ada_upto(11)
            for n in range(len(blocks)):
                params(n)
            ada_upto(15)

            def modulation(t):
                if 8 * t >= n_ada:
                    return
                s, third = divmod(t, 3)
                bank = tile(("ada", t))
                m = MOD[:, s, 8 * third:8 * third + 8]
                dve.tensor_tensor(m, bank[:, 0:8], ADB[:, 8 * t:8 * t + 8], ALU.add).then_inc(*inc("free_D", ("ada", t)))
                dve.wait_ge(*past("free_D", ("ada", t)))
                if third == 0:
                    return
                ins = dve.tensor_scalar(m, m, 1.0, None, ALU.add)
                if third == 2:
                    ins.then_inc(*inc("gate_cols", s))
                    dve.wait_ge(*past("gate_cols", s))
                    return
                chain(ins)
                if s == 0:
                    chain(dve.tensor_copy(GP[:, s, :], MOD[:, s, 8:16]))
                    dve.tensor_copy(BP[:, s, :], MOD[:, s, 0:8]).then_inc(*inc("mod_ready", s))
                else:
                    g, b = LN[s - 1][2], LN[s - 1][3]
                    chain(dve.tensor_tensor(GP[:, s, :], MOD[:, s, 8:16], g, ALU.mult))
                    chain(dve.tensor_tensor(BP[:, s, :], MOD[:, s, 8:16], b, ALU.mult))
                    dve.tensor_tensor(BP[:, s, :], BP[:, s, :], MOD[:, s, 0:8], ALU.add).then_inc(*inc("mod_ready", s))
                dve.wait_ge(*past("mod_ready", s))

            def prep(s):
                def lo(e):
                    dve.wait_ge(*past("xh_ready", (s, e)))
                    dve.tensor_tensor(XL[:, 2 * e:2 * e + 2, :], XTF[:, 2 * e:2 * e + 2, :],
                                          XH[:, 2 * e:2 * e + 2, :].bitcast(F32), ALU.subtract).then_inc(*inc("xl_ready", (s, e)))

                gp, bp = (GP[:, s, :], BP[:, s, :]) if s < 4 else (LN[s - 1][2], LN[s - 1][3])
                for e in (0, 2):
                    bank = tile(("xt", s, e))
                    for kk in range(2):
                        k = 2 * e + kk
                        ins = dve.tensor_scalar(XTF[:, k, :], bank[:, kk * S:(kk + 1) * S], gp[:, k:k + 1], bp[:, k:k + 1],
                                                ALU.mult, ALU.add)
                        if kk == 0:
                            ins.then_inc(*inc("xtf_half", (s, e)))
                    ins.then_inc(*inc("free_D", ("xt", s, e)))
                for e in range(4):
                    lo(e)

            modulation(0)
            lo_upto(0)
            modulation(1)
            prep(0)
            for i in range(6):
                step((0, "in", i))
                if i > 0:
                    r = i - 1
                    bank = tile(("rot", r))
                    src = (QT[0:32, 2 * r:2 * r + 2, :] if r < 4 else KT[0:32, :, :]).rearrange("p a b -> p (a b)")
                    dve.tensor_tensor(RTMP[:, r % 2, :], bank[0:32, :], SIN[:, :], ALU.mult).then_inc(*inc("free_D", ("rot", r)))
                    chain(dve.tensor_tensor(src, src, COS[:, :], ALU.mult))
                    dve.wait_ge(*past("free_D", ("rot", r)))
                    dve.tensor_tensor(src, src, RTMP[:, r % 2, :], ALU.add).then_inc(*inc("rope_ready", r))
                ada_upto(17 + 2 * i)
            def norm1(h):
                dve.wait_ge(*past("p_exp", h))
                w = slice(2 * h, 2 * h + 2)
                chain(dve.tensor_tensor(AT1[:, 4, w], AT1[:, 2, w], AT1[:, 3, w], ALU.add))
                chain(dve.reciprocal(AT1[:, 5, w], AT1[:, 4, w]))
                for b in range(2):
                    dve.tensor_scalar(PR[:, h, b, :], PR[:, h, b, :], AT1[:, 5, 2 * h + b:2 * h + b + 1], None, ALU.mult).then_inc(*inc("probs_ready", h))

            for h in range(NH1 + 3):
                if h < NH1:
                    bank = tile(("sc", h))
                    w = slice(2 * h, 2 * h + 2)
                    dve.scalar_tensor_tensor(PR[:, h, :, :].rearrange("p a b -> p (a b)"), bank, HD1 ** -0.5, WIN[:, :],
                                                 ALU.mult, ALU.add).then_inc(*inc("free_D", ("sc", h)))
                    dve.wait_ge(*past("free_D", ("sc", h)))
                    chain(dve.tensor_reduce(AT1[:, 0, w], PR[:, h, :, :], AX.X, ALU.max))
                    dve.tensor_scalar(AT1[:, 1, w], AT1[:, 0, w], SNK[:, h:h + 1], -1.0, ALU.max, ALU.mult).then_inc(*inc("neg_max", h))
                if 1 <= h <= NH1:
                    norm1(h - 1)
                if h >= 4 and h % 2 == 0:
                    i = (h - 4) // 2
                    dve.wait_ge(*past("oh_ready", (0, i)))
                    dve.tensor_tensor(OL[:, 2 * i:2 * i + 2, :], pair_of(y_bank(2 + i % 2)), OH[:, 2 * i:2 * i + 2, :].bitcast(F32),
                                          ALU.subtract).then_inc(*inc("free_D", ("o", i)))
                if h in (2, 3, 7):
                    modulation({2: 2, 3: 3, 7: 4}[h])
                ada_upto(29 + 2 * h)
            for i in range(4):
                step((0, "out", i))
                if i == 1:
                    modulation(5)
                ada_upto(50 + i)

            def norm(s):
                for t in range(NT):
                    dve.wait_ge(*past(*(("y_half", s) if t == 0 else y_end[s])))
                    dve.wait_ge(*past("xs_ready", (s - 1, t)))
                    if s < 4:
                        if t == 0:
                            dve.wait_ge(*past("free_A", ("gate", s, 1)))
                        dve.tensor_tensor(XN[:, t, :], Y[:, t, :], GATE[:, :], ALU.mult).then_inc(*inc("y_free", (s, t)))
                        dve.wait_ge(*past("y_free", (s, t)))
                        chain(dve.tensor_tensor(XN[:, t, :], XN[:, t, :], XS[:, t, :], ALU.add))
                    else:
                        dve.scalar_tensor_tensor(XN[:, t, :], Y[:, t, :], 1.0 if is_mix(s) else 0.5, XS[:, t, :],
                                                     ALU.mult, ALU.add).then_inc(*inc("y_free", (s, t)))
                        dve.wait_ge(*past("y_free", (s, t)))
                    for h in range(2):
                        ins = dve.bn_stats(ST[:, t, h, :], XN[:, t, h * 512:(h + 1) * 512])
                    chain(ins)
                    chain(dve.bn_aggr(MV[:, t, :], ST[:, t, :, :].rearrange("p a b -> p (a b)")))
                    chain(dve.tensor_scalar(RV[:, t, 0:1], MV[:, t, 1:2], LN_EPS, None, ALU.add))
                    dve.reciprocal(RV[:, t, 0:1], RV[:, t, 0:1]).then_inc(*inc("ln_recip", (s, t)))
                dve.wait_ge(*past("ln_rstd", (s, 1)))
                dve.tensor_scalar(XN[:, 1, :], XN[:, 1, :], MV[:, 1, 0:1], RV[:, 1, 1:2], ALU.subtract, ALU.mult).then_inc(*inc("xn_ready1", (s, 1)))
                if s + 1 < n_sub:
                    prep(s + 1)
                else:
                    dve.wait_ge(*past("gb_in", s))
                    for t in range(NT):
                        dve.wait_ge(*past(f"xn_ready{t}", (s, t)))
                        chain(dve.tensor_tensor(XN[:, t, :], XN[:, t, :], GB[:, 0, :], ALU.mult))
                        dve.tensor_tensor(XN[:, t, :], XN[:, t, :], GB[:, 1, :], ALU.add).then_inc(*inc("out_rows", t))

            def lo_hidden(s, i):
                dve.wait_ge(*past("hh_ready", (s, i)))
                dve.tensor_tensor(HL[:, i % 2, :], VB[:, i % 2, :], HH[:, i % 2, :].bitcast(F32), ALU.subtract).then_inc(*inc("hid_ready", (s, i)))

            def mlp(s):
                n = FF1 // 256
                for i in range(n + 1):
                    if i < n:
                        step((s, "w1", i))
                        dve.wait_ge(*past("free_A", (s, "w1", i)))
                        dve.tensor_tensor(VB[:, i % 2, :], RB[:, i % 2, :], RB[:, i % 2, :], ALU.mult).then_inc(*inc("hid_v", (s, i)))
                        dve.wait_ge(*past("hid_v", (s, i)))
                        lo_hidden(s, i)
                    if s == 1 and i in (2, 4, 8, 11, 14, 16):
                        modulation((2, 4, 8, 11, 14, 16).index(i) + 6)
                    if s == 1:
                        ada_upto(58 + 5 * i // 2)
                    if i > 0:
                        step((s, "w2", i - 1))

            def ffn(s):
                n = FF2 // 256
                for i in range(n + 1):
                    if i < n:
                        step((s, "g", i))
                        step((s, "u", i))
                        bank = tile((s, "u", i))
                        dve.wait_ge(*past("free_A", (s, "g", i)))
                        dve.tensor_tensor(VB[:, i % 2, :], RB[:, i % 2, :], bank, ALU.mult).then_inc(*inc("free_D", (s, "u", i)))
                        lo_hidden(s, i)
                    if i > 0:
                        step((s, "w2", i - 1))

            def softplus(x, ax, e, t0, t1, exp_wait):
                exp_wait()
                chain(dve.tensor_scalar(t0, e, 2.0, None, ALU.add))
                chain(dve.reciprocal(t0, t0))
                chain(dve.tensor_tensor(e, e, t0, ALU.mult))
                chain(dve.tensor_tensor(t1, e, e, ALU.mult))
                chain(dve.tensor_scalar(t0, t1, 1.0 / 17, None, ALU.mult))
                for d in (15, 13, 11, 9, 7, 5, 3):
                    chain(dve.scalar_tensor_tensor(t0, t0, 1.0 / d, t1, ALU.add, ALU.mult))
                chain(dve.scalar_tensor_tensor(t0, t0, 1.0, e, ALU.add, ALU.mult))
                chain(dve.tensor_scalar(x, x, 0.0, 0.5, ALU.max, ALU.mult))
                chain(dve.tensor_tensor(t0, t0, x, ALU.add))
                chain(dve.tensor_scalar(t0, t0, 2.0, None, ALU.mult))

            def recurrence(s):
                x, ax, e, t0, t1 = (RCOL[:, q, :] for q in range(2, 7))
                chain(dve.tensor_scalar(x, RC2[:, 64:96], -1.0, None, ALU.mult))
                dve.tensor_tensor(ax, x, RC2[:, 64:96], ALU.max).then_inc(*inc("lam_abs"))
                softplus(x, ax, e, t0, t1, lambda: dve.wait_ge(*past("lam_exp")))
                chain(dve.tensor_scalar(RCOL[:, 0, :], t0, -4.0, None, ALU.mult))
                dve.tensor_scalar(RCOL[:, 1, :], t0, 4.0, None, ALU.mult).then_inc(*inc("decay_cols"))
                for i in range(8):
                    step((s, "gt", i))
                for i in range(12):
                    if i < 8:
                        step((s, "in", i))
                        dve.wait_ge(*past("free_A", (s, "in", i)))
                        for jj in range(2):
                            ct = 2 * i + jj
                            xin = XP[:, i % 2, jj, :]
                            chain(dve.tensor_scalar(XC[:, ct, :], xin[:, 0:S], RC1[:, ct:ct + 1], RC1[:, 64 + ct:65 + ct],
                                                    ALU.mult, ALU.add))
                            for j in range(1, 4):
                                ins = dve.scalar_tensor_tensor(XC[:, ct, :], xin[:, j:j + S], RC1[:, 16 * j + ct:16 * j + ct + 1],
                                                               XC[:, ct, :], ALU.mult, ALU.add)
                                if j < 3:
                                    chain(ins)
                            ins.then_inc(*inc("xc_ready", ct))
                    g = i - 1
                    if i >= 4:
                        step((s, "out", i - 4))
                    if 0 <= g - 1 < 8:
                        dve.wait_ge(*past("yh", g - 1))
                        dve.tensor_tensor(YL[:, (g - 1) % 4, :, :], RR[:, (g - 1) % 2, 0, :, :],
                                              YH[:, (g - 1) % 4, :, :].bitcast(F32), ALU.subtract).then_inc(*inc("yl", g - 1))
                    if 0 <= g < 8:
                        r = RR[:, g % 2]
                        for d in range(2):
                            dve.wait_ge(*past("rnn_a", (g, d, 1)))
                            chain(dve.tensor_tensor(RTM[:, d, :, :], RA[:, g % 2, d, :, :], RA[:, g % 2, d, :, :], ALU.mult))
                            dve.wait_ge(*past("rnn_th", (g, d, 1)))
                            dve.scalar_tensor_tensor(r[:, d, :, :], RTM[:, d, :, :], 1.0, r[:, d, :, :], ALU.add, ALU.mult).then_inc(*inc("rnn_one", (g, d)))
                        dve.wait_ge(*past("rnn_mult", g))
                        dve.wait_ge(*past("rnn_ix", g))
                        chain(dve.tensor_tensor(RI[:, g % 2, :, :, :], RI[:, g % 2, :, :, :], r, ALU.mult))
                        for d in range(2):
                            for b in range(2):
                                a_, u_, o_ = RA[:, g % 2, d, b, :], RI[:, g % 2, d, b, :], RR[:, g % 2, d, b, :]
                                if d == 1:
                                    a_, u_, o_ = a_[:, ::-1], u_[:, ::-1], o_[:, ::-1]
                                ins = dve.tensor_tensor_scan(o_, a_, u_, 0.0, ALU.mult, ALU.add)
                                ins.then_inc(*inc("rnn_scan", (g, d, b)))
                        dve.wait_ge(*past("rnn_scan", (g, 1, 1)))
                        chain(dve.tensor_tensor(r[:, 0, :, :], r[:, 0, :, :], r[:, 1, :, :], ALU.add))
                        dve.scalar_tensor_tensor(r[:, 0, :, :], r[:, 0, :, :], 0.5, GG[:, 2 * g:2 * g + 2, :], ALU.mult,
                                                     ALU.mult).then_inc(*inc("rnn_v", g))

            def mixer(s):
                l = (s - 4) // 3
                for i in range(4):
                    step((s, "qa", i))
                step((s, "ka", 0))
                step((s, "va", 0))
                step((s, "bd", 0))
                dve.wait_ge(*past("free_A", (s, "bd", 0)))
                x, t0, e, t1 = ROWS[0:8, 3, :], ROWS[0:8, 4, :], ROWS[0:8, 5, :], ROWS[0:8, 1, :]
                dve.scalar_tensor_tensor(t0, x, -1.0, x, ALU.mult, ALU.max).then_inc(*inc("dt_abs", s))

                def norm_a(j):
                    r = j % 3
                    dve.wait_ge(*past("pa_exp", (s, j)))
                    chain(dve.tensor_tensor(A2S[:, r, 4:6], A2S[:, r, 2:4], A2S[:, r, 4:6], ALU.add))
                    chain(dve.reciprocal(A2S[:, r, 6:8], A2S[:, r, 4:6]))
                    for b, (lo, hi) in enumerate(((0, P), (P, 384))):
                        dve.tensor_scalar(PA[:, r, lo:hi], PA[:, r, lo:hi], A2S[:, r, 6 + b:7 + b], None, ALU.mult).then_inc(*inc("pa_ready", (s, j)))

                for j in range(19):
                    if j < 12:
                        step((s, "cv", j))
                        dve.wait_ge(*past("tap0", (s, j)))
                        for tap in range(1, 4):
                            for jj in range(2):
                                ct = 2 * j + jj
                                w = CW2[:, l, 24 * tap + ct:24 * tap + ct + 1]
                                ins = dve.scalar_tensor_tensor(CB[:, ct, :], CIN[:, j % 2, jj, tap:tap + S], w, CB[:, ct, :],
                                                               ALU.mult, ALU.add)
                                if tap < 3 or jj == 0:
                                    ins.then_inc(*inc("conv_tap", (s, j, tap, jj)))
                            if tap < 3:
                                dve.wait_ge(*past("conv_tap", (s, j, tap, 1)))
                        ins.then_inc(*inc("conv_done", (s, j)))
                    elif j < 16:
                        step((s, "z", j - 12))
                    if j < 16:
                        t, hh = divmod(j, 2)
                        head = (2 * (t // 4) + hh) * 4 + t % 4
                        r = j % 3
                        bank = tile((s, "sc", j))
                        dve.wait_ge(*past(f"bias_in{r}", (s, j)))
                        if j >= 3:
                            dve.wait_ge(*past("tile_done", (s, "pt", j - 3)))
                        dve.scalar_tensor_tensor(PA[:, r, 0:P], bank[:, 0:P], 0.125, BI[:, r, P:S], ALU.mult, ALU.add).then_inc(*inc("pa_part", (s, j)))
                        dve.scalar_tensor_tensor(PA[:, r, P:384], bank[:, P:384], 0.125, BI[:, r, :], ALU.mult, ALU.add).then_inc(*inc("free_D", (s, "sc", j)))
                        dve.wait_ge(*past("pa_part", (s, j)))
                        chain(dve.tensor_reduce(A2S[:, r, 6:7], PA[:, r, 0:P], AX.X, ALU.max))
                        dve.wait_ge(*past("free_D", (s, "sc", j)))
                        chain(dve.tensor_reduce(A2S[:, r, 7:8], PA[:, r, P:384], AX.X, ALU.max))
                        dve.tensor_scalar(A2S[:, r, 0:2], A2S[:, r, 6:8], SNK2[:, l, head:head + 1], -1.0, ALU.max, ALU.mult).then_inc(*inc("neg_max_a", (s, j)))
                    if 1 <= j <= 16:
                        norm_a(j - 1)
                    if j >= 4 and j % 2 == 0:
                        t = (j - 4) // 2
                        bank = y_bank(2 + t % 2)
                        dve.wait_ge(*past("oh_ready", (s, t)))
                        dve.tensor_tensor(OL[:, t, :], bank[:, 0:S], OH[:, t, :].bitcast(F32), ALU.subtract).then_inc(*inc("free_D", (s, "oa", t)))
                softplus(x, None, e, t0, t1, lambda: dve.wait_ge(*past("dt_exp", s)))
                dve.wait_ge(*past("a_exp"))
                chain(dve.tensor_scalar(t0, t0, AL2[:, 4 + l:5 + l], -1.0, ALU.mult, ALU.mult))
                for c in range(2):
                    w = slice(c * P, (c + 1) * P)
                    dve.tensor_tensor_scan(ROWS[0:8, 1, w], ONES[0:8, 0:P], ROWS[0:8, 4, w], 0.0, ALU.mult, ALU.add).then_inc(*inc("g_rows", s))
                for i in range(3):
                    step((s, "ba", i))
                bank = tile((s, "nrm"))
                dve.tensor_scalar(ROWS[0:16, 4, :], bank[0:16, 0:S], NORM_EPS, None, ALU.add).then_inc(*inc("free_D", (s, "nrm")))
                dve.wait_ge(*past("free_D", (s, "nrm")))
                dve.reciprocal(ROWS[0:16, 4, :], ROWS[0:16, 4, :]).then_inc(*inc("nrm_recip", s))
                bank = tile((s, "gcol"))
                dve.tensor_copy(GCOL[:, :, :], bank[:, 0:32].rearrange("p (a b) -> p a b", a=4)).then_inc(*inc("free_D", (s, "gcol")))
                step((s, "ba", 3))
                for hf in range(2):
                    k_ = (s, hf)
                    for j in range(5):
                        if j < 4:
                            h = 4 * hf + j
                            b0 = tile((s, "bc", h, 0))
                            dve.tensor_copy(GLT[:, 0, h:h + 1], b0[:, P - 1:P]).then_inc(*inc("gl_part", (s, h)))
                            for c in range(2):
                                dve.wait_ge(*past("free_D", (s, "gcol")))
                                dve.scalar_tensor_tensor(EA[:, c, j, :], b0[:, c * P:(c + 1) * P], GCOL[:, c, h:h + 1], TRI[:, :],
                                                             ALU.subtract, ALU.add).then_inc(*inc("e_raw", (s, h)))
                            b1 = tile((s, "bc", h, 1))
                            k, q = CB[:, 8 + h, :], CB[:, h, :]
                            chain(dve.tensor_tensor(k, k, b1[:, S:2 * S], ALU.mult))
                            dve.tensor_tensor(q, q, b1[:, 0:S], ALU.mult).then_inc(*inc("free_D", (s, "bc", h, 1)))
                            dve.wait_ge(*past("eg_ready", (s, h)))
                            dve.tensor_tensor(KBT[:, h % 2, :], k, b0[:, S:2 * S], ALU.mult).then_inc(*inc("free_D", (s, "bc", h, 0)))
                            dve.wait_ge(*past("free_D", (s, "bc", h, 0)))
                            chain(dve.tensor_tensor(KBG[:, j, :], KBT[:, h % 2, P:S], EG[:, h % 2, P:S], ALU.mult))
                            dve.tensor_tensor(QD[:, j, :], q[:, P:S], EG[:, h % 2, P:S], ALU.mult).then_inc(*inc("kb_ready", (s, h)))
                        if j >= 1:
                            h = 4 * hf + j - 1
                            bank = tile((s, "la", h))
                            dve.wait_ge(*past("e_ready", (s, h)))
                            dve.tensor_tensor(LT[:, :, h % 4, :], pair_of(bank[:, 0:S]), EA[:, :, h % 4, :], ALU.mult).then_inc(*inc("lt_ready", (s, h)))
                            dve.wait_ge(*past("lt_ready", (s, h)))
                            dve.tensor_tensor(EA[:, :, h % 4, :], pair_of(bank[:, S:2 * S]), EA[:, :, h % 4, :], ALU.mult).then_inc(*inc("free_D", (s, "la", h)))
                    for c in range(2):
                        dve.wait_ge(*past("m_ready", (k_, 0, c)))
                        eye = IDN[:, :].rearrange("p (a b) -> p a b", a=1).broadcast_to([P, 4, P])
                        dve.tensor_tensor(UU[:, c, :, :], eye, MM[:, c, :, :], ALU.subtract).then_inc(*inc("u0_ready", (k_, c)))
                    for i in range(1, 7):
                        if i <= 4:
                            step((s, "ga" if hf else "gb", i - 1))
                        if hf == 1 and 2 <= i <= 5:
                            dve.wait_ge(*past("free_A", (s, "ga", i - 2)))
                            m = M1[:, 2 * i - 4:2 * i - 2, :]
                            dve.tensor_tensor(m, m, GT[:, :, :], ALU.mult).then_inc(*inc("gate_a_used", (s, i - 2)))
                        for c in range(2):
                            for kind, dst in (("dt", TT), ("du", UU)):
                                if kind == "dt" and i == 6:
                                    continue
                                bank = tile((k_, kind, i, c))
                                m = dst[:, c, :, :]
                                if i == 1:
                                    dve.wait_ge(*past("free_A", (k_, "t0", c)))
                                dve.tensor_tensor(m, m, bank.rearrange("p (a b) -> p a b", a=4), ALU.subtract).then_inc(*inc("free_D", (k_, kind, i, c)))
                    for c in range(2):
                        bank = tile((k_, "vt", c))
                        for j in range(4):
                            ins = dve.tensor_scalar(XX[:, c, j, :], bank[:, j * P:(j + 1) * P],
                                                    GCOL[:, 2 + c, 4 * hf + j:4 * hf + j + 1], None, ALU.mult)
                            ins.then_inc(*(inc("free_D", (k_, "vt", c)) if j == 3 else inc("vb_part", (k_, c, j))))
                    bank = tile((k_, "kt"))
                    dve.wait_ge(*past("tail_ready", (s, 4 * hf + 3)))
                    for j in range(4):
                        ins = dve.tensor_scalar(KTL[:, j, :], bank[:, j * P:(j + 1) * P],
                                                GLT[:, 1, 4 * hf + j:4 * hf + j + 1], None, ALU.mult)
                        ins.then_inc(*(inc("free_D", (k_, "kt")) if j == 3 else inc("kt_part", (k_, j))))
                    bank = tile((k_, "ks"))
                    dve.wait_ge(*past("free_D", (k_, "vt", 1)))
                    dve.tensor_tensor(XX[:, 1, :, :], XX[:, 1, :, :], bank.rearrange("p (a b) -> p a b", a=4), ALU.subtract).then_inc(*inc("free_D", (k_, "ks")))
                bank = tile((s, "onrm"))
                dve.tensor_scalar(ROWS[0:8, 4, :], bank[0:8, 0:S], 1.0 / 128, NORM_EPS, ALU.mult, ALU.add).then_inc(*inc("free_D", (s, "onrm")))
                dve.wait_ge(*past("free_D", (s, "onrm")))
                dve.reciprocal(ROWS[0:8, 3, :], ROWS[0:8, 4, :]).then_inc(*inc("onrm_recip", s))

                def lo_pair(dst, hi, m, wait, name):
                    dve.wait_ge(*past(wait, (s, m)))
                    dve.tensor_tensor(dst[:, 2 * m:2 * m + 2, :], CB[:, 2 * m:2 * m + 2, :],
                                          hi[:, 2 * m:2 * m + 2, :].bitcast(F32), ALU.subtract).then_inc(*inc(name, (s, m)))

                for m in range(4):
                    bank = tile((s, "obc", m))
                    o = CB[:, 2 * m:2 * m + 2, :]
                    of = o.rearrange("p a b -> p (a b)")
                    dve.scalar_tensor_tensor(of, of, DNG[:, l:l + 1], bank, ALU.mult, ALU.mult).then_inc(*inc("free_D", (s, "obc", m)))
                    dve.wait_ge(*past("free_D", (s, "obc", m)))
                    dve.wait_ge(*past("cb_ready", (s, 15)))
                    dve.tensor_tensor(o, o, ZT[:, 2 * m:2 * m + 2, :], ALU.mult).then_inc(*inc("ov_ready", (s, m)))
                    if m:
                        lo_pair(OL, OH, m - 1, "ohb_ready", "olb_ready")
                lo_pair(OL, OH, 3, "ohb_ready", "olb_ready")
                for i in range(4):
                    step((s, "bb", i))
                    bank = tile((s, "bb", i))
                    dve.wait_ge(*past("free_A", (s, "gb", i)))
                    o = CB[:, 2 * i:2 * i + 2, :]
                    dve.tensor_tensor(o, GBT[:, 2 * i:2 * i + 2, :], pair_of(bank), ALU.mult).then_inc(*inc("free_D", (s, "bb", i)))
                    dve.wait_ge(*past("free_D", (s, "bb", i)))
                    dve.tensor_tensor(o, o, M1[:, 2 * i:2 * i + 2, :], ALU.add).then_inc(*inc("mv_ready", (s, i)))
                    dve.wait_ge(*past("mv_ready", (s, i)))
                    lo_pair(XL, XH, i, "mh_ready", "ml_ready")
                for i in range(4):
                    step((s, "out", i))

            norm(0)
            for s in range(1, n_sub):
                if s in (1, 3):
                    mlp(s)
                elif s == 2:
                    recurrence(s)
                elif is_mix(s):
                    mixer(s)
                else:
                    ffn(s)
                norm(s)

        @block.gpsimd
        def _(pool):
            def chain(ins):
                link(pool, ins, "pool_chain")

            def const(dst, src):
                pool.dma_start(dst, src).then_inc(*inc("const_in", None, 16))

            pool.memset(ONES[:, :], 1.0).then_inc(*inc("ones_part"))
            pool.wait_ge(*past("ones_part"))
            chain(pool.memset(ESEL[:, :], 0.0))
            pool.memset(ESEL[:, 15:16], 1.0).then_inc(*inc("ones_ready"))
            pool.wait_ge(*past("ones_ready"))
            def load_gb(s):
                for q in range(2):
                    v = LN[s][q]
                    pool.dma_start(GB[:, q, :], bass.AP(v.tensor, v.offset, [[0, P], [1, D]])).then_inc(*inc("gb_in", s, 16))

            def scaled_part(s, t, part):
                if part == 0:
                    pool.wait_ge(*past(f"xn_ready{t}", (s, t)))
                    chain(pool.tensor_tensor(XS[:, t, :], XN[:, t, :], GB[:, 0, :], ALU.mult))
                elif part == 1:
                    chain(pool.tensor_tensor(XS[:, t, :], XS[:, t, :], GB[:, 1, :], ALU.add))
                else:
                    pool.tensor_scalar(XS[:, t, :], XS[:, t, :], ALPHA, None, ALU.mult).then_inc(*inc("xs_ready", (s, t)))
                    pool.wait_ge(*past("xs_ready", (s, t)))

            def scaled(s):
                pool.wait_ge(*past("gb_in", s))
                for t in range(NT):
                    for part in range(3):
                        scaled_part(s, t, part)
                pool.wait_ge(*past("xs_ready", (s, 1)))

            def bcast_rows(vec, n):
                return bass.AP(vec.tensor, vec.offset, [[0, P], [1, n]])

            const(NSC[:, :], C["norm_scale"])
            const(WIN[:, :], C["window"])
            const(COS[:, :], C["rope_cos"])
            const(SIN[:, :], C["rope_sin"])
            const(ROT[:, :], C["rope_rot"])
            const(SNK[:, :], bcast_rows(I["attn_sinks"], 8))
            for l in range(2):
                const(SNK2[:, l, :], bcast_rows(I["sinks_2"][l], 16))
                const(AL2[:, l:l + 1], I["a_log_2"][l].rearrange("(a b) -> a b", b=1))
                const(AL2[:, 2 + l:3 + l], I["dt_bias_2"][l].rearrange("(a b) -> a b", b=1))
            load_gb(0)
            for t in range(NT):
                pool.wait_ge(*past("x_in"))
                pool.tensor_scalar(XS[:, t, :], XN[:, t, :], ALPHA, None, ALU.mult).then_inc(*inc("xs_ready", (-1, t)))
                pool.wait_ge(*past("xs_ready", (-1, t)))

            def ada_load(q0, q1):
                for q in range(q0, min(q1, n_ada)):
                    pool.wait_ge(*past("ada_used", q - NADR))
                    pool.dma_start(ADR[:, q % NADR, :], ada_src(q)).then_inc(*inc(f"ada_next{q % NADR}", q, 16))

            ada_load(20, 58)
            if n_sub > 1:
                pool.wait_ge(*past("xn_ready1", (0, 1)))
                pool.dma_start(HOT[:, :], C["bucket_hot"]).then_inc(*inc("rel_in", None, 16))
                pool.dma_start(RBI[0:32, :], I["rel_bias_2"]).then_inc(*inc("rel_in", None, 16))
                pool.memset(RBI[32:33, :], 1.0).then_inc(*inc("rel_one"))
                pool.wait_ge(*past("rel_one"))
                ada_load(58, 64)
                pool.wait_ge(*past("gb_in", 0))
                for t in range(NT):
                    for part in range(3):
                        scaled_part(0, t, part)
                        ada_load(64 + 5 * (3 * t + part), 69 + 5 * (3 * t + part))
                load_gb(1)
                ada_load(94, n_ada)
            if n_sub > 2:
                scaled(1)
            for s in range(2, n_sub):
                l = (s - 4) // 3
                if s == 2:
                    pool.wait_ge(*past("xl_ready", (2, 3)))
                    pool.memset(XP[:, :, :, :], 0.0).then_inc(*inc("xp_zero"))
                    pool.wait_ge(*past("xp_zero"))

                    def gate_weights(g):
                        if g >= 2:
                            pool.wait_ge(*past("tile_done", ("gate", g - 2, 1, 1)))
                        for d in range(2):
                            for q, name in enumerate(("rnn_w_a", "rnn_w_x")):
                                i0 = 4 * d + 2 * q
                                pool.dma_start(WG[:, g % 2, i0:i0 + 2, :], I[name][0, d, 2 * g:2 * g + 2].rearrange("b i j -> i b j")).then_inc(*inc(f"rnn_w_in{g % 2}", g, 16))

                    pool.wait_ge(*past("tile_done", ("ada", n_ada // 8 - 1)))
                    for g in range(2):
                        gate_weights(g)
                    for g in range(8):
                        pool.wait_ge(*past("free_A", ("gate", g, 1, 1)))
                        xc = XC[:, 2 * g:2 * g + 2, :].rearrange("p (o b) s -> p o b s", o=1).broadcast_to([RB_W, 2, 2, S])
                        chain(pool.tensor_tensor(RI[:, g % 2, :, :, :], RI[:, g % 2, :, :, :], xc, ALU.mult))
                        pool.tensor_tensor(RI[:, g % 2, :, :, :], RI[:, g % 2, :, :, :], xc, ALU.add).then_inc(*inc("rnn_ix", g))
                        pool.wait_ge(*past("rnn_ix", g))
                        if g < 6:
                            gate_weights(g + 2)
                    load_gb(2)
                elif is_mix(s):
                    if s == 5:
                        pool.wait_ge(*past("y_free", (3, 1)))
                    pool.wait_ge(*past("xl_ready", (s, 3)))
                    pool.memset(CIN[:, :, :, :], 0.0).then_inc(*inc("cin_zero", s))
                    pool.wait_ge(*past("cin_zero", s))

                    def bias(j):
                        t, hh = divmod(j, 2)
                        head = (2 * (t // 4) + hh) * 4 + t % 4
                        if j >= 3:
                            pool.wait_ge(*past("free_D", (s, "sc", j - 3)))
                        src = bass.AP(BIAS.tensor, head * P * EXT + P - 1, [[EXT - 1, P], [1, S]])
                        pool.dma_start(BI[:, j % 3, :], src).then_inc(*inc(f"bias_in{j % 3}", (s, j), 16))

                    if s == 5:
                        pool.dma_start(LVL[:, :], C["levels_t"]).then_inc(*inc("dn_const_in", None, 16))
                        pool.dma_start(TRI[:, :], C["causal_t"]).then_inc(*inc("dn_const_in", None, 16))
                        pool.wait_ge(*past("dn_const_in"))
                    for n in range(4):
                        pool.wait_ge(*past(f"bias_out{n}", 12 + n))
                    for j in range(19):
                        if j < 16:
                            bias(j)
                        if j >= 3:
                            u = j - 3
                            pool.wait_ge(*past(*(("tanh_ready", (s, u)) if u < 12 else ("free_A", (s, "z", u - 12)))))
                            v = CB[:, 2 * u:2 * u + 2, :] if u < 12 else ZT[:, 2 * u - 24:2 * u - 22, :]
                            chain(pool.tensor_tensor(TH[:, u % 2, :, :], TH[:, u % 2, :, :], v, ALU.mult))
                            pool.tensor_tensor(v, v, TH[:, u % 2, :, :], ALU.add).then_inc(*inc("cb_ready", (s, u)))
                            pool.wait_ge(*past("cb_ready", (s, u)))
                    for hf in range(2):
                        k_ = (s, hf)
                        for i in range(7):
                            for c in range(2):
                                if i == 0:
                                    pool.wait_ge(*past("free_D", (s, "la", 4 * hf + 3)))
                                elif i == 1:
                                    pool.wait_ge(*past("u0_ready", (k_, c)))
                                else:
                                    pool.wait_ge(*past("tile_done", (k_, "x", i - 1, c)))
                                lev = LVL[:, i * P:(i + 1) * P].rearrange("p (a b) -> p a b", a=1).broadcast_to([P, 4, P])
                                pool.tensor_tensor(MM[:, c, :, :], LT[:, c, :, :], lev, ALU.mult).then_inc(*inc("m_ready", (k_, i, c)))
                                pool.wait_ge(*past("m_ready", (k_, i, c)))
                    pool.wait_ge(*past("olb_ready", (s, 3)))
                    load_gb(s)
                else:
                    load_gb(s)
                if s + 1 < n_sub:
                    scaled(s)

    return made


_INS = ["x", "c", "ada_w", "ada_b", "ln_g", "ln_b", "attn_w_in", "attn_w_out", "attn_sinks", "rnn_w_in", "rnn_conv_w",
        "rnn_conv_b", "rnn_w_a", "rnn_b_a", "rnn_w_x", "rnn_b_x", "rnn_lam", "rnn_w_out", "mlp_w1", "mlp_w2",
        "rel_bias_2", "ln_g_2", "ln_b_2", "ffn_w13_2", "ffn_w2_2", "w_in_2", "conv_w_2", "a_log_2", "dt_bias_2",
        "dn_norm_g_2", "sinks_2", "w_branch_a_2", "w_branch_b_2", "w_out_2"]


def kernel(**inputs):
    import concourse.bacc as _bacc
    from concourse.bass_utils import run_bass_kernel_spmd as _run

    arrays = {n: np.ascontiguousarray(inputs[n]) for n in _INS}
    tables = shape_constants()

    def program(counts):
        nc = _bacc.Bacc("TRN2", target_bir_lowering=False, num_devices=1)

        def dram(name, a, kind):
            return nc.dram_tensor(name, a.shape, mybir.dt.from_np(a.dtype), kind=kind).ap()

        ins = {n: dram(f"in_{n}_dram", a, "ExternalInput") for n, a in arrays.items()}
        consts = {n: dram(f"table_{n}_dram", a, "ExternalInput") for n, a in tables.items()}
        out = nc.dram_tensor("out_0_dram", (1, S, D), F32, kind="ExternalOutput").ap()
        return nc, build(nc, ins, consts, out, counts, N_SUB)

    _, counts = program({})
    nc, _ = program(counts)
    feed = {f"in_{n}_dram": a for n, a in arrays.items()}
    feed.update({f"table_{n}_dram": a for n, a in tables.items()})
    r = _run(nc, [feed], core_ids=[0])
    return r.results[0]["out_0_dram"]
```
